# Optimizing a Trainium2 kernel written in Bass

```python
import math
import jax, jax.numpy as jnp
from jax import lax
import numpy as np

D_MODEL = 1024
BATCH = 1
SEQ = 1024
DEPTH = 1

HEAD_DIM = 64
GDN_HEADS = 6
GDN_DIM = GDN_HEADS * HEAD_DIM
GDN_CONV = 4
GDN_CHUNK = 64
NSA_HEADS = 6
NSA_KV_HEADS = 2
NSA_GROUP = NSA_HEADS // NSA_KV_HEADS
NSA_DIM = NSA_HEADS * HEAD_DIM
NSA_KV_DIM = NSA_KV_HEADS * HEAD_DIM
CMP_STRIDE = 16
CMP_LEN = 2 * CMP_STRIDE
SEL_BLOCK = 64
SEL_TOPK = 8
WINDOW = 512
Q_BLOCK = 128
CONV_CH = 256
CONV_WIDTH = 31
MIX_DIM = GDN_DIM + NSA_DIM + CONV_CH
D_FF = 2816
FFN_CONV = 3
ROPE_THETA = 10000.0
EPS = 1e-6
NEG = -1e30
FORCE = 1e4
SPLIT_SIZES = (GDN_DIM, GDN_DIM, GDN_DIM, GDN_DIM, GDN_HEADS, GDN_HEADS,
               NSA_DIM, NSA_KV_DIM, NSA_KV_DIM, NSA_KV_DIM, NSA_KV_DIM, NSA_KV_DIM, NSA_KV_DIM,
               3 * NSA_HEADS, 2 * CONV_CH)
IN_DIM = sum(SPLIT_SIZES)

kernel_name = "hybrid_gdn_nsa_conformer_block"

def rms_norm(x, g):
    xf = x.astype(jnp.float32)
    y = xf * lax.rsqrt(jnp.mean(xf * xf, axis=-1, keepdims=True) + EPS)
    return (y * g.astype(jnp.float32)).astype(x.dtype)

def causal_dwconv(x, w):
    k = w.shape[0]
    xp = jnp.pad(x, ((0, 0), (k - 1, 0), (0, 0)))
    return lax.conv_general_dilated(xp, w[:, None, :].astype(x.dtype), window_strides=(1,), padding='VALID',
                                    dimension_numbers=('NWC', 'WIO', 'NWC'), feature_group_count=x.shape[-1])

def rope_tables(positions):
    inv = 1.0 / (ROPE_THETA ** (jnp.arange(0, HEAD_DIM, 2, dtype=jnp.float32) / HEAD_DIM))
    ang = positions.astype(jnp.float32)[..., None] * inv
    return jnp.cos(ang), jnp.sin(ang)

def apply_rope(x, cos, sin):
    x1, x2 = jnp.split(x.astype(jnp.float32), 2, axis=-1)
    c = cos[:, :, None]
    s = sin[:, :, None]
    return jnp.concatenate([x1 * c - x2 * s, x1 * s + x2 * c], axis=-1).astype(x.dtype)

def masked_softmax(s, valid):
    s = jnp.where(valid, s.astype(jnp.float32), NEG)
    return jnp.where(valid, jax.nn.softmax(s, axis=-1), 0.0)

def gated_deltanet(q, k, v, z, a, b, conv_w, a_log, dt_bias, norm_g):
    bsz, seq, _ = q.shape
    f32 = jnp.float32
    qkv = jax.nn.silu(causal_dwconv(jnp.concatenate([q, k, v], axis=-1), conv_w))
    q, k, v = jnp.split(qkv, 3, axis=-1)
    heads = lambda t: t.reshape(bsz, seq, GDN_HEADS, HEAD_DIM).transpose(0, 2, 1, 3).astype(f32)
    q, k, v = heads(q), heads(k), heads(v)
    q = q * lax.rsqrt(jnp.sum(q * q, -1, keepdims=True) + EPS) * (HEAD_DIM ** -0.5)
    k = k * lax.rsqrt(jnp.sum(k * k, -1, keepdims=True) + EPS)
    beta = jax.nn.sigmoid(b.astype(f32)).transpose(0, 2, 1)
    g = (-jnp.exp(a_log.astype(f32))[:, None]
         * jax.nn.softplus(a.astype(f32) + dt_bias.astype(f32)).transpose(0, 2, 1))
    n_chunks = seq // GDN_CHUNK
    ch = lambda t: t.reshape(bsz, GDN_HEADS, n_chunks, GDN_CHUNK, *t.shape[3:])
    q, k, v, beta, g = ch(q), ch(k), ch(v), ch(beta), ch(g)
    g = jnp.cumsum(g, axis=-1)
    tri = jnp.tril(jnp.ones((GDN_CHUNK, GDN_CHUNK), bool))
    tri_strict = jnp.tril(jnp.ones((GDN_CHUNK, GDN_CHUNK), bool), -1)
    decay = jnp.exp(jnp.where(tri, g[..., :, None] - g[..., None, :], -jnp.inf))
    kk = jnp.einsum('bhnid,bhnjd->bhnij', k, k)
    lower = jnp.where(tri_strict, beta[..., :, None] * kk * decay, 0.0)
    rhs = jnp.concatenate([v * beta[..., None], k * (beta * jnp.exp(g))[..., None]], axis=-1)
    sol = lax.linalg.triangular_solve(jnp.eye(GDN_CHUNK, dtype=f32) + lower, rhs,
                                      left_side=True, lower=True, unit_diagonal=True)
    u, w = jnp.split(sol, 2, axis=-1)
    qk = jnp.einsum('bhnid,bhnjd->bhnij', q, k) * decay

    def step(state, inp):
        q_c, k_c, u_c, w_c, g_c, qk_c = inp
        v_new = u_c - jnp.einsum('bhcd,bhde->bhce', w_c, state)
        o = (jnp.einsum('bhcd,bhde->bhce', q_c * jnp.exp(g_c)[..., None], state)
             + jnp.einsum('bhij,bhje->bhie', qk_c, v_new))
        g_last = g_c[..., -1:]
        state = (state * jnp.exp(g_last)[..., None]
                 + jnp.einsum('bhcd,bhce->bhde', k_c * jnp.exp(g_last - g_c)[..., None], v_new))
        return state, o

    xs = tuple(jnp.moveaxis(t, 2, 0) for t in (q, k, u, w, g, qk))
    state0 = jnp.zeros((bsz, GDN_HEADS, HEAD_DIM, HEAD_DIM), f32)
    _, o = lax.scan(step, state0, xs)
    o = o.transpose(1, 0, 3, 2, 4).reshape(bsz, seq, GDN_HEADS, HEAD_DIM)
    o = rms_norm(o, norm_g) * jax.nn.silu(z.astype(f32).reshape(bsz, seq, GDN_HEADS, HEAD_DIM))
    return o.reshape(bsz, seq, GDN_DIM).astype(z.dtype)

def compress(t, w, pe):
    bsz, seq, h, d = t.shape
    c = t.reshape(bsz, seq // CMP_STRIDE, CMP_STRIDE, h, d)
    blk = jnp.concatenate([c[:, :-1], c[:, 1:]], axis=2) + pe[:, None, :].astype(t.dtype)
    return jnp.einsum('bnlhd,lde->bnhe', blk, w.astype(t.dtype))

def native_sparse_attention(q, k_cmp, v_cmp, k_sel, v_sel, k_win, v_win, gate_logits, cos, sin,
                            w_ck, w_cv, pe_ck, pe_cv):
    bsz, seq, _ = q.shape
    dt = q.dtype
    nqb = seq // Q_BLOCK
    n_cmp = seq // CMP_STRIDE - 1
    n_slc = seq // SEL_BLOCK
    topk = min(SEL_TOPK, n_slc)
    scale = HEAD_DIM ** -0.5
    perm = (1, 0, 3, 4, 2, 5)
    q = apply_rope(q.reshape(bsz, seq, NSA_HEADS, HEAD_DIM), cos, sin)
    q = q.reshape(bsz, nqb, Q_BLOCK, NSA_KV_HEADS, NSA_GROUP, HEAD_DIM).transpose(perm)
    gates = jax.nn.sigmoid(gate_logits).reshape(bsz, nqb, Q_BLOCK, NSA_KV_HEADS, NSA_GROUP, 3).transpose(perm)
    kvh = lambda t: t.reshape(bsz, seq, NSA_KV_HEADS, HEAD_DIM)
    cmp_end = np.arange(n_cmp) * CMP_STRIDE + CMP_LEN - 1
    kc = apply_rope(compress(kvh(k_cmp), w_ck, pe_ck), cos[:, cmp_end], sin[:, cmp_end]).transpose(0, 2, 1, 3)
    vc = compress(kvh(v_cmp), w_cv, pe_cv).transpose(0, 2, 1, 3)
    ks = apply_rope(kvh(k_sel), cos, sin).transpose(0, 2, 1, 3).reshape(bsz, NSA_KV_HEADS, n_slc, SEL_BLOCK, HEAD_DIM)
    vs = kvh(v_sel).transpose(0, 2, 1, 3).reshape(bsz, NSA_KV_HEADS, n_slc, SEL_BLOCK, HEAD_DIM)
    pad = ((0, 0), (0, 0), (WINDOW, 0), (0, 0))
    kw = jnp.pad(apply_rope(kvh(k_win), cos, sin).transpose(0, 2, 1, 3), pad)
    vw = jnp.pad(kvh(v_win).transpose(0, 2, 1, 3), pad)
    cmp_end_j = jnp.asarray(cmp_end)
    ci = np.arange(n_cmp)[:, None] * CMP_STRIDE
    sj = np.arange(n_slc)[None, :] * SEL_BLOCK
    overlap = jnp.asarray(((ci < sj + SEL_BLOCK) & (ci + CMP_LEN > sj)).astype(np.float32))
    slc = jnp.arange(n_slc)
    bi = jnp.arange(bsz)[:, None, None, None]
    hi = jnp.arange(NSA_KV_HEADS)[None, :, None, None]
    span = WINDOW + Q_BLOCK

    def block(inp):
        qi, q_b, g_b = inp
        t = qi * Q_BLOCK + jnp.arange(Q_BLOCK)
        s = jnp.einsum('bhgqd,bhnd->bhgqn', q_b, kc) * scale
        p_c = masked_softmax(s, cmp_end_j[None, :] <= t[:, None])
        o_c = jnp.einsum('bhgqn,bhnd->bhgqd', p_c.astype(dt), vc)
        imp = jnp.einsum('bhgqn,nj->bhqj', p_c, overlap)
        cur = t // SEL_BLOCK
        forced = (slc[None, :] == 0) | (slc[None, :] == cur[:, None]) | (slc[None, :] == cur[:, None] - 1)
        imp = jnp.where(forced, FORCE, jnp.where(slc[None, :] * SEL_BLOCK <= t[:, None], imp, -1.0))
        _, idx = lax.top_k(imp, topk)
        k_g = ks[bi, hi, idx].reshape(bsz, NSA_KV_HEADS, Q_BLOCK, topk * SEL_BLOCK, HEAD_DIM)
        v_g = vs[bi, hi, idx].reshape(bsz, NSA_KV_HEADS, Q_BLOCK, topk * SEL_BLOCK, HEAD_DIM)
        kpos = (idx[..., None] * SEL_BLOCK + jnp.arange(SEL_BLOCK)).reshape(bsz, NSA_KV_HEADS, Q_BLOCK, -1)
        s = jnp.einsum('bhgqd,bhqkd->bhgqk', q_b, k_g) * scale
        p_s = masked_softmax(s, kpos[:, :, None] <= t[:, None])
        o_s = jnp.einsum('bhgqk,bhqkd->bhgqd', p_s.astype(dt), v_g)
        k_b = lax.dynamic_slice_in_dim(kw, qi * Q_BLOCK, span, axis=2)
        v_b = lax.dynamic_slice_in_dim(vw, qi * Q_BLOCK, span, axis=2)
        wpos = qi * Q_BLOCK - WINDOW + jnp.arange(span)
        diff = t[:, None] - wpos[None, :]
        s = jnp.einsum('bhgqd,bhkd->bhgqk', q_b, k_b) * scale
        p_w = masked_softmax(s, (diff >= 0) & (diff < WINDOW) & (wpos[None, :] >= 0))
        o_w = jnp.einsum('bhgqk,bhkd->bhgqd', p_w.astype(dt), v_b)
        return g_b[..., 0:1] * o_c + g_b[..., 1:2] * o_s + g_b[..., 2:3] * o_w

    out = lax.map(block, (jnp.arange(nqb), q, gates))
    return out.transpose(1, 0, 4, 2, 3, 5).reshape(bsz, seq, NSA_DIM)

def conformer_conv(u, dw_w, dw_b, ln_g, ln_b):
    a, gt = jnp.split(u, 2, axis=-1)
    h = causal_dwconv(a * jax.nn.sigmoid(gt), dw_w) + dw_b.astype(u.dtype)
    hf = h.astype(jnp.float32)
    mu = jnp.mean(hf, -1, keepdims=True)
    var = jnp.mean(jnp.square(hf - mu), -1, keepdims=True)
    hf = (hf - mu) * lax.rsqrt(var + EPS) * ln_g.astype(jnp.float32) + ln_b.astype(jnp.float32)
    return jax.nn.silu(hf).astype(u.dtype)

def conv_gated_mlp(x, w_up, conv_w, w_down):
    h = causal_dwconv(x @ w_up, conv_w)
    gt, val = jnp.split(h, 2, axis=-1)
    return (jax.nn.silu(gt) * val) @ w_down

def setup_inputs(seed: int = 0) -> dict:
    key = jax.random.key(seed)
    ks = jax.random.split(key, 26)
    f32 = jnp.float32
    nrm = lambda k, shape, sc: jax.random.normal(k, shape, f32) * sc
    gain = lambda k, n: 1.0 + 0.05 * jax.random.normal(k, (DEPTH, n), f32)
    dt = jnp.exp(jax.random.uniform(ks[10], (DEPTH, GDN_HEADS), f32, math.log(1e-3), math.log(1e-1)))
    return {
        "x": jax.random.normal(ks[0], (BATCH, SEQ, D_MODEL), f32),
        "positions": (jnp.arange(SEQ, dtype=jnp.int32)[None, :]
                      + jax.random.randint(ks[1], (BATCH, 1), 0, SEQ, dtype=jnp.int32)),
        "norm_mix_pre": gain(ks[2], D_MODEL),
        "norm_mix_post": gain(ks[3], D_MODEL),
        "norm_ffn_pre": gain(ks[4], D_MODEL),
        "norm_ffn_post": gain(ks[5], D_MODEL),
        "w_in": nrm(ks[6], (DEPTH, D_MODEL, IN_DIM), D_MODEL ** -0.5),
        "w_out": nrm(ks[7], (DEPTH, MIX_DIM, D_MODEL), MIX_DIM ** -0.5),
        "gdn_conv_w": nrm(ks[8], (DEPTH, GDN_CONV, 3 * GDN_DIM), GDN_CONV ** -0.5),
        "gdn_a_log": jnp.log(jax.random.uniform(ks[9], (DEPTH, GDN_HEADS), f32, 1.0, 16.0)),
        "gdn_dt_bias": dt + jnp.log(-jnp.expm1(-dt)),
        "gdn_norm_g": gain(ks[11], HEAD_DIM),
        "nsa_cmp_wk": nrm(ks[12], (DEPTH, CMP_LEN, HEAD_DIM, HEAD_DIM), (CMP_LEN * HEAD_DIM) ** -0.5),
        "nsa_cmp_wv": nrm(ks[13], (DEPTH, CMP_LEN, HEAD_DIM, HEAD_DIM), (CMP_LEN * HEAD_DIM) ** -0.5),
        "nsa_cmp_pe_k": nrm(ks[14], (DEPTH, CMP_LEN, HEAD_DIM), 0.02),
        "nsa_cmp_pe_v": nrm(ks[15], (DEPTH, CMP_LEN, HEAD_DIM), 0.02),
        "cc_dw_w": nrm(ks[16], (DEPTH, CONV_WIDTH, CONV_CH), CONV_WIDTH ** -0.5),
        "cc_dw_b": nrm(ks[17], (DEPTH, CONV_CH), 0.02),
        "cc_ln_g": gain(ks[18], CONV_CH),
        "cc_ln_b": nrm(ks[19], (DEPTH, CONV_CH), 0.02),
        "ffn_w_up": nrm(ks[20], (DEPTH, D_MODEL, 2 * D_FF), D_MODEL ** -0.5),
        "ffn_conv_w": nrm(ks[21], (DEPTH, FFN_CONV, 2 * D_FF), FFN_CONV ** -0.5),
        "ffn_w_down": nrm(ks[22], (DEPTH, D_FF, D_MODEL), D_FF ** -0.5),
    }

def reference(x, positions, norm_mix_pre, norm_mix_post, norm_ffn_pre, norm_ffn_post, w_in, w_out,
              gdn_conv_w, gdn_a_log, gdn_dt_bias, gdn_norm_g, nsa_cmp_wk, nsa_cmp_wv, nsa_cmp_pe_k,
              nsa_cmp_pe_v, cc_dw_w, cc_dw_b, cc_ln_g, cc_ln_b, ffn_w_up, ffn_conv_w, ffn_w_down):
    cos, sin = rope_tables(positions)
    split_idx = [int(s) for s in np.cumsum(SPLIT_SIZES)[:-1]]
    for l in range(DEPTH):
        h = rms_norm(x, norm_mix_pre[l])
        (gq, gk, gv, gz, ga, gb, nq, nkc, nvc, nks, nvs, nkw, nvw, ngate, cu) = jnp.split(h @ w_in[l], split_idx, axis=-1)
        o_a = gated_deltanet(gq, gk, gv, gz, ga, gb, gdn_conv_w[l], gdn_a_log[l], gdn_dt_bias[l], gdn_norm_g[l])
        o_b = native_sparse_attention(nq, nkc, nvc, nks, nvs, nkw, nvw, ngate, cos, sin,
                                      nsa_cmp_wk[l], nsa_cmp_wv[l], nsa_cmp_pe_k[l], nsa_cmp_pe_v[l])
        o_c = conformer_conv(cu, cc_dw_w[l], cc_dw_b[l], cc_ln_g[l], cc_ln_b[l])
        mix = jnp.concatenate([o_a, o_b, o_c], axis=-1) @ w_out[l]
        x = x + rms_norm(mix, norm_mix_post[l])
        h = rms_norm(x, norm_ffn_pre[l])
        x = x + rms_norm(conv_gated_mlp(h, ffn_w_up[l], ffn_conv_w[l], ffn_w_down[l]), norm_ffn_post[l])
    return x


_drawn_inputs = setup_inputs


def setup_inputs(seed=0):
    import zlib

    import numpy as np

    out = dict(_drawn_inputs(seed))
    spreads = {}
    factors = {'nsa_cmp_pe_k': 22.322, 'nsa_cmp_pe_v': 4.584, 'cc_dw_b': 3.027, 'cc_ln_b': 5.28}
    for name, (base, spread) in spreads.items():
        noise = np.random.default_rng([zlib.crc32(name.encode()), seed]).standard_normal(out[name].shape)
        drawn = base * np.exp(spread * noise) if base else spread * noise
        out[name] = __import__('jax').numpy.asarray(drawn.astype(out[name].dtype))
    for name, factor in factors.items():
        out[name] = (out[name] * factor).astype(out[name].dtype)
    return out
```

```python
import math
from contextlib import ExitStack

import numpy as np

import concourse.bass as bass
from concourse import mybir

F32 = mybir.dt.float32
BF16 = mybir.dt.bfloat16
I32 = mybir.dt.int32
ACT = mybir.ActivationFunctionType
ALU = mybir.AluOpType
AX = mybir.AxisListType

P = 128
S = 1024
D = 1024
NT = S // P
KD = D // P
HD = 64
GH = 6
GDIM = GH * HD
CH = 64
NH = 6
KV = 2
GRP = NH // KV
STRIDE = 16
CLEN = 32
NCMP = S // STRIDE - 1
SLC = 64
NSLC = S // SLC
TOPK = 8
WINDOW = 512
CCH = 256
CW = 31
DFF = 2816
NF = DFF // P
EPS = 1e-6
FORCE = 1e4
NEG = -1e30
THETA = 10000.0

_W = (GDIM, GDIM, GDIM, GDIM, GH, GH, NH * HD, 128, 128, 128, 128, 128, 128, 3 * NH, 2 * CCH)
_O = [sum(_W[:i]) for i in range(len(_W) + 1)]
(C_GQ, C_GK, C_GV, C_GZ, C_GA, C_GB, C_NQ, C_NKC, C_NVC, C_NKS, C_NVS, C_NKW, C_NVW, C_NG, C_CU, IN_DIM) = _O

CM_BLOCKS = [(C_CU, 512), (C_GQ, 384), (C_GK, 384), (C_GV, 384), (C_NKC, 256)]
TM_BLOCKS = [(C_GZ, GDIM + 2 * GH), (C_NKS, 512), (C_NQ, NH * HD + 3 * NH)]
CM_TILES = [(b, j) for b, (_, n) in enumerate(CM_BLOCKS) for j in range(n // P)]


class Regions:

    def __init__(self, arena):
        self.arena = arena

    def view(self, at, shape, dtype=F32):
        words = int(np.prod(shape)) * (1 if dtype in (F32, I32) else 2) // (1 if dtype in (F32, I32) else 4)
        v = self.arena[:, at:at + words]
        if dtype != F32:
            v = v.bitcast(dtype)
        if len(shape) > 1:
            names = " ".join(f"d{i}" for i in range(len(shape)))
            v = v.rearrange(f"p ({names}) -> p {names}", **{f"d{i}": n for i, n in enumerate(shape)})
        return v


def bc(ap, dim, n):
    v = ap.unsqueeze(dim)
    shape = list(v.shape)
    shape[dim] = n
    return v.broadcast_to(shape)


class Count:

    def __init__(self, sem):
        self.sem, self.n = sem, 0

    def up(self, ins):
        ins.then_inc(self.sem, 1)
        self.n += 1
        return ins

    def settle(self, eng):
        eng.wait_ge(self.sem, self.n)


def inv_freq():
    return (1.0 / (np.float32(THETA) ** (np.arange(0, HD, 2, dtype=np.float32) / np.float32(HD)))).astype(np.float32)


PC_GMIX, PC_GFFN, PC_GCONV, PC_CCW, PC_CCB, PC_LNG, PC_LNB, PC_GNG = 0, 8, 16, 52, 114, 116, 118, 120
PC_FCONV, PC_PEK, PC_PEV = 128, 128 + 3 * 2 * NF, 128 + 3 * 2 * NF + CLEN

CM_ORDER = [(0, 0), (0, 2), (0, 1), (0, 3)] + CM_TILES[4:]
CM_AFTER = [1 + max(i for i, (b, _) in enumerate(CM_ORDER) if b == n) for n in range(len(CM_BLOCKS))]
BLOCKS = CM_BLOCKS + TM_BLOCKS
NCM = len(CM_BLOCKS)


def merge(*lists):
    tagged = [((i + 0.5) / len(l), n, s) for n, l in enumerate(lists) for i, s in enumerate(l)]
    return [s for _, _, s in sorted(tagged, key=lambda x: x[:2])]


LEVELS = 6


def gdn_prepare(t):
    steps = [("A1a", t), ("A1r", t), ("A1s", t), ("A1n", t), ("A1b", t), ("A2a", t), ("A2b", t), ("A3a", t), ("A3b", t)]
    for l in range(LEVELS):
        steps.append(("M", t, l))
        if 1 <= l < LEVELS - 1:
            steps.append(("X", t, l))
        steps.append(("XT", t, l))
    return steps + [("A4", t)]


def gdn_scan(t):
    return [("B1", t, 0), ("B2", t, 0), ("B1", t, 1), ("B2", t, 1), ("B3", t), ("C1", t), ("C1r", t), ("C1s", t), ("C1n", t), ("C2", t)]


def win_blocks(t):
    return max(0, t - WINDOW // P), t + 1


def key_blocks(t, kind):
    return (0, t + 1) if kind == 0 else win_blocks(t)


def batches(t, kind):
    k0, k1 = key_blocks(t, kind)
    n = -(-(k1 - k0) // 4)
    cut = [k0 + (k1 - k0) * i // n for i in range(n + 1)]
    return list(zip(cut, cut[1:]))


GAP = "gap"
RANK_PARTS = 4


def nsa():
    heads = [(t, kind, h) for t in range(NT) for kind in (1, 0) for h in range(NH)]
    steps = [("Nq", 0), GAP, ("Nc1", 0), GAP, ("Ns", 0, 1, 0), GAP, ("Nc1b", 0)]
    behind = []
    for i, (t, kind, h) in enumerate(heads):
        chosen = (t + 1) * P > TOPK * SLC
        last = kind == 0 and h == NH - 1
        if not last:
            steps.append(("Ns",) + heads[i + 1])
            if kind == 0 and h == NH - 2 and t + 1 < NT:
                steps.append(("Nq", t + 1))
        cuts = batches(t, kind)
        for n in range(len(cuts)):
            steps += [("NT", t, kind, h, n), GAP] + behind + [GAP]
            behind = [("NV", t, kind, h, n)]
        if h == NH - 1:
            behind.append(("Ne", t, kind))
        if last and t + 1 < NT:
            steps += [("Nc1", t + 1), GAP] + behind + [("Ns",) + heads[i + 1], GAP, ("Nc1b", t + 1)]
            behind = []
        if kind == 1:
            if h == 0 and t:
                steps += [GAP, ("No", t - 1)]
            if chosen and h < 4:
                steps += [("Nr", t) + divmod(2 * h + e, RANK_PARTS) for e in range(2)]
            if chosen and h == 4:
                steps += [("Nidx", t), GAP]
            if h == NH - 1:
                steps += [("Nc2", t), GAP] + behind + [GAP]
                behind = [("Nc3", t)]
    return steps + behind + [GAP, ("No", NT - 1)]


def cost(step):
    if step[0] in ("NT", "NV"):
        b0, b1 = batches(step[1], step[2])[step[4]]
        return b1 - b0
    if step[0] == "Ns":
        k0, k1 = key_blocks(step[1], step[2])
        return k1 - k0 + 1
    return 3 if step[0] in ("Nq", "Nc1", "Nc2", "Nc3", "No") else 1 if step[0] == "Nidx" else 0


def fill_gaps(steps, fillers):
    total = sum(map(cost, steps))
    out, done, used = [], 0.0, 0
    for s in steps:
        if s == GAP:
            n = int(len(fillers) * done / total)
            out += fillers[used:n]
            used = n
        else:
            out.append(s)
            done += cost(s)
    return out + fillers[used:]


GDN = gdn_prepare(0)
for _t in range(NT):
    GDN += merge(gdn_scan(_t), gdn_prepare(_t + 1)) if _t + 1 < NT else gdn_scan(_t)
MIX = fill_gaps(nsa(), GDN)


def uses(kinds, upto):
    return sum(1 for s in MIX[:upto] if s[0] in kinds)


LATE = {
    "wo_mm": ("cm_done", 15),
    "v_tp": ("h_tp", 8),
    "up_mm": ("tm_done", 24),
    "dn_mm": ("kT_done", 8),
    "dn_t": ("cc_tp", 8),
    "wo_hi": ("w_hi", 32),
    "w_sq": ("ssq", 8),
    "w_ln": ("rms", 8),
    "w_rs": ("tap0", 9),
    "v_sq": ("qkv_ready", 9),
    "v_ln": ("z_out", 8),
    "v_rs": ("kT_out", 8),
    "v_hi": ("h_hi", 8),
    "up_hi": ("w_hi", 40),
    "up_tap": ("tm_act", 24),
    "up_silu": ("cu_out", 4),
    "a_hi": ("rope_tab", 2),
    "f_sq": ("ssq", 16),
    "f_ln": ("rms", 16),
    "f_rs": ("tap0", 17),
    "dn_hi": ("w_hi", 62),
    "w_y": ("h_scaled", 8),
    "v_hn": ("h_gained", 8),
    "v_hg": ("conv_done", 9),
    "wcol": ("cat_out", 4),
    "up_c1": ("rot_mul", 16),
    "up_conv": ("cc_tok", 8),
    "y_out": ("cc_st", 8),
    "f_y": ("cc_ag", 8),
    "wo_lo": ("w_lo", 32),
    "x1": ("h_lo", 8),
    "v_lo": ("rot", 32),
    "up_lo": ("w_lo", 40),
    "up_prod": ("ident_ready", 2),
    "a_lo": ("rot", 40),
    "dn_lo": ("w_lo", 62),
    "fin": ("h_lo", 16),
    "wo_st0": ("w_st0", 128),
    "wo_st1": ("w_st1", 128),
    "wo_st2": ("w_st2", 128),
    "wo_st3": ("w_st3", 128),
    "xr_in0": ("x_in0", 32),
    "xr_in1": ("x_in1", 32),
    "up_st0": ("x_in2", 32),
    "up_st1": ("x_in3", 32),
    "dn_st0": ("w_st0", 160),
    "dn_st1": ("w_st1", 160),
    "x1r0": ("w_st2", 160),
    "x1r1": ("w_st3", 160),
}


def build(nc, a, out, scratch):
    ctx = ExitStack()
    with ctx:
        sem_names = {}

        def sem(name):
            if name not in sem_names:
                sem_names[name] = ctx.enter_context(nc.semaphore(name))
            return sem_names[name]

        def late(name, value=0):
            early, base = LATE[name]
            return sem(early), base + value

        arena = ctx.enter_context(nc.sbuf_tensor("arena", [P, 53200], F32))
        R = Regions(arena)
        psum = ctx.enter_context(nc.psum_tensor("psum", [P, 8, 512], F32))

        hT_hi = R.view(0, [KD, S], BF16)
        hT_lo = R.view(4096, [KD, S], BF16)
        wst = [R.view(8192 + 1024 * c, [2, 512]) for c in range(4)]
        wb_hi = [R.view(12288 + 4096 * s, [KD, 512], BF16) for s in range(2)]
        wb_lo = [R.view(12288 + 4096 * s + 2048, [KD, 512], BF16) for s in range(2)]
        qkvT = R.view(20480, [9, S])
        x_in = [R.view(20480 + 1024 * s, [S]) for s in range(4)]
        x_hn = [R.view(24576 + 1024 * s, [S]) for s in range(2)]
        x_hg = [R.view(26624 + 1024 * s, [KD, P]) for s in range(2)]
        zab = R.view(29696, [NT, GDIM + 2 * GH])
        qr = R.view(32864, [NT, GRP, KV, HD])
        vsw = R.view(35936, [NT, 2, KV * HD])
        kT2 = R.view(37984, [2, S])
        kcat = R.view(40032, [2, S])
        vcat = R.view(42080, [2, S])
        glu = R.view(44128, [2, S])
        cacc = R.view(46176, [2, S])
        tmc = [R.view(48224 + 768 * s, [384]) for s in range(2)]
        tms = [R.view(48224 + 768 * s + 384, [384]) for s in range(2)]
        kr = [R.view(49760 + 256 * s, [2, P]) for s in range(2)]
        at = [50272]

        def small(shape, dtype=F32):
            words = int(np.prod(shape))
            if dtype == BF16:
                words = (words + 1) // 2
            v = R.view(at[0], shape, dtype)
            at[0] += words
            assert at[0] <= 53200
            return v

        ident = small([P])
        identb = small([P], BF16)
        prow = R.view(44128, [3, P])
        pcol = small([3 * P])
        eps_c = small([1])
        ssq = small([NT])
        rms = small([NT])
        rstd = small([NT])
        pos_i = small([NT + 1], I32)
        pos_f = small([NT + 1])
        cos_t = small([NT + 1, HD // 2])
        sin_t = small([NT + 1, HD // 2])
        ang = R.view(44512, [NT + 1, HD // 2])
        turns = R.view(44800, [NT + 1, HD // 2])
        inv_t = R.view(45088, [HD // 2])
        gate = small([NT, 3 * NH])
        lnst = small([NT, 6])
        lnag = small([NT, 2])
        lnr = small([NT])

        ones_c = small([1])
        gng = small([1])
        dtb = small([GH])
        alog = small([GH])
        maskD = small([CH], BF16)
        negI = small([CH], BF16)
        causal = small([P], BF16)
        far = small([P], BF16)
        EG = small([NT * GH])
        ED = small([NT * GH])
        EGL = small([NT, 2, 3])
        graw = small([NT * GH])
        beta = small([NT * GH])
        stat_a = small([NT * GH])
        stat_b = small([NT * GH])
        stat_c = small([NT, GH])
        Ic = small([CH])
        tri = small([NSLC, NSLC], BF16)
        forced = small([4, NSLC])
        scored = small([4, NSLC])
        kcT = small([CH])
        ss, rs, rh = small([12]), small([12]), small([12])
        ss2, rs2 = small([GH]), small([GH])
        cmx, csum = small([NH]), small([NH])
        nmx, psums, coef = small([2]), small([2 * NH]), small([NH])
        pg = small([CH + 1])
        imp, rank = small([NSLC]), small([NSLC])
        selb = small([KV, NSLC])
        selT = small([KV, P], BF16)
        wck = R.view(10240, [CLEN, P])
        wcv = R.view(14336, [CLEN, P])
        m1 = [8192]

        def mix1(shape, dtype=F32):
            w = int(np.prod(shape)) // (2 if dtype == BF16 else 1)
            v_ = R.view(m1[0], shape, dtype)
            m1[0] += w
            assert m1[0] <= 20480, m1
            return v_

        m2 = [40032]

        def mix2(shape, dtype=F32):
            w = int(np.prod(shape)) // (2 if dtype == BF16 else 1)
            v_ = R.view(m2[0], shape, dtype)
            m2[0] += w
            assert m2[0] <= 50272, m2
            return v_

        Umask = mix1([CH])
        SL = mix1([P])
        strict = mix1([CH])
        Ucum = mix1([P])
        half_ones = [mix1([P]) for _ in range(2)]
        blk_of = mix1([S], BF16)
        cmask = mix1([NT, CH], BF16)
        nm = mix1([LEVELS, CH])
        assert m1[0] <= 10240
        ctok = R.view(44128, [NT, CCH])
        cact = R.view(46176, [2, S])
        mix_hi = R.view(0, [KD, S], BF16)
        mix_lo = R.view(4096, [KD, S], BF16)
        qn, kn, kb, kbg, qg, vb = [mix1([GH, HD]) for _ in range(6)]
        MIbd = mix1([GH, P])
        kTn = mix1([3, P])
        kbTp = mix1([3, 2, P])
        qTp = mix1([3, 2, P])
        Drhs = mix1([GH, CH])
        DTc = mix1([GH, CH])
        DTs = mix1([GH, CH])
        LTc = mix1([GH, CH])
        sq = R.view(m1[0] - GH * CH, [2 * GH, HD])
        QTc = mix1([GH, CH])
        LTbd = mix1([GH, P])
        Tbd = mix1([GH, P])
        Xc, Tc, MIc = Drhs, qg, kb
        Sbd = mix1([3, P])
        vn = mix1([GH, HD])
        on = mix1([GH, HD])
        sq2 = mix1([GH, HD])
        mtmp = sq2.rearrange("p h d -> p (h d)").rearrange("p (h c) -> p h c", h=3)
        vcbd = mix1([3, P])
        kdec = [mix2([GH, HD]) for _ in range(2)]
        qgT = [mix2([3, P]) for _ in range(2)]
        uu = [mix2([GH, HD]) for _ in range(2)]
        nwT = [mix2([3, P]) for _ in range(2)]
        QTbd = [mix2([GH, P]) for _ in range(2)]
        qpad = mix2([KV, GRP, P])
        Pb = [mix2([S]) for _ in range(2)]
        PTs = [mix2([512]) for _ in range(2)]
        oacc = mix2([NH, HD])
        otmp = mix2([NH, HD])
        mtmp_n = otmp.rearrange("p h d -> p (h d)").rearrange("p (h c) -> p h c", h=3)
        csc = mix2([NH, CH])
        cmpg = mix2([NSLC, NSLC])
        cmpe = mix2([NSLC, NSLC])

        wo_hi = R.view(8192, [KD, D], BF16)
        wo_lo = R.view(12288, [KD, D], BF16)
        wo_st = [R.view(16384 + 1024 * c, [D]) for c in range(4)]
        xr = [R.view(20480 + 1024 * c, [D]) for c in range(2)]
        x1 = [R.view(22528 + 1024 * c, [D]) for c in range(2)]
        hn2 = [R.view(24576 + 1024 * c, [D]) for c in range(2)]
        hg2 = [R.view(26624 + 1024 * c, [KD, P]) for c in range(2)]
        gpost_mix = R.view(28672, [D])
        h2_hi, h2_lo = hT_hi, hT_lo
        wss, wrs = stat_a[:, 0:2 * NT], stat_b[:, 0:2 * NT]
        act_hi = R.view(8192, [NF, S], BF16)
        act_lo = R.view(8192 + NF * 512, [NF, S], BF16)
        up_st = [R.view(30720 + 2048 * c, [KD, 2 * P]) for c in range(2)]
        up_hi = [R.view(34816 + 1024 * c, [KD, 2 * P], BF16) for c in range(2)]
        up_lo = [R.view(36864 + 1024 * c, [KD, 2 * P], BF16) for c in range(2)]
        y_up = [R.view(38912 + 2048 * c, [2, S]) for c in range(2)]
        prod = [R.view(43008 + 1024 * c, [S]) for c in range(2)]
        wcol = [stat_c.rearrange("p a b -> p (a b)")[:, 6 * c:6 * c + 6] for c in range(2)]
        dn_st = [R.view(45056 + 512 * c, [512]) for c in range(2)]
        dn_hi = [R.view(46080 + 256 * c, [512], BF16) for c in range(2)]
        dn_lo = [R.view(46592 + 256 * c, [512], BF16) for c in range(2)]
        gpost_ffn = R.view(47104, [D])
        x1r = [R.view(48128 + 1024 * c, [D]) for c in range(2)]
        y_dn = R.view(0, [NT, D])
        junk2 = R.view(30720, [D])
        junk = R.view(29696, [D])
        tq_ps = [psum[:, 4 + 2 * c:6 + 2 * c, :].rearrange("p a b -> p (a b)") for c in range(2)]
        up_ps = [psum[:, 4 * c:4 * c + 4, :].rearrange("p (g a) b -> p g (a b)", g=2) for c in range(2)]

        cm_ps = [psum[:, 2 * s:2 * s + 2, :].rearrange("p a b -> p (a b)") for s in range(2)]
        tm_ps = [psum[:, 4 + s, :] for s in range(2)]
        tp_ps = [psum[:, 6 + s, :] for s in range(2)]

        block = ctx.enter_context(nc.Block())
        x_d, w_in = a["x"], a["w_in"]

        def conf_transpose(pe, t):
            if t == 0:
                pe.wait_ge(sem("cc_conv"), 1)
                pe.wait_ge(sem("kT_out"), NT)
            if t >= 2:
                pe.wait_ge(sem("cc_tok"), t - 1)
            for c in range(2):
                ins = pe.transpose(tp_ps[t % 2][:, c * P:(c + 1) * P], cacc[:, c, t * P:(t + 1) * P], ident)
            ins.then_inc(sem("cc_tp"), 1)

        def conf_stats(v, t):
            v.wait_ge(sem("cc_tp"), t + 1)
            v.tensor_copy(ctok[:, t], tp_ps[t % 2][:, 0:CCH]).then_inc(sem("cc_tok"), 1)
            v.wait_ge(sem("cc_tok"), t + 1)
            v.bn_stats(lnst[:, t], ctok[:, t]).then_inc(sem("cc_st"), 1)
            v.wait_ge(sem("cc_st"), t + 1)
            v.bn_aggr(lnag[:, t], lnst[:, t]).then_inc(sem("cc_ag"), 1)

        def conf_dve(v):
            v.wait_ge(sem("cc_rt"), 1)
            v.reciprocal(lnr, rstd).then_inc(sem("cc_rs"), 1)
            v.wait_ge(sem("cc_rs"), 1)
            for t in range(NT):
                v.tensor_scalar(ctok[:, t], ctok[:, t], lnag[:, t, 0:1], lnr[:, t:t + 1], ALU.subtract, ALU.mult)\
                    .then_inc(sem("cc_nrm"), 1)

        def conf_back(pe):
            for t in range(NT):
                pe.wait_ge(sem("cc_nrm"), t + 1)
                if t == 0:
                    pe.wait_ge(sem("cat_out"), 4)
                for c in range(2):
                    ins = pe.transpose(cm_ps[c][:, t * P:(t + 1) * P], ctok[:, t, c * P:(c + 1) * P], ident)
            ins.then_inc(sem("cc_bk"), 1)

        def conf_act(act):
            act.wait_ge(sem("cc_ag"), NT)
            act.activation(rstd, lnag[:, :, 1], ACT.Sqrt, bias=eps_c).then_inc(sem("cc_rt"), 1)
            act.wait_ge(sem("cc_bk"), 1)
            for c in range(2):
                act.activation(cact[:, c], cm_ps[c], ACT.Silu, scale=pcol[:, PC_LNG + c:PC_LNG + c + 1],
                               bias=pcol[:, PC_LNB + c:PC_LNB + c + 1]).then_inc(sem("cc_act"), 1)
            act.wait_ge(sem("cc_act"), 2)
            act.wait_ge(sem("tm_done"), 3 * NT)
            act.activation(mix_hi[:, 6:8, :], cact, ACT.Copy).then_inc(sem("cc_hi"), 1)

        nsa_pt = [s for s in MIX if s[0] in ("Nq", "Nc2", "Nidx", "NT", "No")]

        def pt_use(step):
            return nsa_pt.index(step)

        nsa_slot = [s for s in nsa_pt if s[0] in ("Nc2", "NT")]

        def pts(step):
            return PTs[nsa_slot.index(step) % 2]

        def s_use(t, kind, h):
            return 2 * NH * t + NH * (1 - kind) + h

        def bd(dst, src, rows):
            c = slice(rows.start, rows.stop)
            return dst[rows, :, c], src[rows]

        LO, HI = slice(0, CH), slice(CH, P)

        def mixer_loads(sp):
            sp.dma_start(dtb, a["gdn_dt_bias"][0].partition_broadcast(P)).then_inc(sem("gp_in"), 16)
            sp.dma_start(alog, a["gdn_a_log"][0].partition_broadcast(P)).then_inc(sem("gp_in"), 16)
            sp.wait_ge(sem("wc_zero"), 1)
            for w, dst, name in (("nsa_cmp_wk", wck, "wck_in"), ("nsa_cmp_wv", wcv, "wcv_in")):
                if dst is wcv:
                    sp.wait_ge(sem("wc_zero"), 2)
                for kv in range(KV):
                    r = slice(HD * kv, HD * kv + HD)
                    sp.dma_start(dst[r, :, HD * kv:HD * kv + HD], a[w][0].rearrange("l d e -> d l e")).then_inc(sem(name), 16)
            sp.wait_ge(sem("vc_out"), 4)
            for p, kv in ((0, 0), (1, 1), (2, 1)):
                sp.dma_start(vcbd[CH:CH + NCMP, p, HD:P], qn.rearrange("p h d -> p (h d)")[0:NCMP, P + HD * kv:P + HD * kv + HD])\
                    .then_inc(sem("vcbd_in"), 16)

        def mixer_pool(pool):
            own = Count(sem("pool_own2"))

            def fill(m, value):
                own.up(pool.memset(m, value))

            def keep(m, pattern, base, cm, fill_, op=ALU.is_ge):
                own.settle(pool)
                own.up(pool.affine_select(out=m, in_=m, compare_op=op, fill=fill_, base=base, pattern=pattern, channel_multiplier=cm))

            pool.wait_ge(sem("w_hi"), 4 * len(BLOCKS))
            pool.wait_ge(sem("w_lo"), 4 * len(BLOCKS))
            fill(ones_c, 1.0)
            fill(tri, 1.0)
            keep(tri, [[1, NSLC], [-1, NSLC]], 0, 0, 0.0, ALU.is_gt)
            for m in (maskD, negI, Ic, Ucum, SL):
                fill(m, 0.0)
            for m in (Umask, strict):
                fill(m, 1.0)
            for m in (causal, far):
                fill(m, 0.0)
            fill(cmask, 0.0)
            fill(blk_of[0:NSLC], 1.0)
            fill(nm, -1.0)
            fill(half_ones[0], 0.0)
            fill(half_ones[1], 0.0)
            fill(forced, 0.0)
            fill(scored, 1.0)
            own.settle(pool)
            for rows in (LO, HI):
                keep(maskD[rows], [[1, CH]], 0, -1, NEG)
                keep(negI[rows], [[1, CH]], 0, -1, -1.0, ALU.not_equal)
                keep(Ic[rows], [[1, CH]], 0, -1, 1.0, ALU.not_equal)
                keep(Umask[rows], [[1, CH]], 0, -1, 0.0)
                keep(strict[rows], [[1, CH]], 0, -1, 0.0, ALU.is_gt)
                fill(Ucum[rows, rows], 1.0)
                fill(SL[rows, rows], 1.0)
                keep(Ucum[rows, rows], [[1, CH]], 0, -1, 0.0)
                keep(SL[rows, rows], [[-1, CH]], 0, 1, 0.0, ALU.is_gt)
                fill(half_ones[rows.start // CH][rows], 1.0)
                for l in range(LEVELS):
                    b = 1 << l
                    n = CH // (2 * b)
                    m = nm[rows, l].rearrange("p (n h c) -> p n h c", n=n, h=2)
                    own.settle(pool)
                    fill(m[:, :, 1], 0.0)
                    keep(m[:, :, 0], [[-2 * b, n], [0, b]], -b, 1, 0.0)
                    keep(m[:, :, 0], [[2 * b, n], [0, b]], 2 * b - 1, -1, 0.0)
                    keep(nm[rows, l], [[1, CH]], 0, -1, -1.0, ALU.not_equal)
            keep(causal, [[-1, P]], 0, 1, NEG)
            keep(far, [[1, P]], 0, -1, NEG, ALU.is_gt)
            keep(cmask, [[P, NT], [-STRIDE, CH]], -(CLEN - 1), 1, NEG)
            keep(blk_of[0:NSLC], [[1, S]], 0, -SLC, 0.0)
            keep(blk_of[0:NSLC], [[-1, S]], SLC - 1, SLC, 0.0)
            for i in range(4):
                for half, rows in enumerate((LO, HI)):
                    cur = 2 * (4 + i) + half
                    for c0, c1, value in ((0, 1, FORCE), (cur - 1, cur + 1, FORCE), (cur + 1, NSLC, -1.0)):
                        if c0 < c1:
                            fill(forced[rows, i, c0:c1], value)
                            fill(scored[rows, i, c0:c1], 0.0)
            own.settle(pool)
            pool.memset(rank, 0.0).then_inc(sem("mix_consts"), 1)
            pool.wait_ge(sem("tm_done"), 2 * NT)
            pool.memset(wck, 0.0).then_inc(sem("wc_zero"), 1)
            pool.wait_ge(sem("tm_done"), 3 * NT)
            pool.memset(wcv, 0.0).then_inc(sem("wc_zero"), 1)
            pool.wait_ge(sem("cc_hi"), 1)
            pool.tensor_tensor(mix_lo[:, 6:8, :], cact, mix_hi[:, 6:8, :], ALU.subtract).then_inc(sem("cc_lo"), 1)
            pool.wait_ge(sem("kc_mul"), 2)
            pool.wait_ge(sem("vc_mm"), 1)
            kc = qn.rearrange("p h d -> p (h d)")[:, 0:P]
            pool.memset(vcbd, 0.0).then_inc(sem("kc_zero"), 1)
            pool.memset(kc, 0.0).then_inc(sem("kc_zero"), 1)
            pool.wait_ge(sem("kc_zero"), 2)
            o = kc[0:NCMP].rearrange("p (h e d) -> p h e d", h=2, e=2)
            c_ = vn.rearrange("p h d -> p (h d)")[0:NCMP, 0:P].rearrange("p (h e d) -> p h e d", h=2, e=2)
            s_ = on.rearrange("p h d -> p (h d)")[0:NCMP, 0:P].rearrange("p (h e d) -> p h e d", h=2, e=2)
            pool.tensor_tensor(o[:, :, 0, :], c_[:, :, 0, :], s_[:, :, 1, :], ALU.subtract).then_inc(sem("kc_rot"), 1)
            pool.tensor_tensor(o[:, :, 1, :], s_[:, :, 0, :], c_[:, :, 1, :], ALU.add).then_inc(sem("kc_rot"), 1)
            pool.wait_ge(sem("kcT_out"), 1)
            pool.wait_ge(sem("vcbd_in"), 48)
            for m in (Sbd, kbTp, qTp, LTbd, Tbd, MIbd, QTbd[0], QTbd[1], qpad):
                pool.memset(m, 0.0).then_inc(sem("mix_zero"), 1)

            def scaled(dst, src, by, t):
                return pool.tensor_tensor(dst, src, bc(by[:, GH * t:GH * t + GH], 2, HD), ALU.mult)

            def A1b(t):
                pool.wait_ge(sem("g_n"), 2 * t + 2)
                scaled(kb, kn, beta, t).then_inc(sem("g_kq"), 1)
                scaled(qg, qn, EG, t).then_inc(sem("g_kq"), 1)
                pool.wait_ge(sem("g_kq"), 2 * t + 2)
                scaled(kbg, kb, EG, t).then_inc(sem("g_kk2"), 1)
                if t >= 2:
                    pool.wait_ge(sem("b_dm"), 2 * t - 2)
                scaled(kdec[t % 2], kn, ED, t).then_inc(sem("g_kk2"), 1)

            def A3a(t):
                if t:
                    pool.wait_ge(sem("g_uwm"), 2 * t)
                pool.tensor_tensor(Drhs, bc(Umask, 1, GH), bc(graw[:, GH * t:GH * t + GH], 2, CH), ALU.mult).then_inc(sem("g_drhs"), 1)
                pool.wait_ge(sem("g_DT"), t + 1)
                pool.tensor_tensor(DTs, DTc, bc(strict, 1, GH), ALU.mult).then_inc(sem("g_DTs"), 1)

            def A3b(t):
                pool.wait_ge(sem("g_QTc"), t + 1)
                if t >= 2:
                    pool.wait_ge(sem("b_o"), t - 1)
                for rows in (LO, HI):
                    d_, s_ = bd(QTbd[t % 2], QTc, rows)
                    pool.tensor_copy(d_, s_).then_inc(sem("g_QT"), 1)
                pool.wait_ge(sem("g_QT"), 2 * t + 2)

            def C1(t):
                pool.wait_ge(sem("c_on"), t + 1)
                pool.tensor_tensor(on, on, zab[:, t, 0:GDIM].rearrange("p (h d) -> p h d", h=GH), ALU.mult).then_inc(sem("c_og"), 1)

            def C2(t):
                pool.wait_ge(sem("c_hi"), t + 1)
                tok = slice(t * P, (t + 1) * P)
                pool.tensor_tensor(mix_lo[:, 0:3, tok], mtmp, mix_hi[:, 0:3, tok], ALU.subtract).then_inc(sem("m_lo"), 1)

            def Nc1(t):
                if t == 0:
                    pool.wait_ge(sem("n_pcn"), 1)
                    pool.affine_select(out=csc, in_=csc, compare_op=ALU.is_ge, fill=0.0, base=-(CLEN - 1),
                                       pattern=[[0, NH], [-STRIDE, CH]], channel_multiplier=1).then_inc(sem("n_pc0"), 1)

            def add(t, n):
                pool.wait_ge(sem("n_ot"), 2 * t + n + 1)
                pool.tensor_tensor(oacc, oacc, otmp, ALU.add).then_inc(sem("n_acc"), 1)

            def Nc3(t):
                add(t, 0)

            def Ne(t, kind):
                if kind == 0:
                    add(t, 1)

            def No(t):
                pool.wait_ge(sem("n_hi"), t + 1)
                tok = slice(t * P, (t + 1) * P)
                pool.tensor_tensor(mix_lo[:, 3:6, tok], mtmp_n, mix_hi[:, 3:6, tok], ALU.subtract).then_inc(sem("mn_lo"), 1)

            run(dict(A1b=A1b, A3a=A3a, A3b=A3b, C1n=C1, C2=C2, Nc1b=Nc1, Nc3=Nc3, Ne=Ne, No=No))

        def run(steps):
            for step in MIX:
                if step[0] in steps:
                    steps[step[0]](*step[1:])

        def mixer_act(act):
            flat = lambda x: x.rearrange("p h d -> p (h d)")
            act.preload_act_table_set("natural_log_exp_and_others")
            act.wait_ge(sem("gp_abs"), 1)
            act.wait_ge(sem("mix_consts"), 1)
            act.activation(stat_a, stat_b, ACT.Exp, scale=-1.0).then_inc(sem("gp_e"), 1)
            act.wait_ge(sem("gp_e"), 1)
            act.activation(stat_a, stat_a, ACT.Ln, bias=ones_c).then_inc(sem("gp_e"), 1)
            act.activation(alog, alog, ACT.Exp).then_inc(sem("gp_e"), 1)
            act.activation(stat_c, zab[:, :, GDIM + GH:], ACT.Exp, scale=-1.0).then_inc(sem("gp_e"), 1)
            act.activation(gate, gate, ACT.Exp, scale=-1.0).then_inc(sem("gp_e"), 1)
            act.wait_ge(sem("gp_cum"), 1)
            act.activation(EG, psum[:, 4, 0:48], ACT.Exp).then_inc(sem("gp_exp"), 1)
            act.activation(ED, psum[:, 4, 64:112], ACT.Exp).then_inc(sem("gp_exp"), 1)
            for c in range(2):
                for par, rows in enumerate((LO, HI)):
                    src = psum[rows, 4, 128 + 64 * c:176 + 64 * c].rearrange("p (t h e) -> p t h e", t=NT, e=2)[:, :, :, par]
                    act.activation(EGL[rows, :, c, :], src, ACT.Exp).then_inc(sem("gp_exp"), 1)
            act.wait_ge(sem("vc_mm"), 1)
            act.wait_ge(sem("kc_zero"), 2)
            vc = psum[0:NCMP, 1, 0:P]
            for p, kv in ((0, 0), (1, 0), (2, 1)):
                act.activation(vcbd[0:NCMP, p, 0:HD], vc[:, HD * kv:HD * kv + HD], ACT.Copy).then_inc(sem("vc_out"), 1)
            act.activation(flat(qn)[0:NCMP, P:2 * P], vc, ACT.Copy).then_inc(sem("vc_out"), 1)
            act.wait_ge(sem("kcT_mm"), 1)
            act.activation(kcT, psum[:, 2, 0:CH], ACT.Copy).then_inc(sem("kcT_out"), 1)

            def A1a(t):
                act.wait_ge(sem("g_qk"), t + 1)
                if t == 0:
                    act.wait_ge(sem("mix_zero"), 9)
                else:
                    act.wait_ge(sem("g_QT"), 2 * t)
                for i in range(2):
                    act.activation(flat(sq)[:, GDIM * i:GDIM * i + GDIM], psum[:, i, 0:GDIM], ACT.Square).then_inc(sem("g_sq"), 1)

            def A1s(t):
                act.wait_ge(sem("g_ss"), t + 1)
                act.activation(rs, ss, ACT.Ln, bias=eps_c).then_inc(sem("g_ln"), 1)
                act.wait_ge(sem("g_ln"), t + 1)
                act.activation(rs, rs, ACT.Exp, scale=-0.5).then_inc(sem("g_rs"), 1)

            def A2a(t):
                act.wait_ge(sem("g_t1"), 2 * t + 2)
                act.activation(kTn, psum[:, 1, 0:GDIM].rearrange("p (h c) -> p h c", h=3), ACT.Copy).then_inc(sem("g_kT"), 1)

            def A2b(t):
                act.wait_ge(sem("g_t2"), 2 * t + 2)
                ps = psum[:, 1, 0:GDIM].rearrange("p (h c) -> p h c", h=3)
                for par, rows in enumerate((LO, HI)):
                    act.activation(qTp[rows, :, par, :], ps[rows], ACT.Copy).then_inc(sem("g_qT"), 1)

            def A3a(t):
                act.wait_ge(sem("g_D"), t + 1)
                act.activation(flat(DTc), psum[:, 0, 0:GDIM], ACT.Exp).then_inc(sem("g_DT"), 1)

            def X(t, l):
                act.wait_ge(sem("g_Xm"), 4 * t + l)
                act.activation(flat(Xc), psum[:, 1, 0:GDIM], ACT.Copy).then_inc(sem("g_X"), 1)

            def XT(t, l):
                act.wait_ge(sem("g_Tm"), LEVELS * t + l + 1)
                act.activation(flat(Tc), psum[:, 0, 0:GDIM], ACT.Copy).then_inc(sem("g_Tc"), 1)

            def A4(t):
                act.wait_ge(sem("g_uwm"), 2 * t + 1)
                act.activation(flat(uu[t % 2]), psum[:, 0, 0:GDIM], ACT.Copy).then_inc(sem("g_uw"), 1)
                act.wait_ge(sem("g_uwm"), 2 * t + 2)
                act.activation(flat(nwT[t % 2]), psum[:, 1, 0:GDIM], ACT.Copy, scale=-1.0).then_inc(sem("g_uw"), 1)

            def C1(t):
                act.wait_ge(sem("b_o"), t + 1)
                if t:
                    act.wait_ge(sem("m_lo"), t)
                act.activation(flat(sq2), psum[:, 3, 0:GDIM], ACT.Square).then_inc(sem("c_sq"), 1)

            def C1s(t):
                act.wait_ge(sem("c_ss"), t + 1)
                act.activation(rs2, ss2, ACT.Ln, bias=eps_c, scale=1.0 / HD).then_inc(sem("c_ln"), 1)
                act.wait_ge(sem("c_ln"), t + 1)
                act.activation(rs2, rs2, ACT.Exp, scale=-0.5).then_inc(sem("c_rs"), 1)

            def C2(t):
                act.wait_ge(sem("c_tp"), t + 1)
                tok = slice(t * P, (t + 1) * P)
                act.activation(flat(mtmp), psum[:, 2, 0:GDIM], ACT.Copy, scale=gng).then_inc(sem("c_m"), 1)
                act.wait_ge(sem("c_m"), t + 1)
                act.activation(mix_hi[:, 0:3, tok], mtmp, ACT.Copy).then_inc(sem("c_hi"), 1)

            def Nq(t):
                act.wait_ge(sem("n_ptm"), pt_use(("Nq", t)) + 1)
                ps = psum[:, 6, 0:GDIM].rearrange("p (g c) -> p g c", g=GRP)
                act.activation(qpad[LO, 0], ps[LO], ACT.Copy).then_inc(sem("n_q"), 1)
                act.activation(qpad[HI, 1], ps[HI], ACT.Copy).then_inc(sem("n_pt"), 1)

            def Nc1(t):
                act.wait_ge(sem("n_csc"), t + 1)
                act.activation(flat(csc), flat(csc), ACT.Exp).then_inc(sem("n_cex"), 1)

            def Nc2(t):
                u = pt_use(("Nc2", t))
                act.wait_ge(sem("n_ptm"), u + 1)
                act.activation(pts(("Nc2", t))[:, 0:GDIM], psum[:, 6, 0:GDIM], ACT.Copy).then_inc(sem("n_pt"), 1)

            def Nidx(t):
                act.wait_ge(sem("n_ptm"), pt_use(("Nidx", t)) + 1)
                act.activation(selT[0:NSLC], psum[0:NSLC, 6, 0:2 * P].rearrange("p (k c) -> p k c", k=KV), ACT.Copy).then_inc(sem("n_pt"), 1)

            def Ns(t, kind, h):
                k0, k1 = key_blocks(t, kind)
                u = s_use(t, kind, h)
                n = (k1 - k0) * P
                act.wait_ge(sem("n_mx"), u + 1)
                act.activation(Pb[u % 2][:, 0:n], psum[:, 4:6, :].rearrange("p a b -> p (a b)")[:, 0:n], ACT.Exp,
                               bias=nmx[:, u % 2:u % 2 + 1], accum_out=psums[:, NH * kind + h:NH * kind + h + 1]).then_inc(sem("n_exp"), 1)

            def NT_(t, kind, h, n):
                u = pt_use(("NT", t, kind, h, n))
                b0, b1 = batches(t, kind)[n]
                act.wait_ge(sem("n_ptm"), u + 1)
                act.activation(pts(("NT", t, kind, h, n))[:, 0:(b1 - b0) * P], psum[:, 6, 0:(b1 - b0) * P], ACT.Copy).then_inc(sem("n_pt"), 1)

            def No(t):
                act.wait_ge(sem("n_ptm"), pt_use(("No", t)) + 1)
                tok = slice(t * P, (t + 1) * P)
                act.activation(flat(mtmp_n), psum[:, 6, 0:GDIM], ACT.Copy).then_inc(sem("n_pt"), 1)
                act.wait_ge(sem("n_pt"), pt_use(("No", t)) + 1)
                act.activation(mix_hi[:, 3:6, tok], mtmp_n, ACT.Copy).then_inc(sem("n_hi"), 1)

            run(dict(A1a=A1a, A1s=A1s, A2a=A2a, A2b=A2b, A3a=A3a, X=X, XT=XT, A4=A4, C1=C1, C1s=C1s, C2=C2, Nq=Nq, Nc1=Nc1, Nc2=Nc2,
                     Nidx=Nidx, Ns=Ns, NT=NT_, No=No))

        def mixer_dve(v):
            flat = lambda x: x.rearrange("p h d -> p (h d)")
            own = Count(sem("dve_own2"))

            def then(ins):
                own.up(ins)
                own.settle(v)

            v.wait_ge(sem("gp_in"), 32)
            v.wait_ge(sem("mix_consts"), 1)
            v.wait_ge(sem("tm_act"), 3 * NT)
            y3 = beta.rearrange("p (t h) -> p t h", h=GH)
            then(v.tensor_tensor(y3, zab[:, :, GDIM:GDIM + GH], bc(dtb, 1, NT), ALU.add))
            v.scalar_tensor_tensor(out=stat_b, in0=beta, scalar=-1.0, in1=beta, op0=ALU.mult, op1=ALU.max).then_inc(sem("gp_abs"), 1)
            v.wait_ge(sem("gp_e"), 5)
            then(v.scalar_tensor_tensor(out=graw, in0=beta, scalar=0.0, in1=stat_a, op0=ALU.max, op1=ALU.add))
            g3 = graw.rearrange("p (t h) -> p t h", h=GH)
            v.scalar_tensor_tensor(out=g3, in0=g3, scalar=-1.0, in1=bc(alog, 1, NT), op0=ALU.mult, op1=ALU.mult).then_inc(sem("graw"), 1)
            then(v.tensor_scalar(stat_c, stat_c, 1.0, None, ALU.add))
            then(v.reciprocal(beta.rearrange("p (t h) -> p t h", h=GH), stat_c))
            then(v.tensor_scalar(gate, gate, 1.0, None, ALU.add))
            then(v.reciprocal(gate, gate))
            v.wait_ge(sem("kc_mm"), 1)
            ps = psum[0:NCMP, 0, 0:P].rearrange("p (c d) -> p c d", d=32)
            for tab, dst in ((cos_t, vn), (sin_t, on)):
                v.tensor_tensor(flat(dst)[0:NCMP, 0:P].rearrange("p (c d) -> p c d", d=32), ps, bc(tab[0:NCMP, NT], 1, 4), ALU.mult)\
                    .then_inc(sem("kc_mul"), 1)
            v.wait_ge(sem("mix_zero"), 9)

            def A1r(t):
                v.wait_ge(sem("g_sq"), 2 * t + 2)
                v.tensor_reduce(ss, sq, AX.X, ALU.add).then_inc(sem("g_ss"), 1)

            def A1n(t):
                v.wait_ge(sem("g_rs"), t + 1)
                v.scalar_tensor_tensor(out=qn, in0=psum[:, 0, 0:GDIM].rearrange("p (h d) -> p h d", h=GH), scalar=HD ** -0.5,
                                       in1=bc(rs[:, 0:GH], 2, HD), op0=ALU.mult, op1=ALU.mult).then_inc(sem("g_n"), 1)
                v.tensor_tensor(kn, psum[:, 1, 0:GDIM].rearrange("p (h d) -> p h d", h=GH), bc(rs[:, GH:], 2, HD), ALU.mult)\
                    .then_inc(sem("g_n"), 1)

            def A1b(t):
                v.wait_ge(sem("g_v"), t + 1)
                v.tensor_tensor(vb, psum[:, 0, 0:GDIM].rearrange("p (h d) -> p h d", h=GH),
                                bc(beta[:, GH * t:GH * t + GH], 2, HD), ALU.mult).then_inc(sem("g_vb"), 1)

            def A2a(t):
                v.wait_ge(sem("g_t1"), 2 * t + 2)
                ps = psum[:, 0, 0:GDIM].rearrange("p (h c) -> p h c", h=3)
                for par, rows in enumerate((LO, HI)):
                    v.tensor_copy(kbTp[rows, :, par, :], ps[rows]).then_inc(sem("g_kbT"), 1)

            def A2b(t):
                v.wait_ge(sem("g_t2"), 2 * t + 2)
                v.tensor_copy(flat(qgT[t % 2]), psum[:, 0, 0:GDIM]).then_inc(sem("g_qgT"), 1)

            def A3a(t):
                v.wait_ge(sem("g_DTs"), t + 1)
                v.wait_ge(sem("g_kk"), t + 1)
                then(v.tensor_tensor(flat(LTc), psum[:, 1, 0:GDIM], flat(DTs), ALU.mult))
                for rows in (LO, HI):
                    d_, s_ = bd(LTbd, LTc, rows)
                    v.tensor_copy(d_, s_).then_inc(sem("g_LT"), 1)

            def A3b(t):
                v.wait_ge(sem("g_qk2"), t + 1)
                if t:
                    v.wait_ge(sem("g_QT"), 2 * t)
                v.tensor_tensor(flat(QTc), psum[:, 0, 0:GDIM], flat(DTc), ALU.mult).then_inc(sem("g_QTc"), 1)

            def M(t, l):
                v.wait_ge(sem("g_M"), LEVELS * t + l + 1)
                v.tensor_tensor(MIc, psum[:, 0, 0:GDIM].rearrange("p (h c) -> p h c", h=GH), bc(nm[:, l], 1, GH), ALU.mult)\
                    .then_inc(sem("g_MIc"), 1)
                v.wait_ge(sem("g_MIc"), LEVELS * t + l + 1)
                for rows in (LO, HI):
                    d_, s_ = bd(MIbd, MIc, rows)
                    v.tensor_copy(d_, s_).then_inc(sem("g_MI"), 1)

            def XT(t, l):
                v.wait_ge(sem("g_Tc"), LEVELS * t + l + 1)
                for rows in (LO, HI):
                    d_, s_ = bd(Tbd, Tc.rearrange("p h d -> p (h d)").rearrange("p (h c) -> p h c", h=GH), rows)
                    v.tensor_copy(d_, s_).then_inc(sem("g_Tbd"), 1)

            def B1(t, c):
                rows = (LO, HI)[c]
                n = 2 * t + c
                v.wait_ge(sem("b_vm"), n + 1)
                v.tensor_tensor(flat(vn)[rows], psum[rows, 2, 0:GDIM], flat(uu[t % 2])[rows], ALU.add).then_inc(sem("b_vn"), 1)
                v.wait_ge(sem("b_o1"), n + 1)
                then(v.tensor_tensor(Sbd, Sbd, bc(EGL[:, t, c], 2, P), ALU.mult))

            def B2(t, c):
                n = 2 * t + c
                v.wait_ge(sem("b_dm"), n + 1)
                ps = psum[:, 2, 0:GDIM].rearrange("p (h c) -> p h c", h=3)
                for rows in (LO, HI):
                    v.tensor_tensor(Sbd[rows, :, rows], Sbd[rows, :, rows], ps[rows, :, rows], ALU.add).then_inc(sem("b_S"), 1)

            def C1r(t):
                v.wait_ge(sem("c_sq"), t + 1)
                v.tensor_reduce(ss2, sq2, AX.X, ALU.add).then_inc(sem("c_ss"), 1)

            def C1n(t):
                v.wait_ge(sem("c_rs"), t + 1)
                v.tensor_tensor(on, psum[:, 3, 0:GDIM].rearrange("p (h d) -> p h d", h=GH), bc(rs2, 2, HD), ALU.mult).then_inc(sem("c_on"), 1)

            gates = gate.rearrange("p t (h k) -> p t h k", k=3)
            heads = lambda ap: ap.rearrange("p (h d) -> p h d", h=NH)

            def Nc1(t):
                v.wait_ge(sem("n_cm"), t + 1)
                ps = heads(psum[:, 4, 0:GDIM])
                then(v.tensor_reduce(cmx, ps, AX.X, ALU.max))
                if t:
                    v.wait_ge(sem("n_ptm"), pt_use(("Nc2", t - 1)) + 1)
                v.tensor_tensor(csc, ps, bc(cmx, 2, CH), ALU.subtract).then_inc(sem("n_csc"), 1)

            def Nc1b(t):
                v.wait_ge(sem("n_cex"), t + 1)
                then(v.tensor_reduce(csum, csc, AX.X, ALU.add))
                then(v.reciprocal(csum, csum))
                v.tensor_tensor(csc, csc, bc(csum, 2, CH), ALU.mult).then_inc(sem("n_pcn"), 1)

            def Nc3(t):
                v.wait_ge(sem("n_om"), 3 * t + 2)
                if t:
                    v.wait_ge(sem("mn_lo"), t)
                v.tensor_tensor(otmp, heads(psum[:, 7, 0:GDIM]), bc(gates[:, t, :, 0], 2, HD), ALU.mult).then_inc(sem("n_ot"), 1)

            def Nr(t, kv, part):
                i4 = t - 4
                of_i, of_j = bc(imp, 1, NSLC), bc(imp, 2, NSLC)
                if part == 0:
                    pcs = csc[:, GRP * kv:GRP * kv + GRP].rearrange("p g n -> p n g")
                    if kv == 0:
                        then(v.memset(pg[:, 0:1], 0.0))
                    then(v.tensor_reduce(pg[:, 1:1 + CH], pcs, AX.X, ALU.add))
                    then(v.tensor_reduce(imp, pg[:, 1:1 + CH].rearrange("p (j i) -> p j i", i=4), AX.X, ALU.add))
                elif part == 1:
                    then(v.tensor_tensor(imp, imp, pg[:, 0:CH].rearrange("p (j i) -> p j i", i=4)[:, :, 0], ALU.add))
                    then(v.tensor_tensor(imp, imp, scored[:, i4], ALU.mult))
                    then(v.tensor_tensor(imp, imp, forced[:, i4], ALU.add))
                elif part == 2:
                    then(v.tensor_tensor(cmpe, of_i, of_j, ALU.is_equal))
                    then(v.tensor_tensor(cmpe, cmpe, tri, ALU.mult))
                    then(v.tensor_tensor(cmpg, of_i, of_j, ALU.is_gt))
                else:
                    then(v.tensor_tensor(cmpg, cmpg, cmpe, ALU.add))
                    then(v.tensor_reduce(rank, cmpg, AX.X, ALU.add))
                    if kv == 0 and i4:
                        v.wait_ge(sem("n_ptm"), pt_use(("Nidx", t - 1)) + 1)
                    v.tensor_scalar(selb[:, kv], rank, float(TOPK), NEG, ALU.is_ge, ALU.mult).then_inc(sem("n_sel"), 1)

            def Ns(t, kind, h):
                k0, k1 = key_blocks(t, kind)
                u = s_use(t, kind, h)
                n = (k1 - k0) * P
                v.wait_ge(sem("n_sm"), u + 1)
                v.tensor_reduce(nmx[:, u % 2:u % 2 + 1], psum[:, 4:6, :].rearrange("p a b -> p (a b)")[:, 0:n], AX.X, ALU.max,
                                negate=True).then_inc(sem("n_mx"), 1)

            def Ne(t, kind):
                v.wait_ge(sem("n_exp"), s_use(t, kind, NH - 1) + 1)
                then(v.reciprocal(coef, psums[:, NH * kind:NH * kind + NH]))
                then(v.tensor_tensor(coef, coef, gates[:, t, :, 1 + kind], ALU.mult))
                v.wait_ge(sem("n_om"), 3 * t + (1 if kind else 3))
                o = heads(psum[:, 7, 0:GDIM])
                if kind:
                    if t:
                        v.wait_ge(sem("n_ptm"), pt_use(("No", t - 1)) + 1)
                    v.tensor_tensor(oacc, o, bc(coef, 2, HD), ALU.mult).then_inc(sem("n_oc"), 1)
                else:
                    v.wait_ge(sem("n_acc"), 2 * t + 1)
                    v.tensor_tensor(otmp, o, bc(coef, 2, HD), ALU.mult).then_inc(sem("n_ot"), 1)

            run(dict(A1r=A1r, A1n=A1n, A1b=A1b, A2a=A2a, A2b=A2b, A3a=A3a, A3b=A3b, M=M, XT=XT, B1=B1, B2=B2, C1r=C1r,
                     C1n=C1n, Nc1=Nc1, Nc1b=Nc1b, Nc3=Nc3, Nr=Nr, Ns=Ns, Ne=Ne))

        def mixer_pe(pe):
            pe.wait_ge(sem("graw"), 1)
            pe.wait_ge(sem("mix_consts"), 1)
            pe.wait_ge(sem("tm_act"), 3 * NT)
            pe.wait_ge(sem("rot_mul"), 2 * NT)
            for i, m in enumerate((Ucum, SL, half_ones[0], half_ones[1])):
                ins = pe.matmul(psum[:, 4, 64 * i:64 * i + 48], m, graw, start=True, stop=True)
            ins.then_inc(sem("gp_cum"), 1)
            for cat, w, bank, name, out_ in ((kcat, wck, 0, "wck_in", "kc_mm"), (vcat, wcv, 1, "wcv_in", "vc_mm")):
                pe.wait_ge(sem(name), 32)
                pe.wait_ge(sem("cc_act"), 2)
                for l in range(CLEN):
                    lhs = cat[:, l // STRIDE, l:l + STRIDE * (NCMP - 1) + 1:STRIDE]
                    ins = pe.matmul(psum[0:NCMP, bank, 0:P], lhs, w[:, l], start=(l == 0), stop=(l == CLEN - 1))
                ins.then_inc(sem(out_), 1)
            pe.wait_ge(sem("kc_rot"), 2)
            pe.transpose(psum[:, 2, 0:CH], qn.rearrange("p h d -> p (h d)")[0:CH, 0:P], ident[0:CH, 0:CH]).then_inc(sem("kcT_mm"), 1)
            pe.wait_ge(sem("mix_zero"), 9)

            def blocks(bank, src, s):
                for p in range(3):
                    ins = pe.transpose(psum[:, bank, p * P:(p + 1) * P], src[:, p * P:(p + 1) * P], ident)
                return ins.then_inc(sem(s), 1)

            flat = lambda x: x.rearrange("p h d -> p (h d)")

            def A1a(t):
                if t:
                    pe.wait_ge(sem("g_uw"), 2 * t)
                tok = slice(t * P, (t + 1) * P)
                for i in range(2):
                    for p in range(3):
                        ins = pe.transpose(psum[:, i, p * P:(p + 1) * P], qkvT[:, 3 * i + p, tok], ident)
                ins.then_inc(sem("g_qk"), 1)

            def A1b(t):
                pe.wait_ge(sem("g_n"), 2 * t + 2)
                tok = slice(t * P, (t + 1) * P)
                for p in range(3):
                    ins = pe.transpose(psum[:, 0, p * P:(p + 1) * P], qkvT[:, 6 + p, tok], ident)
                ins.then_inc(sem("g_v"), 1)

            def A2a(t):
                blocks(1, flat(kn), "g_t1")
                pe.wait_ge(sem("g_vb"), t + 1)
                pe.wait_ge(sem("g_kq"), 2 * t + 2)
                blocks(0, flat(kb), "g_t1")

            def A2b(t):
                pe.wait_ge(sem("g_kT"), t + 1)
                blocks(1, flat(qn), "g_t2")
                pe.wait_ge(sem("g_kbT"), 2 * t + 2)
                blocks(0, flat(qg), "g_t2")

            def products(bank, rhs, s):
                for c, rows in enumerate((LO, HI)):
                    for p in range(3):
                        ins = pe.matmul(psum[rows, bank, p * P:(p + 1) * P].rearrange("p (e i) -> p e i", e=2),
                                        kTn[:, p, rows], rhs[:, p, :, rows], start=True, stop=True)
                ins.then_inc(sem(s), 1)

            def A3a(t):
                pe.wait_ge(sem("g_qgT"), t + 1)
                pe.wait_ge(sem("g_drhs"), t + 1)
                o = psum[:, 0, 0:GDIM].rearrange("p (h c) -> p h c", h=GH)
                pe.matmul(o, identb, bc(maskD, 1, GH), start=True, stop=True, skip_group_check=True)
                pe.matmul(o, SL, Drhs, start=False, stop=True, skip_group_check=True).then_inc(sem("g_D"), 1)
                pe.wait_ge(sem("g_qT"), 2 * t + 2)
                products(1, kbTp, "g_kk")

            def A3b(t):
                pe.wait_ge(sem("g_DT"), t + 1)
                products(0, qTp, "g_qk2")

            def M(t, l):
                if l == 0:
                    pe.wait_ge(sem("g_QTc"), t + 1)
                    pe.wait_ge(sem("g_LT"), 2 * t + 2)
                else:
                    pe.wait_ge(sem("g_Tc"), LEVELS * t + l)
                    if l >= 2:
                        pe.wait_ge(sem("g_X"), 4 * t + l - 1)
                o = psum[:, 0, 0:GDIM].rearrange("p (h c) -> p h c", h=GH)
                pe.matmul(o, identb, bc(negI, 1, GH), start=True, stop=True, skip_group_check=True)
                x = [Ic] * GH if l == 0 else [(MIc if l == 1 else Xc)[:, h] for h in range(GH)]
                for h in range(GH):
                    ins = pe.matmul(o[:, h], LTbd[:, h], x[h], start=False, stop=True, skip_group_check=True)
                ins.then_inc(sem("g_M"), 1)

            def X(t, l):
                pe.wait_ge(sem("g_MIc"), LEVELS * t + l + 1)
                pe.wait_ge(sem("g_Tbd"), 2 * (LEVELS * t + l))
                for h in range(GH):
                    ins = pe.matmul(psum[:, 1, h * CH:(h + 1) * CH], Tbd[:, h], MIc[:, h], start=True, stop=True)
                ins.then_inc(sem("g_Xm"), 1)

            def XT(t, l):
                pe.wait_ge(sem("g_MI"), 2 * (LEVELS * t + l + 1))
                tc_ = Tc.rearrange("p h d -> p (h d)")
                for h in range(GH):
                    r = Ic if l == 0 else tc_[:, h * CH:(h + 1) * CH]
                    ins = pe.matmul(psum[:, 0, h * CH:(h + 1) * CH], MIbd[:, h], r, start=True, stop=True)
                ins.then_inc(sem("g_Tm"), 1)

            def A4(t):
                pe.wait_ge(sem("g_Tbd"), 2 * LEVELS * (t + 1))
                pe.wait_ge(sem("g_kk2"), 2 * t + 2)
                for h in range(GH):
                    ins = pe.matmul(psum[:, 0, h * HD:(h + 1) * HD], Tbd[:, h], vb[:, h], start=True, stop=True)
                ins.then_inc(sem("g_uwm"), 1)
                for h in range(GH):
                    rows = (LO, HI)[h % 2]
                    ins = pe.matmul(psum[rows, 1, (h // 2) * P:(h // 2 + 1) * P], kbg[:, h], Tbd[:, h], start=True, stop=True)
                ins.then_inc(sem("g_uwm"), 1)

            def B1(t, c):
                n = 2 * t + c
                rows = (LO, HI)[c]
                pe.wait_ge(sem("g_uw"), 2 * t + 2)
                if n:
                    pe.wait_ge(sem("b_S"), 2 * n)
                if c == 0 and t:
                    pe.wait_ge(sem("c_m"), t)
                for p in range(3):
                    ins = pe.matmul(psum[rows, 2, p * P:(p + 1) * P], nwT[t % 2][:, p, rows], Sbd[:, p], start=True, stop=True)
                ins.then_inc(sem("b_vm"), 1)
                if c == 0 and t:
                    pe.wait_ge(sem("c_on"), t)
                for p in range(3):
                    ins = pe.matmul(psum[rows, 3, p * P:(p + 1) * P], qgT[t % 2][:, p, rows], Sbd[:, p], start=(p == 0), stop=True,
                                    skip_group_check=True)
                ins.then_inc(sem("b_o1"), 1)

            def B2(t, c):
                rows = (LO, HI)[c]
                pe.wait_ge(sem("b_vn"), 2 * t + c + 1)
                for p in range(3):
                    ins = pe.matmul(psum[:, 2, p * P:(p + 1) * P], flat(kdec[t % 2])[rows, p * P:(p + 1) * P],
                                    flat(vn)[rows, p * P:(p + 1) * P], start=True, stop=True)
                ins.then_inc(sem("b_dm"), 1)

            def B3(t):
                pe.wait_ge(sem("g_QT"), 2 * t + 2)
                for h in range(GH):
                    ins = pe.matmul(psum[:, 3, h * HD:(h + 1) * HD], QTbd[t % 2][:, h], vn[:, h], start=False, stop=True,
                                    skip_group_check=True)
                ins.then_inc(sem("b_o"), 1)

            def C2(t):
                pe.wait_ge(sem("c_og"), t + 1)
                pe.wait_ge(sem("b_S"), 4 * t + 4)
                blocks(2, flat(on), "c_tp")

            def pt_free(step):
                u = pt_use(step)
                if u:
                    pe.wait_ge(sem("n_pt"), u)

            def Nq(t):
                pt_free(("Nq", t))
                for g in range(GRP):
                    ins = pe.transpose(psum[:, 6, g * P:(g + 1) * P], qr[:, t, g].rearrange("p k d -> p (k d)"), ident)
                ins.then_inc(sem("n_ptm"), 1)

            def Nc1(t):
                pe.wait_ge(sem("n_pt"), pt_use(("Nq", t)) + 1)
                pe.wait_ge(sem("n_q"), t + 1)
                if t:
                    pe.wait_ge(sem("n_exp"), 2 * NH * t)
                else:
                    pe.wait_ge(sem("gp_exp"), 6)
                o = psum[:, 4, 0:GDIM].rearrange("p (h c) -> p h c", h=NH)
                pe.matmul(o, identb, bc(cmask[:, t], 1, NH), start=True, stop=True, skip_group_check=True)
                for h in range(NH):
                    ins = pe.matmul(o[:, h], qpad[:, h // GRP, h % GRP], kcT, start=False, stop=True, skip_group_check=True)
                ins.then_inc(sem("n_cm"), 1)

            def Nc2(t):
                pt_free(("Nc2", t))
                pe.wait_ge(sem("n_pc0"), 1) if t == 0 else pe.wait_ge(sem("n_pcn"), t + 1)
                for p in range(3):
                    ins = pe.transpose(psum[:, 6, p * P:(p + 1) * P], csc.rearrange("p h c -> p (h c)")[:, p * P:(p + 1) * P], ident)
                ins.then_inc(sem("n_ptm"), 1)

            def o_free(n):
                t, k = divmod(n, 3)
                if k == 0 and t:
                    pe.wait_ge(sem("n_ot"), 2 * t)
                elif k == 1:
                    pe.wait_ge(sem("n_oc"), t + 1)
                elif k == 2:
                    pe.wait_ge(sem("n_ot"), 2 * t + 1)

            def Nc3(t):
                u = pt_use(("Nc2", t))
                pe.wait_ge(sem("n_pt"), u + 1)
                o_free(3 * t + 1)
                for p in range(3):
                    ins = pe.matmul(psum[:, 7, p * P:(p + 1) * P], pts(("Nc2", t))[:, p * P:(p + 1) * P], vcbd[:, p], start=True, stop=True)
                ins.then_inc(sem("n_om"), 1)

            def Nidx(t):
                pt_free(("Nidx", t))
                pe.wait_ge(sem("n_sel"), 2 * (t - 3))
                for kv in range(KV):
                    ins = pe.transpose(psum[0:NSLC, 6, kv * P:(kv + 1) * P], selb[:, kv], ident)
                ins.then_inc(sem("n_ptm"), 1)

            def Ns(t, kind, h):
                k0, k1 = key_blocks(t, kind)
                u = s_use(t, kind, h)
                kv, g = divmod(h, GRP)
                if u % (2 * NH):
                    pe.wait_ge(sem("n_exp"), u)
                else:
                    pe.wait_ge(sem("n_csc"), t + 1)
                if kind == 0 and h == 0 and t >= 4:
                    pe.wait_ge(sem("n_pt"), pt_use(("Nidx", t)) + 1)
                for c0 in range(k0, k1, 4):
                    c1 = min(c0 + 4, k1)
                    bank = 4 + (c0 - k0) // 4
                    o = psum[:, bank, 0:(c1 - c0) * P]
                    last = c1 == k1
                    sel = kind == 0 and t >= 4
                    far_c = kind == 1 and t >= WINDOW // P and c0 == k0
                    ins = pe.matmul(o, qpad[:, kv, g], kT2[:, kind, c0 * P:c1 * P], start=True, stop=True, skip_group_check=True)
                    if sel:
                        ins = pe.matmul(o, selT[0:NSLC, kv], blk_of[0:NSLC, c0 * P:c1 * P], start=False, stop=True,
                                    skip_group_check=True)
                    if far_c:
                        ins = pe.matmul(o[:, 0:P], identb, far, start=False, stop=True, skip_group_check=True)
                    if last:
                        ins = pe.matmul(o[:, (c1 - c0 - 1) * P:], identb, causal, start=False, stop=True, skip_group_check=True)
                ins.then_inc(sem("n_sm"), 1)

            def NT_(t, kind, h, n):
                step = ("NT", t, kind, h, n)
                pt_free(step)
                u = s_use(t, kind, h)
                pe.wait_ge(sem("n_exp"), u + 1)
                k0, _ = key_blocks(t, kind)
                b0, b1 = batches(t, kind)[n]
                for b in range(b0, b1):
                    ins = pe.transpose(psum[:, 6, (b - b0) * P:(b - b0 + 1) * P], Pb[u % 2][:, (b - k0) * P:(b - k0 + 1) * P], ident)
                ins.then_inc(sem("n_ptm"), 1)

            def NV(t, kind, h, n):
                u = pt_use(("NT", t, kind, h, n))
                pe.wait_ge(sem("n_pt"), u + 1)
                if h == 0 and n == 0:
                    o_free(3 * t + 2 * (1 - kind))
                k0, k1 = key_blocks(t, kind)
                b0, b1 = batches(t, kind)[n]
                kv = h // GRP
                for b in range(b0, b1):
                    ins = pe.matmul(psum[:, 7, h * HD:(h + 1) * HD], pts(("NT", t, kind, h, n))[:, (b - b0) * P:(b - b0 + 1) * P],
                                    vsw[:, b, kind, kv * HD:kv * HD + HD], start=(h == 0 and b == k0), stop=True,
                                    skip_group_check=True)
                if h == NH - 1 and b1 == k1:
                    ins.then_inc(sem("n_om"), 1)

            def No(t):
                pt_free(("No", t))
                pe.wait_ge(sem("n_acc"), 2 * t + 2)
                for p in range(3):
                    ins = pe.transpose(psum[:, 6, p * P:(p + 1) * P], flat(oacc)[:, p * P:(p + 1) * P], ident)
                ins.then_inc(sem("n_ptm"), 1)

            run(dict(A1a=A1a, A1b=A1b, A2a=A2a, A2b=A2b, A3a=A3a, A3b=A3b, M=M, X=X, XT=XT, A4=A4, B1=B1, B2=B2, B3=B3,
                     C2=C2, Nq=Nq, Nc1=Nc1, Nc2=Nc2, Nc3=Nc3, Nidx=Nidx, Ns=Ns, NT=NT_, NV=NV, No=No))

        W_ORDER = [x for t in range(NT + 1) for x in ([("W1", t)] if t < NT else []) + ([("W2", t - 1)] if t else [])]

        def wrun(steps):
            for name, t in W_ORDER:
                steps[name](t)

        def wout_loads(sp):
            for c in range(KD):
                if c < 4:
                    sp.wait_ge(sem("m_lo"), NT)
                    sp.wait_ge(sem("mn_lo"), NT)
                    sp.wait_ge(sem("b_S"), 4 * NT)
                else:
                    sp.wait_ge(*late("wo_lo", c - 3))
                if c == 4:
                    sp.dma_start(gpost_mix, a["norm_mix_post"][0].partition_broadcast(P)).then_inc(sem("gpost_in"), 16)
                sp.dma_start(wo_st[c % 4], a["w_out"][0, c * P:(c + 1) * P, :]).then_inc(late(f"wo_st{c % 4}")[0], 16)
            for t in range(2):
                sp.dma_start(xr[t], x_d[0, t * P:(t + 1) * P, :]).then_inc(late(f"xr_in{t}")[0], 16)
            for t in range(NT):
                sp.wait_ge(*late("x1", t + 1))
                sp.dma_start(scratch[t * P:(t + 1) * P, :], x1[t % 2]).then_inc(sem(f"x1_st{t % 2}"), 16)
                if t + 2 < NT:
                    sp.dma_start(xr[t % 2], x_d[0, (t + 2) * P:(t + 3) * P, :]).then_inc(late(f"xr_in{t % 2}")[0], 16)

        def wout_act(act):
            for c in range(KD):
                act.wait_ge(*late(f"wo_st{c % 4}", 16 * (c // 4 + 1)))
                act.activation(wo_hi[:, c], wo_st[c % 4], ACT.Copy).then_inc(late("wo_hi")[0], 1)

            def W1(t):
                act.wait_ge(*late("wo_mm", t + 1))
                act.activation(junk, cm_ps[t % 2], ACT.Square, accum_out=wss[:, t:t + 1]).then_inc(late("w_sq")[0], 1)
                act.wait_ge(*late("w_sq", t + 1))
                act.activation(wrs[:, t:t + 1], wss[:, t:t + 1], ACT.Ln, bias=eps_c, scale=1.0 / D).then_inc(late("w_ln")[0], 1)
                act.wait_ge(*late("w_ln", t + 1))
                act.activation(wrs[:, t:t + 1], wrs[:, t:t + 1], ACT.Exp, scale=-0.5).then_inc(late("w_rs")[0], 1)

            def W2(t):
                act.wait_ge(*late("x1", t + 1))
                act.activation(junk, x1[t % 2], ACT.Square, accum_out=wss[:, NT + t:NT + t + 1]).then_inc(late("v_sq")[0], 1)
                act.wait_ge(*late("v_sq", t + 1))
                act.activation(wrs[:, NT + t:NT + t + 1], wss[:, NT + t:NT + t + 1], ACT.Ln, bias=eps_c, scale=1.0 / D).then_inc(late("v_ln")[0], 1)
                act.wait_ge(*late("v_ln", t + 1))
                act.activation(wrs[:, NT + t:NT + t + 1], wrs[:, NT + t:NT + t + 1], ACT.Exp, scale=-0.5).then_inc(late("v_rs")[0], 1)
                act.wait_ge(*late("v_hg", t + 1))
                act.activation(h2_hi[:, :, t * P:(t + 1) * P], hg2[t % 2], ACT.Copy).then_inc(late("v_hi")[0], 1)

            wrun(dict(W1=W1, W2=W2))

        def wout_pool(pool):
            for c in range(KD):
                pool.wait_ge(*late("wo_hi", c + 1))
                pool.tensor_tensor(wo_lo[:, c], wo_st[c % 4], wo_hi[:, c], ALU.subtract).then_inc(late("wo_lo")[0], 1)

            def W1(t):
                pool.wait_ge(*late("w_y", t + 1))
                pool.wait_ge(*late(f"xr_in{t % 2}", 16 * (t // 2 + 1)))
                pool.tensor_tensor(x1[t % 2], x1[t % 2], xr[t % 2], ALU.add).then_inc(late("x1")[0], 1)

            def W2(t):
                pool.wait_ge(*late("v_hi", t + 1))
                tok = slice(t * P, (t + 1) * P)
                pool.tensor_tensor(h2_lo[:, :, tok], hg2[t % 2], h2_hi[:, :, tok], ALU.subtract).then_inc(late("v_lo")[0], 1)

            wrun(dict(W1=W1, W2=W2))

        def wout_dve(v):
            v.wait_ge(sem("gpost_in"), 16)

            def W1(t):
                v.wait_ge(*late("w_rs", t + 1))
                if t >= 2:
                    v.wait_ge(sem(f"x1_st{t % 2}"), 16 * (t // 2))
                v.scalar_tensor_tensor(out=x1[t % 2], in0=cm_ps[t % 2], scalar=wrs[:, t:t + 1], in1=gpost_mix,
                                       op0=ALU.mult, op1=ALU.mult).then_inc(late("w_y")[0], 1)

            def W2(t):
                v.wait_ge(*late("v_rs", t + 1))
                v.tensor_scalar(hn2[t % 2], x1[t % 2], wrs[:, NT + t:NT + t + 1], None, ALU.mult).then_inc(late("v_hn")[0], 1)
                v.wait_ge(*late("v_tp", t + 1))
                if t >= 2:
                    v.wait_ge(*late("v_lo", t - 1))
                v.tensor_tensor(hg2[t % 2], tq_ps[t % 2].rearrange("p (k c) -> p k c", k=KD), bc(pcol[:, PC_GFFN:PC_GFFN + KD], 2, P),
                                ALU.mult).then_inc(late("v_hg")[0], 1)

            wrun(dict(W1=W1, W2=W2))

        def three(pe, outs, lhs, rhs, first):
            for part, side in ((0, 0), (0, 1), (1, 0)):
                for o, r in zip(outs, rhs):
                    ins = pe.matmul(o, lhs[part], r[side], start=first and part == side == 0, stop=True, skip_group_check=True)
            return ins

        def wout_pe(pe):
            pe.wait_ge(*late("wo_lo", KD))
            pe.wait_ge(sem("cc_lo"), 1)
            pe.wait_ge(sem("m_lo"), NT)
            pe.wait_ge(sem("mn_lo"), NT)

            def W1(t):
                if t >= 2:
                    pe.wait_ge(*late("w_y", t - 1))
                tok = slice(t * P, (t + 1) * P)
                for k in range(KD):
                    ins = three(pe, [cm_ps[t % 2][:, 0:512], cm_ps[t % 2][:, 512:1024]], (mix_hi[:, k, tok], mix_lo[:, k, tok]),
                                [(wo_hi[:, k, h * 512:(h + 1) * 512], wo_lo[:, k, h * 512:(h + 1) * 512]) for h in range(2)], k == 0)
                ins.then_inc(late("wo_mm")[0], 1)

            def W2(t):
                pe.wait_ge(*late("v_hn", t + 1))
                if t >= 2:
                    pe.wait_ge(*late("v_hg", t - 1))
                for k in range(KD):
                    ins = pe.transpose(tq_ps[t % 2][:, k * P:(k + 1) * P], hn2[t % 2][:, k * P:(k + 1) * P], ident)
                ins.then_inc(late("v_tp")[0], 1)

            wrun(dict(W1=W1, W2=W2))

        def up_load(sp, j, s):
            for g in range(2):
                sp.dma_start(up_st[s][:, :, g * P:(g + 1) * P],
                             a["ffn_w_up"][0].rearrange("(k p) n -> p k n", p=P)[:, :, bass.ds(j * P + g * DFF, P)])\
                    .then_inc(late(f"up_st{s}")[0], 16)

        def up_loads(sp):
            sp.wait_ge(sem("mn_lo"), NT)
            sp.wait_ge(sem("m_lo"), NT)
            for s in range(2):
                up_load(sp, s, s)
            with sp.Fori(1, NF // 2) as i:
                for s in range(2):
                    sp.wait_ge(*late("up_lo", 2 * i + s - 1))
                    up_load(sp, 2 * i + s, s)

        def up_act(act):
            def split(i, s, after):
                act.wait_ge(*late(f"up_st{s}", 32 * i + 32))
                if after is not None:
                    act.wait_ge(*late("up_mm", after))
                act.activation(up_hi[s], up_st[s], ACT.Copy).then_inc(late("up_hi")[0], 1)

            def body(i, more):
                for s in range(2):
                    j = 2 * i + s
                    act.wait_ge(*late("up_mm", j + 1))
                    act.wait_ge(*late("wcol", j + 1))
                    for g in range(2):
                        act.activation(y_up[s][:, g], up_ps[s][:, g], ACT.Copy, scale=wcol[s][:, 4 + g:5 + g]).then_inc(late("up_tap")[0], 1)
                    if more:
                        split(i + 1, s, j + 1)
                    act.wait_ge(*late("up_conv", 2 * j + 1))
                    act.activation(y_up[s][:, 0], y_up[s][:, 0], ACT.Silu).then_inc(late("up_silu")[0], 1)
                    act.wait_ge(*late("up_prod", j + 1))
                    act.activation(act_hi[:, bass.ds(j, 1)].rearrange('p o c -> p (o c)'), prod[s], ACT.Copy).then_inc(late("a_hi")[0], 1)

            split(0, 0, None)
            split(0, 1, None)
            with act.Fori(0, NF // 2 - 1) as i:
                body(i, True)
            body(NF // 2 - 1, False)

        def up_pool(pool):
            def split(s, n):
                pool.wait_ge(*late("up_hi", n))
                pool.tensor_tensor(up_lo[s], up_st[s], up_hi[s], ALU.subtract).then_inc(late("up_lo")[0], 1)

            def body(i, more):
                for s in range(2):
                    j = 2 * i + s
                    if more:
                        split(s, j + 3)
                    pool.wait_ge(*late("up_silu", j + 1))
                    pool.wait_ge(*late("up_conv", 2 * j + 2))
                    pool.tensor_tensor(prod[s], y_up[s][:, 0], y_up[s][:, 1], ALU.mult).then_inc(late("up_prod")[0], 1)
                    pool.wait_ge(*late("a_hi", j + 1))
                    pool.tensor_tensor(act_lo[:, bass.ds(j, 1)].rearrange('p o c -> p (o c)'), prod[s], act_hi[:, bass.ds(j, 1)].rearrange('p o c -> p (o c)'), ALU.subtract).then_inc(late("a_lo")[0], 1)

            split(0, 1)
            split(1, 2)
            with pool.Fori(0, NF // 2 - 1) as i:
                body(i, True)
            body(NF // 2 - 1, False)

        def up_dve(v):
            taps = pcol[:, PC_FCONV:PC_FCONV + 6 * NF].rearrange("p (l j) -> p l j", j=NF)

            def body(i, first):
                for s in range(2):
                    j = 2 * i + s
                    if not first:
                        v.wait_ge(*late("up_tap", 4 * i + 2 * s - 2))
                    v.tensor_copy(wcol[s], taps[:, :, bass.ds(j, 1)].rearrange('p l o -> p (l o)')).then_inc(late("wcol")[0], 1)
                    v.wait_ge(*late("wcol", j + 1))
                    v.wait_ge(*late("up_tap", 2 * j + 2))
                    for g in range(2):
                        ps = up_ps[s][:, g]
                        v.scalar_tensor_tensor(out=y_up[s][:, g, 1:S], in0=ps[:, 0:S - 1], scalar=wcol[s][:, 2 + g:3 + g],
                                               in1=y_up[s][:, g, 1:S], op0=ALU.mult, op1=ALU.add).then_inc(late("up_c1")[0], 1)
                        v.wait_ge(*late("up_c1", 2 * j + g + 1))
                        v.scalar_tensor_tensor(out=y_up[s][:, g, 2:S], in0=ps[:, 0:S - 2], scalar=wcol[s][:, g:g + 1],
                                               in1=y_up[s][:, g, 2:S], op0=ALU.mult, op1=ALU.add).then_inc(late("up_conv")[0], 1)

            body(0, True)
            with v.Fori(1, NF // 2) as i:
                body(i, False)

        def up_pe(pe):
            pe.wait_ge(*late("v_lo", NT))

            def body(i, first):
                for s in range(2):
                    j = 2 * i + s
                    pe.wait_ge(*late("up_lo", j + 1))
                    if not first:
                        pe.wait_ge(*late("up_conv", 2 * j - 2))
                    for g in range(2):
                        cols = slice(g * P, (g + 1) * P)
                        for k in range(KD):
                            ins = three(pe, [up_ps[s][:, g, h * 512:(h + 1) * 512] for h in range(2)],
                                        (up_hi[s][:, k, cols], up_lo[s][:, k, cols]),
                                        [(h2_hi[:, k, h * 512:(h + 1) * 512], h2_lo[:, k, h * 512:(h + 1) * 512]) for h in range(2)],
                                        k == 0)
                    ins.then_inc(late("up_mm")[0], 1)

            body(0, True)
            with pe.Fori(1, NF // 2) as i:
                body(i, False)

        def down_load(sp, n, k, s):
            sp.dma_start(dn_st[s], a["ffn_w_down"][0].rearrange("(k p) n -> p k n", p=P)[:, bass.ds(k, 1), n * 512:(n + 1) * 512]
                         .rearrange("p k n -> p (k n)")).then_inc(late(f"dn_st{s}")[0], 16)

        def down_loads(sp):
            sp.dma_start(gpost_ffn, a["norm_ffn_post"][0].partition_broadcast(P)).then_inc(sem("gpost2_in"), 16)
            for s in range(2):
                down_load(sp, 0, s, s)
            with sp.Fori(1, NF // 2) as i:
                for s in range(2):
                    sp.wait_ge(*late("dn_lo", 2 * i + s - 1))
                    down_load(sp, 0, 2 * i + s, s)
            with sp.Fori(0, NF // 2) as i:
                for s in range(2):
                    sp.wait_ge(*late("dn_lo", 2 * i + s - 1 + NF))
                    down_load(sp, 1, 2 * i + s, s)
            for s in range(2):
                sp.wait_ge(sem(f"x1_st{s}"), 16 * NT // 2)
            for t in range(NT):
                if t >= 2:
                    sp.wait_ge(*late("fin", t - 1))
                sp.dma_start(x1r[t % 2], scratch[t * P:(t + 1) * P, :]).then_inc(late(f"x1r{t % 2}")[0], 16)
                if t >= 1:
                    store(sp, t - 1)
            store(sp, NT - 1)
            sp.wait_ge(sem("stored"), 16 * NT)

        def store(sp, t):
            sp.wait_ge(*late("fin", t + 1))
            sp.dma_start(out[0, t * P:(t + 1) * P, :], y_dn[:, t]).then_inc(sem("stored"), 16)

        def down_act(act):
            for n in range(2):
                def body(i, first):
                    for s in range(2):
                        act.wait_ge(*late(f"dn_st{s}", 16 * i + 16 + 8 * NF * n))
                        if not first:
                            act.wait_ge(*late("dn_mm", 2 * i + s - 1 + (NF - 1) * n))
                        elif n and s == 0:
                            act.wait_ge(*late("dn_mm", NF - 1))
                        elif n:
                            act.wait_ge(*late("dn_t", NT))
                        act.activation(dn_hi[s], dn_st[s], ACT.Copy).then_inc(late("dn_hi")[0], 1)
                body(0, True)
                with act.Fori(1, NF // 2) as i:
                    body(i, False)
            act.preload_act_table_set("natural_log_exp_and_others")
            for t in range(NT):
                act.wait_ge(*late("y_out", NT + t + 1))
                act.activation(junk2, y_dn[:, t], ACT.Square, accum_out=wss[:, t:t + 1]).then_inc(late("f_sq")[0], 1)
                act.wait_ge(*late("f_sq", t + 1))
                act.activation(wrs[:, t:t + 1], wss[:, t:t + 1], ACT.Ln, bias=eps_c, scale=1.0 / D).then_inc(late("f_ln")[0], 1)
                act.wait_ge(*late("f_ln", t + 1))
                act.activation(wrs[:, t:t + 1], wrs[:, t:t + 1], ACT.Exp, scale=-0.5).then_inc(late("f_rs")[0], 1)

        def down_pool(pool):
            with pool.Fori(0, NF) as i:
                for s in range(2):
                    pool.wait_ge(*late("dn_hi", 2 * i + s + 1))
                    pool.tensor_tensor(dn_lo[s], dn_st[s], dn_hi[s], ALU.subtract).then_inc(late("dn_lo")[0], 1)
            for t in range(NT):
                pool.wait_ge(*late("f_y", t + 1))
                pool.wait_ge(*late(f"x1r{t % 2}", 16 * (t // 2 + 1)))
                pool.tensor_tensor(y_dn[:, t], y_dn[:, t], x1r[t % 2], ALU.add).then_inc(late("fin")[0], 1)

        def down_dve(v):
            for n in range(2):
                for t in range(NT):
                    v.wait_ge(*late("dn_t", NT * n + t + 1))
                    v.tensor_copy(y_dn[:, t, n * 512:(n + 1) * 512], psum[:, t, :]).then_inc(late("y_out")[0], 1)
            v.wait_ge(sem("gpost2_in"), 16)
            for t in range(NT):
                v.wait_ge(*late("f_rs", t + 1))
                v.scalar_tensor_tensor(out=y_dn[:, t], in0=y_dn[:, t], scalar=wrs[:, t:t + 1], in1=gpost_ffn,
                                       op0=ALU.mult, op1=ALU.mult).then_inc(late("f_y")[0], 1)

        def down_pe(pe):
            pe.wait_ge(*late("a_lo", NF))
            pe.wait_ge(*late("up_conv", 2 * NF))
            for n in range(2):
                def step(k, s, count, place):
                    pe.wait_ge(*late("dn_lo", count))
                    for t in range(NT):
                        tok = slice(t * P, (t + 1) * P)
                        if place == "first" and n:
                            pe.wait_ge(*late("y_out", t + 1))
                        ins = three(pe, [psum[:, t, :]], (act_hi[:, bass.ds(k, 1), tok].rearrange('p o c -> p (o c)'), act_lo[:, bass.ds(k, 1), tok].rearrange('p o c -> p (o c)')), [(dn_hi[s], dn_lo[s])], place == "first")
                        if place == "last":
                            ins.then_inc(late("dn_t")[0], 1)
                    if place != "last":
                        ins.then_inc(late("dn_mm")[0], 1)
                step(0, 0, NF * n + 1, "first")
                step(1, 1, NF * n + 2, "")
                with pe.Fori(1, NF // 2 - 1) as i:
                    for s in range(2):
                        step(2 * i + s, s, 2 * i + s + 1 + NF * n, "")
                step(NF - 2, 0, NF * n + NF - 1, "")
                step(NF - 1, 1, NF * n + NF, "last")

        def h_hi(act, t):
            act.wait_ge(sem("h_gained"), t + 1)
            act.activation(hT_hi[:, :, t * P:(t + 1) * P], x_hg[t % 2], ACT.Copy).then_inc(sem("h_hi"), 1)

        def silu(act, c):
            act.wait_ge(sem("conv_done"), c + 1)
            act.activation(qkvT[:, c], qkvT[:, c], ACT.Silu).then_inc(sem("qkv_ready"), 1)

        def kt_copy(act, t):
            act.wait_ge(sem("kT_done"), t + 1)
            act.activation(kT2[:, :, t * P:(t + 1) * P],
                           tp_ps[t % 2][:, 0:256].rearrange("p (w c) -> p w c", w=2), ACT.Copy).then_inc(sem("kT_out"), 1)

        def h_gain(v, t):
            v.wait_ge(sem("h_tp"), t + 1)
            if t >= 2:
                v.wait_ge(sem("h_lo"), t - 1)
            ps = cm_ps[t % 2].rearrange("p (k c) -> p k c", k=KD)
            v.tensor_tensor(x_hg[t % 2], ps, bc(pcol[:, PC_GMIX:PC_GMIX + KD], 2, P), ALU.mult).then_inc(sem("h_gained"), 1)

        def kt_transpose(pe, t):
            pe.wait_ge(sem("rot"), 2 * t + 2)
            if t >= 2:
                pe.wait_ge(sem("kT_out"), t - 1)
            else:
                pe.wait_ge(sem("pcol_ready"), 3)
            for w in range(2):
                ins = pe.transpose(tp_ps[t % 2][:, w * P:(w + 1) * P], kr[t % 2][:, w], ident)
            ins.then_inc(sem("kT_done"), 1)


        @block.sync
        def _(sp):
            for t in range(4):
                sp.dma_start(x_in[t], x_d[0, t * P:(t + 1) * P, :]).then_inc(sem(f"x_in{t}"), 16)
            sp.wait_ge(sem("prow_zeroed"), 1)
            rows = [(PC_GMIX, a["norm_mix_pre"][0], 8), (PC_GFFN, a["norm_ffn_pre"][0], 8)]
            for at_, v, n in rows:
                sp.dma_start(prow[at_:at_ + n, 0, :], v.rearrange("(c p) -> c p", p=P)).then_inc(sem("prow_in"), 16)
            for at_, v, n in ((PC_GCONV, a["gdn_conv_w"], 36), (PC_CCW, a["cc_dw_w"], 62)):
                sp.dma_start(prow[at_:at_ + n, 0, :], v[0].rearrange("l (c p) -> (l c) p", p=P)).then_inc(sem("prow_in"), 16)
            for at_, v in ((PC_CCB, a["cc_dw_b"]), (PC_LNG, a["cc_ln_g"]), (PC_LNB, a["cc_ln_b"])):
                sp.dma_start(prow[at_:at_ + 2, 0, :], v[0].rearrange("(c p) -> c p", p=P)).then_inc(sem("prow_in"), 16)
            fc = a["ffn_conv_w"][0].rearrange("l (c p) -> (l c) p", p=P)
            sp.dma_start(prow[:, 1, :], fc[0:P, :]).then_inc(sem("prow_in"), 16)
            sp.dma_start(prow[0:4, 2, :], fc[P:P + 4, :]).then_inc(sem("prow_in"), 16)
            for half in range(2):
                c = slice(HD * half, HD * half + HD)
                sp.dma_start(prow[PC_GNG:PC_GNG + 1, 0, c], a["gdn_norm_g"]).then_inc(sem("prow_in"), 16)
                sp.dma_start(prow[4:4 + CLEN, 2, c], a["nsa_cmp_pe_k"][0]).then_inc(sem("prow_in"), 16)
                sp.dma_start(prow[36:36 + CLEN, 2, c], a["nsa_cmp_pe_v"][0]).then_inc(sem("prow_in"), 16)
            sp.wait_ge(sem("pos_zeroed"), 1)
            sp.dma_start(pos_i[:, 0:NT], a["positions"][0].rearrange("(t p) -> p t", p=P),
                         allow_slow_non_contiguous=True).then_inc(sem("pos_in"), 16)
            sp.dma_start(pos_i[0:NCMP, NT:NT + 1],
                         a["positions"][0, CLEN - 1:S].rearrange("(n o) -> n o", o=1)[0:(NCMP - 1) * STRIDE + 1:STRIDE, :],
                         allow_slow_non_contiguous=True
                         ).then_inc(sem("pos_in"), 16)
            sp.dma_start(inv_t, a["inv"][0].partition_broadcast(P)).then_inc(sem("pos_in"), 16)
            for t in range(4, NT):
                sp.wait_ge(sem("h_scaled"), t - 3)
                sp.dma_start(x_in[t % 4], x_d[0, t * P:(t + 1) * P, :]).then_inc(sem(f"x_in{t % 4}"), 16)

            wv = w_in[0].rearrange("(c k p) n -> c p k n", k=2, p=P)
            for b, (col, n) in enumerate(BLOCKS):
                for c in range(4):
                    if b:
                        sp.wait_ge(sem("w_lo"), 4 * (b - 1) + c + 1)
                    if (col, n) == TM_BLOCKS[2]:
                        sp.dma_start(wst[c][:, :, 0:384], wv[c][:, :, col:col + 384]).then_inc(sem(f"w_st{c}"), 16)
                        sp.dma_start(wst[c][:, :, 384:402], wv[c][:, :, C_NG:C_NG + 18]).then_inc(sem("w_gate"), 16)
                    elif (col, n) == TM_BLOCKS[1]:
                        sp.dma_start(wst[c][:, :, 0:n], wv[c][:, :, col:col + n]).then_inc(sem(f"w_st{c}"), 16)
                    else:
                        sp.dma_start(wst[c][:, :, 0:n], wv[c][:, :, col:col + n]).then_inc(sem(f"w_st{c}"), 16)
            mixer_loads(sp)
            wout_loads(sp)
            up_loads(sp)
            down_loads(sp)

        @block.gpsimd
        def _(pool):
            own = Count(sem("pool_own"))
            pool.memset(prow, 0.0).then_inc(sem("prow_zeroed"), 1)
            pool.memset(pos_i, 0).then_inc(sem("pos_zeroed"), 1)
            own.up(pool.memset(eps_c, EPS))
            own.up(pool.memset(ident, 0.0))
            own.up(pool.memset(identb, 0.0))
            own.settle(pool)
            for m in (ident, identb):
                pool.affine_select(out=m, in_=m, compare_op=ALU.not_equal, fill=1.0, base=0,
                                   pattern=[[-1, P]], channel_multiplier=1).then_inc(sem("ident_ready"), 1)
            for t in range(NT):
                pool.wait_ge(sem("h_hi"), t + 1)
                pool.tensor_tensor(hT_lo[:, :, t * P:(t + 1) * P], x_hg[t % 2], hT_hi[:, :, t * P:(t + 1) * P],
                                   ALU.subtract).then_inc(sem("h_lo"), 1)
            def split_lo(b):
                n = BLOCKS[b][1]
                for c in range(4):
                    pool.wait_ge(sem("w_hi"), 4 * b + c + 1)
                    pool.tensor_tensor(wb_lo[b % 2][:, 2 * c:2 * c + 2, 0:n], wst[c][:, :, 0:n],
                                       wb_hi[b % 2][:, 2 * c:2 * c + 2, 0:n], ALU.subtract).then_inc(sem("w_lo"), 1)

            split_lo(0)
            split_lo(1)
            for b in range(len(BLOCKS)):
                if b == NCM + 1:
                    for t in range(NT):
                        s = t % 2
                        pool.wait_ge(sem("rot_mul"), t + 1)
                        if t >= 2:
                            pool.wait_ge(sem("kT_done"), t - 1)
                        vc = tmc[s][:, 0:256].rearrange("p (w h e d) -> p w h e d", w=2, h=2, e=2)
                        vs = tms[s][:, 0:256].rearrange("p (w h e d) -> p w h e d", w=2, h=2, e=2)
                        o = kr[s].rearrange("p w (h e d) -> p w h e d", h=2, e=2)
                        pool.tensor_tensor(o[:, :, :, 0, :], vc[:, :, :, 0, :], vs[:, :, :, 1, :], ALU.subtract).then_inc(sem("rot"), 1)
                        pool.tensor_tensor(o[:, :, :, 1, :], vs[:, :, :, 0, :], vc[:, :, :, 1, :], ALU.add).then_inc(sem("rot"), 1)
                if b == NCM + 2:
                    for t in range(NT):
                        s = t % 2
                        pool.wait_ge(sem("rot_mul"), NT + t + 1)
                        vc = tmc[s].rearrange("p (k g e d) -> p k g e d", k=KV, g=GRP, e=2)
                        vs = tms[s].rearrange("p (k g e d) -> p k g e d", k=KV, g=GRP, e=2)
                        o = qr[:, t].rearrange("p g k (e d) -> p k g e d", e=2)
                        pool.tensor_tensor(o[:, :, :, 0, :], vc[:, :, :, 0, :], vs[:, :, :, 1, :], ALU.subtract).then_inc(sem("rot"), 1)
                        pool.tensor_tensor(o[:, :, :, 1, :], vs[:, :, :, 0, :], vc[:, :, :, 1, :], ALU.add).then_inc(sem("rot"), 1)
                if b + 2 < len(BLOCKS):
                    split_lo(b + 2)
            mixer_pool(pool)
            wout_pool(pool)
            up_pool(pool)
            down_pool(pool)

        @block.scalar
        def _(act):
            act.wait_ge(sem("pool_own"), 3)
            for t in range(NT):
                act.wait_ge(sem(f"x_in{t % 4}"), 16 * (t // 4 + 1))
                act.activation(psum[:, 4:6, :].rearrange("p a b -> p (a b)"), x_in[t % 4], ACT.Square,
                               accum_out=ssq[:, t:t + 1]).then_inc(sem("ssq"), 1)
                act.wait_ge(sem("ssq"), t + 1)
                act.activation(rms[:, t:t + 1], ssq[:, t:t + 1], ACT.Sqrt, bias=eps_c, scale=1.0 / D).then_inc(sem("rms"), 1)
                if t >= 1:
                    h_hi(act, t - 1)
            h_hi(act, NT - 1)

            def split_hi(b):
                n = BLOCKS[b][1]
                if b >= 2:
                    if b - 2 < NCM:
                        act.wait_ge(sem("cm_done"), CM_AFTER[b - 2])
                    else:
                        act.wait_ge(sem("tm_done"), NT * (b - 1 - NCM))
                for c in range(4):
                    act.wait_ge(sem(f"w_st{c}"), 16 * (b + 1))
                    if b == NCM + 2:
                        act.wait_ge(sem("w_gate"), 64)
                    act.activation(wb_hi[b % 2][:, 2 * c:2 * c + 2, 0:n], wst[c][:, :, 0:n], ACT.Copy).then_inc(sem("w_hi"), 1)

            split_hi(0)
            split_hi(1)
            act.wait_ge(sem("rope_arg"), 1)
            act.activation(sin_t, ang, ACT.Sin).then_inc(sem("rope_tab"), 1)
            act.wait_ge(sem("rope_arg"), 2)
            act.activation(cos_t, turns, ACT.Sin).then_inc(sem("rope_tab"), 1)
            i = 0
            for b in range(NCM):
                for _, j in [x for x in CM_ORDER if x[0] == b]:
                    ps = cm_ps[i % 2]
                    act.wait_ge(sem("cm_done"), i + 1)
                    if b == 0:
                        if j < 2:
                            act.activation(cacc[:, j], ps, ACT.Copy).then_inc(sem("cu_out"), 1)
                        else:
                            act.wait_ge(sem("pcol_ready"), 3)
                            act.wait_ge(sem("rope_tab"), 2)
                            act.activation(glu[:, j - 2], ps, ACT.Tanh, scale=0.5).then_inc(sem("cu_out"), 1)
                    elif b <= 3:
                        c = 3 * (b - 1) + j
                        act.wait_ge(sem("pcol_ready"), 3)
                        act.activation(qkvT[:, c], ps, ACT.Copy,
                                       scale=pcol[:, PC_GCONV + 27 + c:PC_GCONV + 28 + c]).then_inc(sem("tap0"), 1)
                        if c >= 1:
                            silu(act, c - 1)
                    i += 1
                if b + 2 < len(BLOCKS):
                    split_hi(b + 2)
            silu(act, 8)
            for b in range(3):
                for t in range(NT):
                    n = b * NT + t
                    act.wait_ge(sem("tm_done"), n + 1)
                    ps = tm_ps[n % 2]
                    if b == 0:
                        act.activation(zab[:, t, 0:GDIM], ps[:, 0:GDIM], ACT.Silu).then_inc(sem("z_out"), 1)
                        act.activation(zab[:, t, GDIM:], ps[:, GDIM:GDIM + 2 * GH], ACT.Copy).then_inc(sem("tm_act"), 1)
                    elif b == 1:
                        act.activation(vsw[:, t], ps.rearrange("p (w c) -> p w c", w=4)[:, 1:4:2, :], ACT.Copy).then_inc(sem("tm_act"), 1)
                        if t >= 1:
                            kt_copy(act, t - 1)
                    else:
                        act.activation(gate[:, t], ps[:, 384:402], ACT.Copy).then_inc(sem("tm_act"), 1)
                if b == 1:
                    kt_copy(act, NT - 1)
                if NCM + b + 2 < len(BLOCKS):
                    split_hi(NCM + b + 2)
            conf_act(act)
            mixer_act(act)
            wout_act(act)
            up_act(act)
            down_act(act)

        @block.vector
        def _(v):
            own = Count(sem("dve_own"))

            def rope_tables():
                v.wait_ge(sem("pos_in"), 48)
                own.up(v.tensor_copy(pos_f, pos_i))
                own.settle(v)
                own.up(v.tensor_tensor(ang, bc(pos_f, 2, HD // 2), bc(inv_t, 1, NT + 1), ALU.mult))
                own.settle(v)
                magic = 12582912.0
                own.up(v.tensor_scalar(turns, ang, 1.0 / (2 * math.pi), magic, ALU.mult, ALU.add))
                own.settle(v)
                own.up(v.tensor_scalar(turns, turns, -magic, None, ALU.add))
                own.settle(v)
                c1 = 6.28125
                c2 = float(np.float32(round((2 * math.pi - c1) * 2 ** 20) / 2 ** 20))
                c3 = 2 * math.pi - c1 - c2
                for c in (c1, c2, c3):
                    own.up(v.scalar_tensor_tensor(out=ang, in0=turns, scalar=-c, in1=ang, op0=ALU.mult, op1=ALU.add))
                    own.settle(v)
                edge = 3.1415925
                v.tensor_scalar(ang, ang, edge, -edge, ALU.min, ALU.max).then_inc(sem("rope_arg"), 1)
                v.wait_ge(sem("rope_arg"), 1)
                own.up(v.scalar_tensor_tensor(out=turns, in0=ang, scalar=-1.0, in1=ang, op0=ALU.mult, op1=ALU.max))
                own.settle(v)
                v.tensor_scalar(turns, turns, -1.0, math.pi / 2, ALU.mult, ALU.add).then_inc(sem("rope_arg"), 1)

            for t in range(NT):
                v.wait_ge(sem("rms"), t + 1)
                own.up(v.reciprocal(rstd[:, t:t + 1], rms[:, t:t + 1]))
                own.settle(v)
                if t >= 2:
                    v.wait_ge(sem("h_tp"), t - 1)
                v.tensor_scalar(x_hn[t % 2], x_in[t % 4], rstd[:, t:t + 1], None, ALU.mult).then_inc(sem("h_scaled"), 1)
                if t == 0:
                    v.wait_ge(sem("pcol_tp"), 3)
                    for j in range(3):
                        v.tensor_copy(pcol[:, j * P:(j + 1) * P], psum[:, 6, j * P:(j + 1) * P]).then_inc(sem("pcol_ready"), 1)
                    v.wait_ge(sem("pcol_ready"), 3)
                    own.up(v.tensor_scalar(pcol[:, PC_CCW:PC_CCW + 62], pcol[:, PC_CCW:PC_CCW + 62], 0.5, None, ALU.mult))
                if t >= 1:
                    h_gain(v, t - 1)
            h_gain(v, NT - 1)
            rope_tables()

            i = 0
            conv_at = [0]

            def cc_taps(c, s0, s1):
                for s in range(s0, s1):
                    col = PC_CCW + 2 * (CW - 1 - s) + c
                    w = pcol[:, col:col + 1]
                    if s == 0:
                        own.up(v.tensor_scalar(cacc[:, c], glu[:, c], w, pcol[:, PC_CCB + c:PC_CCB + c + 1], ALU.mult, ALU.add))
                    else:
                        own.settle(v)
                        own.up(v.scalar_tensor_tensor(out=cacc[:, c, s:S], in0=glu[:, c, 0:S - s], scalar=w,
                                                      in1=cacc[:, c, s:S], op0=ALU.mult, op1=ALU.add))

            cc_plan = [(c, s0, min(s0 + 5, CW)) for c in range(2) for s0 in range(0, CW, 5)]
            for b in range(NCM):
                for _, j in [x for x in CM_ORDER if x[0] == b]:
                    ps = cm_ps[i % 2]
                    if b == 0 and j >= 2:
                        v.wait_ge(sem("cu_out"), i + 1)
                        own.up(v.scalar_tensor_tensor(out=glu[:, j - 2], in0=glu[:, j - 2], scalar=1.0, in1=cacc[:, j - 2],
                                                      op0=ALU.add, op1=ALU.mult))
                        own.settle(v)
                    elif 1 <= b <= 3:
                        c = 3 * (b - 1) + j
                        v.wait_ge(sem("tap0"), c + 1)
                        for s in range(1, 4):
                            col = PC_GCONV + 9 * (3 - s) + c
                            ins = v.scalar_tensor_tensor(out=qkvT[:, c, s:S], in0=ps[:, 0:S - s], scalar=pcol[:, col:col + 1],
                                                         in1=qkvT[:, c, s:S], op0=ALU.mult, op1=ALU.add)
                            if s < 3:
                                own.up(ins)
                                own.settle(v)
                            else:
                                ins.then_inc(sem("conv_done"), 1)
                    elif b == 4:
                        v.wait_ge(sem("cm_done"), i + 1)
                        dst = (kcat, vcat)[j]
                        pe0 = (PC_PEK, PC_PEV)[j]
                        for half in range(2):
                            pe_ = pcol[:, pe0 + STRIDE * half:pe0 + STRIDE * half + STRIDE]
                            v.tensor_tensor(dst[:, half].rearrange("p (n l) -> p n l", l=STRIDE),
                                            ps.rearrange("p (n l) -> p n l", l=STRIDE), bc(pe_, 1, S // STRIDE),
                                            ALU.add).then_inc(sem("cat_out"), 1)
                    if b >= 1 and cc_plan:
                        cc_taps(*cc_plan.pop(0))
                    i += 1
            while cc_plan:
                cc_taps(*cc_plan.pop(0))
            own.settle(v)
            v.tensor_copy(gng, pcol[:, PC_GNG:PC_GNG + 1]).then_inc(sem("cc_conv"), 1)
            for b in (1, 2):
                for t in range(NT):
                    n = b * NT + t
                    ps = tm_ps[n % 2]
                    v.wait_ge(sem("tm_act"), n + 1)
                    if t == 0:
                        v.wait_ge(sem("rope_tab"), 2)
                    s = t % 2
                    if n >= NT + 2:
                        v.wait_ge(sem("rot"), 2 * (n - NT - 1))
                    for tab, dst in ((cos_t, tmc), (sin_t, tms)):
                        if b == 1:
                            ins = v.tensor_tensor(dst[s][:, 0:256].rearrange("p (w c d) -> p w c d", w=2, d=32),
                                                  ps.rearrange("p (w c d) -> p w c d", w=4, d=32)[:, 0:4:2],
                                                  bc(bc(tab[:, t], 1, 4), 1, 2), ALU.mult)
                        else:
                            ins = v.scalar_tensor_tensor(out=dst[s].rearrange("p (c d) -> p c d", d=32),
                                                         in0=ps[:, 0:384].rearrange("p (c d) -> p c d", d=32),
                                                         scalar=HD ** -0.5, in1=bc(tab[:, t], 1, 12), op0=ALU.mult, op1=ALU.mult)
                        if tab is cos_t:
                            own.up(ins)
                    ins.then_inc(sem("rot_mul"), 1)
                    if b == 2:
                        conf_stats(v, t)
            own.settle(v)
            conf_dve(v)
            mixer_dve(v)
            wout_dve(v)
            up_dve(v)
            down_dve(v)

        @block.tensor
        def _(pe):
            pe.wait_ge(sem("ident_ready"), 2)
            for t in range(NT):
                if t == 1:
                    pe.wait_ge(sem("prow_in"), 16 * 15)
                    for j in range(3):
                        pe.transpose(psum[:, 6, j * P:(j + 1) * P], prow[:, j, :], ident).then_inc(sem("pcol_tp"), 1)
                pe.wait_ge(sem("h_scaled"), t + 1)
                if t >= 2:
                    pe.wait_ge(sem("h_gained"), t - 1)
                for k in range(KD):
                    ins = pe.transpose(cm_ps[t % 2][:, k * P:(k + 1) * P], x_hn[t % 2][:, k * P:(k + 1) * P], ident)
                ins.then_inc(sem("h_tp"), 1)

            def three(outs, lhs, rhs, first, last):
                for o, (r_hi, r_lo) in zip(outs, rhs):
                    pe.matmul(o, lhs[0], r_hi, start=first, stop=False)
                for o, (r_hi, r_lo) in zip(outs, rhs):
                    pe.matmul(o, lhs[0], r_lo, start=False, stop=False)
                for o, (r_hi, r_lo) in zip(outs, rhs):
                    ins = pe.matmul(o, lhs[1], r_hi, start=False, stop=last)
                return ins

            i = 0
            for b in range(NCM):
                pe.wait_ge(sem("w_lo"), 4 * b + 4)
                for _, j in [x for x in CM_ORDER if x[0] == b]:
                    if i < 2:
                        pe.wait_ge(sem("h_lo"), NT)
                    if i >= 2:
                        q = i - 2
                        if q < 4:
                            pe.wait_ge(sem("cu_out"), q + 1)
                        elif q < 13:
                            pe.wait_ge(sem("conv_done"), q - 3)
                        else:
                            pe.wait_ge(sem("cat_out"), 2 * (q - 12))
                    ps = cm_ps[i % 2]
                    cols = slice(j * P, (j + 1) * P)
                    for k in range(KD):
                        ins = three([ps[:, 0:512], ps[:, 512:1024]],
                                    (wb_hi[b % 2][:, k, cols], wb_lo[b % 2][:, k, cols]),
                                    [(hT_hi[:, k, h * 512:(h + 1) * 512], hT_lo[:, k, h * 512:(h + 1) * 512]) for h in range(2)],
                                    k == 0, k == KD - 1)
                    ins.then_inc(sem("cm_done"), 1)
                    i += 1
            for b in range(3):
                B = NCM + b
                n_cols = BLOCKS[B][1]
                pe.wait_ge(sem("w_lo"), 4 * B + 4)
                for t in range(NT):
                    n = b * NT + t
                    if n >= 2:
                        q = n - 2
                        if q < NT:
                            pe.wait_ge(sem("tm_act"), q + 1)
                        else:
                            pe.wait_ge(sem("rot_mul"), q - NT + 1)
                    ps = tm_ps[n % 2][:, 0:n_cols]
                    tok = slice(t * P, (t + 1) * P)
                    for k in range(KD):
                        ins = three([ps], (hT_hi[:, k, tok], hT_lo[:, k, tok]),
                                    [(wb_hi[B % 2][:, k, 0:n_cols], wb_lo[B % 2][:, k, 0:n_cols])], k == 0, k == KD - 1)
                    ins.then_inc(sem("tm_done"), 1)
                    if b == 1 and t >= 1:
                        kt_transpose(pe, t - 1)
                    if b == 2:
                        conf_transpose(pe, t)
                if b == 1:
                    kt_transpose(pe, NT - 1)
            conf_back(pe)
            mixer_pe(pe)
            wout_pe(pe)
            up_pe(pe)
            down_pe(pe)


INPUTS = ["x", "positions", "norm_mix_pre", "norm_mix_post", "norm_ffn_pre", "norm_ffn_post", "w_in", "w_out",
          "gdn_conv_w", "gdn_a_log", "gdn_dt_bias", "gdn_norm_g", "nsa_cmp_wk", "nsa_cmp_wv", "nsa_cmp_pe_k",
          "nsa_cmp_pe_v", "cc_dw_w", "cc_dw_b", "cc_ln_g", "cc_ln_b", "ffn_w_up", "ffn_conv_w", "ffn_w_down"]


def kernel(**inputs):
    import concourse.bacc as bacc
    from concourse.bass_utils import run_bass_kernel_spmd

    nc = bacc.Bacc("TRN2", target_bir_lowering=False, num_devices=1)
    arrays, a = {}, {}
    for name in INPUTS:
        v = np.ascontiguousarray(inputs[name])
        arrays["in_" + name] = v
        a[name] = nc.dram_tensor("in_" + name, v.shape, mybir.dt.from_np(v.dtype), kind="ExternalInput").ap()
    inv = inv_freq().reshape(1, HD // 2)
    arrays["inv_freq"] = inv
    a["inv"] = nc.dram_tensor("inv_freq", inv.shape, F32, kind="ExternalInput").ap()
    out = nc.dram_tensor("out_0", (1, S, D), F32, kind="ExternalOutput").ap()
    scratch = nc.dram_tensor("x_mid", (S, D), F32, kind="Internal").ap()
    build(nc, a, out, scratch)
    r = run_bass_kernel_spmd(nc, [arrays], core_ids=[0])
    return r.results[0]["out_0"]
```

```python
import math
from contextlib import ExitStack

import numpy as np

import concourse.bass as bass
from concourse import mybir

F32 = mybir.dt.float32
BF16 = mybir.dt.bfloat16
I32 = mybir.dt.int32
ACT = mybir.ActivationFunctionType
ALU = mybir.AluOpType
AX = mybir.AxisListType

P = 128
S = 1024
D = 1024
NT = S // P
KD = D // P
HD = 64
GH = 6
GDIM = GH * HD
CH = 64
NH = 6
KV = 2
GRP = NH // KV
STRIDE = 16
CLEN = 32
NCMP = S // STRIDE - 1
SLC = 64
NSLC = S // SLC
TOPK = 8
WINDOW = 512
CCH = 256
CW = 31
DFF = 2816
NF = DFF // P
EPS = 1e-6
FORCE = 1e4
NEG = -1e30
THETA = 10000.0

_W = (GDIM, GDIM, GDIM, GDIM, GH, GH, NH * HD, 128, 128, 128, 128, 128, 128, 3 * NH, 2 * CCH)
_O = [sum(_W[:i]) for i in range(len(_W) + 1)]
(C_GQ, C_GK, C_GV, C_GZ, C_GA, C_GB, C_NQ, C_NKC, C_NVC, C_NKS, C_NVS, C_NKW, C_NVW, C_NG, C_CU, IN_DIM) = _O

CM_BLOCKS = [(C_CU, 512), (C_GQ, 384), (C_GK, 384), (C_GV, 384), (C_NKC, 256)]
TM_BLOCKS = [(C_GZ, GDIM + 2 * GH), (C_NKS, 512), (C_NQ, NH * HD + 3 * NH)]
CM_TILES = [(b, j) for b, (_, n) in enumerate(CM_BLOCKS) for j in range(n // P)]


class Regions:

    def __init__(self, arena):
        self.arena = arena

    def view(self, at, shape, dtype=F32):
        words = int(np.prod(shape)) // (2 if dtype == BF16 else 1)
        v = self.arena[:, at:at + words]
        if dtype != F32:
            v = v.bitcast(dtype)
        if len(shape) > 1:
            names = " ".join(f"d{i}" for i in range(len(shape)))
            v = v.rearrange(f"p ({names}) -> p {names}", **{f"d{i}": n for i, n in enumerate(shape)})
        return v


def bc(ap, dim, n):
    v = ap.unsqueeze(dim)
    shape = list(v.shape)
    shape[dim] = n
    return v.broadcast_to(shape)


class Count:

    def __init__(self, sem):
        self.sem, self.n = sem, 0

    def up(self, ins):
        ins.then_inc(self.sem, 1)
        self.n += 1
        return ins

    def settle(self, eng):
        eng.wait_ge(self.sem, self.n)


def inv_freq():
    return (1.0 / (np.float32(THETA) ** (np.arange(0, HD, 2, dtype=np.float32) / np.float32(HD)))).astype(np.float32)


PC_GMIX, PC_GFFN, PC_GCONV, PC_CCW, PC_CCB, PC_LNG, PC_LNB, PC_GNG = 0, 8, 16, 52, 114, 116, 118, 120
PC_FCONV, PC_PEK, PC_PEV = 128, 128 + 3 * 2 * NF, 128 + 3 * 2 * NF + CLEN

CM_ORDER = [(0, 0), (0, 2), (0, 1), (0, 3)] + CM_TILES[4:]
CM_AFTER = [1 + max(i for i, (b, _) in enumerate(CM_ORDER) if b == n) for n in range(len(CM_BLOCKS))]
BLOCKS = CM_BLOCKS + TM_BLOCKS
NCM = len(CM_BLOCKS)


def merge(*lists):
    tagged = [((i + 0.5) / len(l), n, s) for n, l in enumerate(lists) for i, s in enumerate(l)]
    return [s for _, _, s in sorted(tagged, key=lambda x: x[:2])]


CONST_PARTS = 8
LEVELS = 6


def gdn_prepare(t):
    steps = [("A1a", t), ("A1r", t), ("A1s", t), ("A1n", t), ("A1b", t), ("A2a", t), ("A2b", t), ("A3a", t), ("A3b", t)]
    for l in range(LEVELS):
        steps.append(("M", t, l))
        if 1 <= l < LEVELS - 1:
            steps.append(("X", t, l))
        steps.append(("XT", t, l))
    return steps + [("A4", t)]


def gdn_scan(t):
    return [("B1", t, 0), ("B2", t, 0), ("B1", t, 1), ("B2", t, 1), ("B3", t), ("C1", t), ("C1r", t), ("C1s", t), ("C1n", t), ("C2", t)]


def win_blocks(t):
    return max(0, t - WINDOW // P), t + 1


def key_blocks(t, kind):
    return (0, t + 1) if kind == 0 else win_blocks(t)


def batches(t, kind):
    k0, k1 = key_blocks(t, kind)
    n = -(-(k1 - k0) // 4)
    cut = [k0 + (k1 - k0) * i // n for i in range(n + 1)]
    return list(zip(cut, cut[1:]))


GAP = "gap"
RANK_PARTS = 4


def nsa():
    heads = [(t, kind, h) for t in range(NT) for kind in (1, 0) for h in range(NH)]
    steps = [("Nq", 0), GAP, ("Nc1", 0), GAP, ("Ns", 0, 1, 0), ("Nx", 0, 1, 0), GAP, ("Nc1b", 0)]
    behind = []
    for i, (t, kind, h) in enumerate(heads):
        chosen = (t + 1) * P > TOPK * SLC
        last = kind == 0 and h == NH - 1
        if not last:
            steps.append(("Ns",) + heads[i + 1])
            if kind == 0 and h == NH - 2 and t + 1 < NT:
                steps.append(("Nq", t + 1))
        cuts = batches(t, kind)
        for n in range(len(cuts)):
            steps.append(("NT", t, kind, h, n))
            if n == 0 and not last:
                steps.append(("Nx",) + heads[i + 1])
            steps += [GAP] + behind + [GAP]
            behind = [("NV", t, kind, h, n)]
        if h == NH - 1:
            behind.append(("Ne", t, kind))
        if last and t + 1 < NT:
            steps += [("Nc1", t + 1), GAP] + behind + [("Ns",) + heads[i + 1], ("Nx",) + heads[i + 1], GAP, ("Nc1b", t + 1)]
            behind = []
        if kind == 1:
            if h == 0 and t:
                steps += [GAP, ("No", t - 1)]
            if chosen and h < 4:
                steps += [("Nr", t) + divmod(2 * h + e, RANK_PARTS) for e in range(2)]
            if chosen and h == 4:
                steps += [("Nidx", t), GAP]
            if h == NH - 1:
                steps += [("Nc2", t), GAP] + behind + [GAP]
                behind = [("Nc3", t)]
    return steps + behind + [GAP, ("No", NT - 1)]


def cost(step):
    if step[0] in ("NT", "NV"):
        b0, b1 = batches(step[1], step[2])[step[4]]
        return b1 - b0 + 1
    if step[0] == "Ns":
        k0, k1 = key_blocks(step[1], step[2])
        return k1 - k0 + 2
    return 3 if step[0] in ("Nq", "Nc1", "Nc2", "Nc3", "No") else 1 if step[0] == "Nidx" else 0


def fill_gaps(steps, fillers):
    total = sum(map(cost, steps))
    out, done, used = [], 0.0, 0
    for s in steps:
        if s == GAP:
            n = int(len(fillers) * done / total)
            out += fillers[used:n]
            used = n
        else:
            out.append(s)
            done += cost(s)
    return out + fillers[used:]


GDN = gdn_prepare(0)
for _t in range(NT):
    GDN += merge(gdn_scan(_t), gdn_prepare(_t + 1)) if _t + 1 < NT else gdn_scan(_t)
MIX = fill_gaps(nsa(), GDN)
_from = 1 + max(MIX.index(("A1b", NT - 1)), MIX.index(("Nq", NT - 1)))
for _c in reversed(range(KD)):
    MIX.insert(_from + 8 + (len(MIX) - _from - 8) * _c // KD, ("WO", _c))
HT = NT // 2


def uses(kinds, upto):
    return sum(1 for s in MIX[:upto] if s[0] in kinds)


LATE = {
    "wo_mm": ("cm_done", 15),
    "v_tp": ("h_tp", 8),
    "up_mm": ("tm_done", 24),
    "dn_mm": ("kT_done", 8),
    "dn_t": ("cc_tp", 8),
    "wo_hi": ("w_hi", 32),
    "w_sq": ("ssq", 8),
    "w_ln": ("rms", 8),
    "w_rs": ("tap0", 9),
    "v_sq": ("qkv_ready", 9),
    "v_ln": ("z_out", 8),
    "v_rs": ("kT_out", 8),
    "v_hi": ("h_hi", 8),
    "up_hi": ("w_hi", 40),
    "up_tap": ("tm_act", 24),
    "up_silu": ("cu_out", 4),
    "a_hi": ("rope_tab", 2),
    "f_sq": ("ssq", 16),
    "f_ln": ("rms", 16),
    "f_rs": ("tap0", 17),
    "dn_hi": ("w_hi", 62),
    "w_y": ("h_scaled", 8),
    "v_hn": ("h_gained", 8),
    "v_hg": ("conv_done", 9),
    "wcol": ("cat_out", 4),
    "up_c1": ("rot_mul", 16),
    "up_conv": ("cc_tok", 8),
    "f_y": ("cc_ag", 8),
    "wo_lo": ("w_lo", 32),
    "x1": ("h_lo", 8),
    "v_lo": ("rot", 32),
    "up_lo": ("w_lo", 40),
    "up_prod": ("ident_ready", 2),
    "a_lo": ("rot", 40),
    "dn_lo": ("w_lo", 62),
    "fin": ("h_lo", 16),
    "wo_st0": ("w_st0", 128),
    "wo_st1": ("w_st1", 128),
    "wo_st2": ("w_st2", 128),
    "wo_st3": ("w_st3", 128),
    "xr_in0": ("x_in0", 32),
    "xr_in1": ("x_in1", 32),
    "up_st0": ("x_in2", 32),
    "up_st1": ("x_in3", 32),
    "dn_st0": ("w_st0", 160),
    "dn_st1": ("w_st1", 160),
    "x1r0": ("w_st2", 160),
    "x1r1": ("w_st3", 160),
    "x1r2": ("x_in0", 96),
    "x1r3": ("x_in1", 96),
}


def build(nc, a, out, scratch):
    ctx = ExitStack()
    with ctx:
        sem_names = {}

        def sem(name):
            if name not in sem_names:
                sem_names[name] = ctx.enter_context(nc.semaphore(name))
            return sem_names[name]

        def late(name, value=0):
            early, base = LATE[name]
            return sem(early), base + value

        arena = ctx.enter_context(nc.sbuf_tensor("arena", [P, 53200], F32))
        R = Regions(arena)
        psum = ctx.enter_context(nc.psum_tensor("psum", [P, 8, 512], F32))

        hT_hi = R.view(0, [KD, S], BF16)
        hT_lo = R.view(4096, [KD, S], BF16)
        wst = [R.view(8192 + 1024 * c, [2, 512]) for c in range(4)]
        wb_hi = [R.view(12288 + 4096 * s, [KD, 512], BF16) for s in range(2)]
        wb_lo = [R.view(12288 + 4096 * s + 2048, [KD, 512], BF16) for s in range(2)]
        qkvT = R.view(20480, [9, S])
        x_in = [R.view(20480 + 1024 * s, [S]) for s in range(4)]
        x_hn = [R.view(24576 + 1024 * s, [S]) for s in range(2)]
        x_hg = [R.view(26624 + 1024 * s, [KD, P]) for s in range(2)]
        zab = R.view(29696, [NT, GDIM + 2 * GH])
        qr = R.view(32864, [NT, GRP, KV, HD])
        vsw = R.view(35936, [NT, 2, KV * HD])
        kT2 = R.view(37984, [2, S])
        kcat = R.view(40032, [2, S])
        vcat = R.view(42080, [2, S])
        glu = R.view(44128, [2, S])
        cacc = R.view(46176, [2, S])
        tmc = [R.view(48224 + 768 * s, [384]) for s in range(2)]
        tms = [R.view(48224 + 768 * s + 384, [384]) for s in range(2)]
        kr = [R.view(49760 + 256 * s, [2, P]) for s in range(2)]
        at = [50272]

        def small(shape, dtype=F32):
            words = int(np.prod(shape))
            if dtype == BF16:
                words = (words + 1) // 2
            v = R.view(at[0], shape, dtype)
            at[0] += words
            assert at[0] <= 53200
            return v

        ident = small([P])
        identb = small([P], BF16)
        prow = R.view(44128, [3, P])
        pcol = small([3 * P])
        eps_c = small([1])
        ssq = small([NT])
        rms = small([NT])
        rstd = small([NT])
        pos_i = small([NT + 1], I32)
        pos_f = small([NT + 1])
        cos_t = small([NT + 1, HD // 2])
        sin_t = small([NT + 1, HD // 2])
        ang = R.view(44512, [NT + 1, HD // 2])
        turns = R.view(44800, [NT + 1, HD // 2])
        inv_t = R.view(45088, [HD // 2])
        gate = small([NT, 3 * NH])
        lnst = small([NT, 6])
        lnag = small([NT, 2])
        lnr = small([NT])

        ones_c = small([1])
        gng = small([1])
        dtb = small([GH])
        alog = small([GH])
        maskD = small([CH], BF16)
        negI = small([CH], BF16)
        causal = small([P], BF16)
        far = small([P], BF16)
        EG = small([NT * GH])
        ED = small([NT * GH])
        EGL = small([NT, 2, 3])
        graw = small([NT * GH])
        beta = small([NT * GH])
        stat_a = small([NT * GH])
        stat_b = small([NT * GH])
        stat_c = small([NT, GH])
        Ic = small([CH])
        tri = small([NSLC, NSLC], BF16)
        forced = small([4, NSLC])
        scored = small([4, NSLC])
        kcT = small([CH])
        ss, rs = small([12]), small([12])
        ss2, rs2 = small([GH]), small([GH])
        cmx, csum = small([NH]), small([NH])
        nmx, psums, coef = small([2]), small([2 * NH]), small([NH])
        pg = small([CH + 1])
        imp, rank = small([NSLC]), small([NSLC])
        selb = small([KV, NSLC])
        selT = small([KV, P], BF16)
        wck = R.view(10240, [CLEN, P])
        wcv = R.view(14336, [CLEN, P])
        m1 = [8192]

        def mix1(shape, dtype=F32):
            w = int(np.prod(shape)) // (2 if dtype == BF16 else 1)
            v_ = R.view(m1[0], shape, dtype)
            m1[0] += w
            assert m1[0] <= 20480, m1
            return v_

        m2 = [40032]

        def mix2(shape, dtype=F32):
            w = int(np.prod(shape)) // (2 if dtype == BF16 else 1)
            v_ = R.view(m2[0], shape, dtype)
            m2[0] += w
            assert m2[0] <= 50272, m2
            return v_

        Umask = mix1([CH])
        SL = mix1([P])
        strict = mix1([CH])
        Ucum = mix1([P])
        half_ones = [mix1([P]) for _ in range(2)]
        blk_of = mix1([S], BF16)
        cmask = mix1([NT, CH], BF16)
        nm = mix1([LEVELS, CH])
        assert m1[0] <= 10240
        ctok = R.view(44128, [NT, CCH])
        cact = R.view(46176, [2, S])
        mix_hi = R.view(0, [KD, S], BF16)
        mix_lo = R.view(4096, [KD, S], BF16)
        qn, kn, kb, kbg, qg, vb = [mix1([GH, HD]) for _ in range(6)]
        kTn = mix1([3, P])
        kbT = mix1([3, P])
        qT = mix1([3, P])
        Drhs = mix1([GH, CH])
        DTc = mix1([GH, CH])
        DTs = mix1([GH, CH])
        LTc = mix1([GH, CH])
        sq = mix1([2 * GH, HD])
        Xc, Tc, MIc = Drhs, qg, kb
        Sbd = mix1([3, P])
        m1[0] = 14336 + CLEN * P
        vn = mix1([GH, HD])
        on = mix1([GH, HD])
        sq2 = mix1([GH, HD])
        mtmp = sq2.rearrange("p h d -> p (h d)").rearrange("p (h c) -> p h c", h=3)
        vcbd = mix1([3, P])
        kdec = [mix2([GH, HD]) for _ in range(2)]
        qgT = [mix2([3, P]) for _ in range(2)]
        uu = [mix2([GH, HD]) for _ in range(2)]
        nwT = [mix2([3, P]) for _ in range(2)]
        QTc = [mix2([GH, CH]) for _ in range(2)]
        qpad = mix2([KV, GRP, P])
        Pb = [mix2([S]) for _ in range(2)]
        PTs = [mix2([512]) for _ in range(2)]
        oacc = mix2([NH, HD])
        otmp = mix2([NH, HD])
        mtmp_n = otmp.rearrange("p h d -> p (h d)").rearrange("p (h c) -> p h c", h=3)
        csc = mix2([NH, CH])
        cmpg = mix2([NSLC, NSLC])
        cmpe = mix2([NSLC, NSLC])

        wo_hi = R.view(20480, [KD, D], BF16)
        wo_lo = R.view(24576, [KD, D], BF16)
        wo_st = [R.view(w, [D]) for w in (28672, 32864, 33888, 34912)]
        xr = [R.view(8192 + 1024 * c, [D]) for c in range(2)]
        x1 = [R.view(10240 + 1024 * c, [D]) for c in range(2)]
        hn2 = [R.view(12288 + 1024 * c, [D]) for c in range(2)]
        hg2 = [R.view(14336 + 1024 * c, [KD, P]) for c in range(2)]
        gpost_mix = R.view(16384, [D])
        h2_hi, h2_lo = hT_hi, hT_lo
        wss, wrs = stat_a[:, 0:2 * NT], stat_b[:, 0:2 * NT]
        act_hi = R.view(8192, [NF, S], BF16)
        act_lo = R.view(8192 + NF * 512, [NF, S], BF16)
        up_st = [R.view(30720 + 2048 * c, [KD, 2 * P]) for c in range(2)]
        up_hi = [R.view(34816 + 1024 * c, [KD, 2 * P], BF16) for c in range(2)]
        up_lo = [R.view(36864 + 1024 * c, [KD, 2 * P], BF16) for c in range(2)]
        y_up = [R.view(38912 + 2048 * c, [2, S]) for c in range(2)]
        prod = [R.view(43008 + 1024 * c, [S]) for c in range(2)]
        wcol = [stat_c.rearrange("p a b -> p (a b)")[:, 6 * c:6 * c + 6] for c in range(2)]
        dn_st = [R.view(45056 + 1024 * c, [D]) for c in range(2)]
        dn_hi = [R.view(47104 + 512 * c, [D], BF16) for c in range(2)]
        dn_lo = [R.view(48128 + 512 * c, [D], BF16) for c in range(2)]
        gpost_ffn = R.view(49152, [D])
        x1r = [R.view(30720 + 1024 * c, [D]) for c in range(HT)]
        y_dn = R.view(0, [NT, D])
        junk2 = R.view(34816, [D])
        junk = R.view(29696, [D])
        dn_ps = [psum[:, 2 * c:2 * c + 2, :].rearrange("p a b -> p (a b)") for c in range(HT)]
        tq_ps = [psum[:, 4 + 2 * c:6 + 2 * c, :].rearrange("p a b -> p (a b)") for c in range(2)]
        up_ps = [psum[:, 4 * c:4 * c + 4, :].rearrange("p (g a) b -> p g (a b)", g=2) for c in range(2)]

        cm_ps = [psum[:, 2 * s:2 * s + 2, :].rearrange("p a b -> p (a b)") for s in range(2)]
        tm_ps = [psum[:, 4 + s, :] for s in range(2)]
        tp_ps = [psum[:, 6 + s, :] for s in range(2)]

        block = ctx.enter_context(nc.Block())
        x_d, w_in = a["x"], a["w_in"]

        def conf_transpose(pe, t):
            if t == 0:
                pe.wait_ge(sem("cc_conv"), 1)
                pe.wait_ge(sem("kT_out"), NT)
            if t >= 2:
                pe.wait_ge(sem("cc_tok"), t - 1)
            for c in range(2):
                ins = pe.transpose(tp_ps[t % 2][:, c * P:(c + 1) * P], cacc[:, c, t * P:(t + 1) * P], ident)
            ins.then_inc(sem("cc_tp"), 1)

        def conf_stats(v, t):
            v.wait_ge(sem("cc_tp"), t + 1)
            v.tensor_copy(ctok[:, t], tp_ps[t % 2][:, 0:CCH]).then_inc(sem("cc_tok"), 1)
            v.wait_ge(sem("cc_tok"), t + 1)
            v.bn_stats(lnst[:, t], ctok[:, t]).then_inc(sem("cc_st"), 1)
            v.wait_ge(sem("cc_st"), t + 1)
            v.bn_aggr(lnag[:, t], lnst[:, t]).then_inc(sem("cc_ag"), 1)

        def conf_dve(v):
            v.wait_ge(sem("cc_rt"), 1)
            v.reciprocal(lnr, rstd).then_inc(sem("cc_rs"), 1)
            v.wait_ge(sem("cc_rs"), 1)
            for t in range(NT):
                v.tensor_scalar(ctok[:, t], ctok[:, t], lnag[:, t, 0:1], lnr[:, t:t + 1], ALU.subtract, ALU.mult)\
                    .then_inc(sem("cc_nrm"), 1)

        def conf_back(pe):
            for t in range(NT):
                pe.wait_ge(sem("cc_nrm"), t + 1)
                if t == 0:
                    pe.wait_ge(sem("cat_out"), 4)
                for c in range(2):
                    ins = pe.transpose(cm_ps[c][:, t * P:(t + 1) * P], ctok[:, t, c * P:(c + 1) * P], ident)
            ins.then_inc(sem("cc_bk"), 1)

        def conf_act(act):
            act.wait_ge(sem("cc_ag"), NT)
            act.activation(rstd, lnag[:, :, 1], ACT.Sqrt, bias=eps_c).then_inc(sem("cc_rt"), 1)
            act.wait_ge(sem("cc_bk"), 1)
            for c in range(2):
                act.activation(cact[:, c], cm_ps[c], ACT.Silu, scale=pcol[:, PC_LNG + c:PC_LNG + c + 1],
                               bias=pcol[:, PC_LNB + c:PC_LNB + c + 1]).then_inc(sem("cc_act"), 1)
            act.wait_ge(sem("cc_act"), 2)
            act.wait_ge(sem("tm_done"), 3 * NT)
            act.activation(mix_hi[:, 6:8, :], cact, ACT.Copy).then_inc(sem("cc_hi"), 1)

        nsa_pt = [s for s in MIX if s[0] in ("Nq", "Nc2", "Nidx", "NT", "No")]

        def pt_use(step):
            return nsa_pt.index(step)

        nsa_slot = [s for s in nsa_pt if s[0] in ("Nc2", "NT")]

        def pts(step):
            return PTs[nsa_slot.index(step) % 2]

        def s_use(t, kind, h):
            return 2 * NH * t + NH * (1 - kind) + h

        LO, HI = slice(0, CH), slice(CH, P)

        def mixer_loads(sp):
            sp.dma_start(dtb, a["gdn_dt_bias"][0].partition_broadcast(P)).then_inc(sem("gp_in"), 16)
            sp.dma_start(alog, a["gdn_a_log"][0].partition_broadcast(P)).then_inc(sem("gp_in"), 16)
            sp.wait_ge(sem("wc_zero"), 2)
            for w, dst, name in (("nsa_cmp_wk", wck, "wck_in"), ("nsa_cmp_wv", wcv, "wcv_in")):
                if dst is wcv:
                    sp.wait_ge(sem("wc_zero"), 4)
                for kv in range(KV):
                    r = slice(HD * kv, HD * kv + HD)
                    sp.dma_start(dst[r, :, HD * kv:HD * kv + HD], a[w][0].rearrange("l d e -> d l e")).then_inc(sem(name), 16)
            sp.wait_ge(sem("vc_out"), 4)
            for p, kv in ((0, 0), (1, 1), (2, 1)):
                sp.dma_start(vcbd[CH:CH + NCMP, p, HD:P], qn.rearrange("p h d -> p (h d)")[0:NCMP, P + HD * kv:P + HD * kv + HD])\
                    .then_inc(sem("vcbd_in"), 16)

        def mixer_constants(pool, own, part):
            def fill(m, value):
                own.up(pool.memset(m, value))

            def keep(m, pattern, base, cm, fill_, op=ALU.is_ge):
                own.settle(pool)
                own.up(pool.affine_select(out=m, in_=m, compare_op=op, fill=fill_, base=base, pattern=pattern, channel_multiplier=cm))

            if part == 0:
                pool.wait_ge(sem("w_hi"), 4 * len(BLOCKS))
                pool.wait_ge(sem("w_lo"), 4 * len(BLOCKS))
                fill(ones_c, 1.0)
                fill(tri, 1.0)
                keep(tri, [[1, NSLC], [-1, NSLC]], 0, 0, 0.0, ALU.is_gt)
                for m in (maskD, negI, Ic, Ucum, SL):
                    fill(m, 0.0)
                for m in (Umask, strict):
                    fill(m, 1.0)
                for m in (causal, far):
                    fill(m, 0.0)
                fill(cmask, 0.0)
                fill(blk_of[0:NSLC], 1.0)
                fill(nm, -1.0)
                fill(half_ones[0], 0.0)
                fill(half_ones[1], 0.0)
                fill(forced, 0.0)
                fill(scored, 1.0)
            elif part == CONST_PARTS - 1:
                keep(causal, [[-1, P]], 0, 1, NEG)
                keep(far, [[1, P]], 0, -1, NEG, ALU.is_gt)
                keep(cmask, [[P, NT], [-STRIDE, CH]], -(CLEN - 1), 1, NEG)
                keep(blk_of[0:NSLC], [[1, S]], 0, -SLC, 0.0)
                keep(blk_of[0:NSLC], [[-1, S]], SLC - 1, SLC, 0.0)
                for i in range(4):
                    for half, rows in enumerate((LO, HI)):
                        cur = 2 * (4 + i) + half
                        for c0, c1, value in ((0, 1, FORCE), (cur - 1, cur + 1, FORCE), (cur + 1, NSLC, -1.0)):
                            if c0 < c1:
                                fill(forced[rows, i, c0:c1], value)
                                fill(scored[rows, i, c0:c1], 0.0)
                own.settle(pool)
                pool.memset(rank, 0.0).then_inc(sem("mix_consts"), 1)
            elif part in (1, 4):
                rows = LO if part == 1 else HI
                keep(maskD[rows], [[1, CH]], 0, -1, NEG)
                keep(negI[rows], [[1, CH]], 0, -1, -1.0, ALU.not_equal)
                keep(Ic[rows], [[1, CH]], 0, -1, 1.0, ALU.not_equal)
                keep(Umask[rows], [[1, CH]], 0, -1, 0.0)
                keep(strict[rows], [[1, CH]], 0, -1, 0.0, ALU.is_gt)
                fill(Ucum[rows, rows], 1.0)
                fill(SL[rows, rows], 1.0)
                keep(Ucum[rows, rows], [[1, CH]], 0, -1, 0.0)
                keep(SL[rows, rows], [[-1, CH]], 0, 1, 0.0, ALU.is_gt)
                fill(half_ones[rows.start // CH][rows], 1.0)
            else:
                rows = LO if part < 4 else HI
                for l in range(0, 3) if part in (2, 5) else range(3, LEVELS):
                    b = 1 << l
                    n = CH // (2 * b)
                    m = nm[rows, l].rearrange("p (n h c) -> p n h c", n=n, h=2)
                    own.settle(pool)
                    fill(m[:, :, 1], 0.0)
                    keep(m[:, :, 0], [[-2 * b, n], [0, b]], -b, 1, 0.0)
                    keep(m[:, :, 0], [[2 * b, n], [0, b]], 2 * b - 1, -1, 0.0)
                    keep(nm[rows, l], [[1, CH]], 0, -1, -1.0, ALU.not_equal)
            own.settle(pool)

        def zero_cmp_weights(pool, w):
            for kv in range(KV):
                pool.memset(w[HD * kv:HD * kv + HD, :, HD * (1 - kv):HD * (1 - kv) + HD], 0.0).then_inc(sem("wc_zero"), 1)

        def mixer_pool(pool):
            pool.wait_ge(sem("tm_done"), 3 * NT)
            pool.wait_ge(sem("rot"), 4 * NT)
            zero_cmp_weights(pool, wcv)
            pool.wait_ge(sem("wc_zero"), 4)
            pool.wait_ge(sem("cc_hi"), 1)
            pool.tensor_tensor(mix_lo[:, 6:8, :], cact, mix_hi[:, 6:8, :], ALU.subtract).then_inc(sem("cc_lo"), 1)
            pool.wait_ge(sem("kc_mul"), 2)
            pool.wait_ge(sem("vc_mm"), 1)
            kc = qn.rearrange("p h d -> p (h d)")[:, 0:P]
            pool.memset(vcbd, 0.0).then_inc(sem("kc_zero"), 1)
            pool.memset(kc, 0.0).then_inc(sem("kc_zero"), 1)
            pool.wait_ge(sem("kc_zero"), 2)
            o = kc[0:NCMP].rearrange("p (h e d) -> p h e d", h=2, e=2)
            c_ = vn.rearrange("p h d -> p (h d)")[0:NCMP, 0:P].rearrange("p (h e d) -> p h e d", h=2, e=2)
            s_ = on.rearrange("p h d -> p (h d)")[0:NCMP, 0:P].rearrange("p (h e d) -> p h e d", h=2, e=2)
            pool.tensor_tensor(o[:, :, 0, :], c_[:, :, 0, :], s_[:, :, 1, :], ALU.subtract).then_inc(sem("kc_rot"), 1)
            pool.tensor_tensor(o[:, :, 1, :], s_[:, :, 0, :], c_[:, :, 1, :], ALU.add).then_inc(sem("kc_rot"), 1)
            pool.memset(qpad, 0.0).then_inc(sem("mix_zero"), 1)

            def scaled(dst, src, by, t):
                return pool.tensor_tensor(dst, src, bc(by[:, GH * t:GH * t + GH], 2, HD), ALU.mult)

            def A1b(t):
                pool.wait_ge(sem("g_n"), 2 * t + 2)
                scaled(kb, kn, beta, t).then_inc(sem("g_kq"), 1)
                scaled(qg, qn, EG, t).then_inc(sem("g_kq"), 1)
                pool.wait_ge(sem("g_kq"), 2 * t + 2)
                scaled(kbg, kb, EG, t).then_inc(sem("g_kk2"), 1)
                if t >= 2:
                    pool.wait_ge(sem("b_dm"), 2 * t - 2)
                scaled(kdec[t % 2], kn, ED, t).then_inc(sem("g_kk2"), 1)

            def A3a(t):
                if t:
                    pool.wait_ge(sem("g_uwm"), 2 * t)
                pool.tensor_tensor(Drhs, bc(Umask, 1, GH), bc(graw[:, GH * t:GH * t + GH], 2, CH), ALU.mult).then_inc(sem("g_drhs"), 1)
                pool.wait_ge(sem("g_DT"), t + 1)
                pool.tensor_tensor(DTs, DTc, bc(strict, 1, GH), ALU.mult).then_inc(sem("g_DTs"), 1)

            def C1(t):
                pool.wait_ge(sem("c_on"), t + 1)
                pool.tensor_tensor(on, on, zab[:, t, 0:GDIM].rearrange("p (h d) -> p h d", h=GH), ALU.mult).then_inc(sem("c_og"), 1)

            def C2(t):
                pool.wait_ge(sem("c_hi"), t + 1)
                tok = slice(t * P, (t + 1) * P)
                pool.tensor_tensor(mix_lo[:, 0:3, tok], mtmp, mix_hi[:, 0:3, tok], ALU.subtract).then_inc(sem("m_lo"), 1)

            def Nc1(t):
                if t == 0:
                    pool.wait_ge(sem("n_pcn"), 1)
                    pool.affine_select(out=csc, in_=csc, compare_op=ALU.is_ge, fill=0.0, base=-(CLEN - 1),
                                       pattern=[[0, NH], [-STRIDE, CH]], channel_multiplier=1).then_inc(sem("n_pc0"), 1)

            def add(t, n):
                pool.wait_ge(sem("n_ot"), 2 * t + n + 1)
                pool.tensor_tensor(oacc, oacc, otmp, ALU.add).then_inc(sem("n_acc"), 1)

            def Nc3(t):
                add(t, 0)

            def Ne(t, kind):
                if kind == 0:
                    add(t, 1)

            def No(t):
                pool.wait_ge(sem("n_hi"), t + 1)
                tok = slice(t * P, (t + 1) * P)
                pool.tensor_tensor(mix_lo[:, 3:6, tok], mtmp_n, mix_hi[:, 3:6, tok], ALU.subtract).then_inc(sem("mn_lo"), 1)

            def WO(c):
                pool.wait_ge(*late("wo_hi", c + 1))
                pool.tensor_tensor(wo_lo[:, c], wo_st[c % 4], wo_hi[:, c], ALU.subtract).then_inc(late("wo_lo")[0], 1)

            run(dict(WO=WO, A1b=A1b, A3a=A3a, C1n=C1, C2=C2, Nc1b=Nc1, Nc3=Nc3, Ne=Ne, No=No))

        def run(steps):
            for step in MIX:
                if step[0] in steps:
                    steps[step[0]](*step[1:])

        def mixer_act(act):
            flat = lambda x: x.rearrange("p h d -> p (h d)")
            act.preload_act_table_set("natural_log_exp_and_others")
            act.wait_ge(sem("gp_abs"), 1)
            act.wait_ge(sem("mix_consts"), 1)
            act.activation(stat_a, stat_b, ACT.Exp, scale=-1.0).then_inc(sem("gp_e"), 1)
            act.wait_ge(sem("gp_e"), 1)
            act.activation(stat_a, stat_a, ACT.Ln, bias=ones_c).then_inc(sem("gp_e"), 1)
            act.activation(alog, alog, ACT.Exp).then_inc(sem("gp_e"), 1)
            act.activation(stat_c, zab[:, :, GDIM + GH:], ACT.Exp, scale=-1.0).then_inc(sem("gp_e"), 1)
            act.activation(gate, gate, ACT.Exp, scale=-1.0).then_inc(sem("gp_e"), 1)
            act.wait_ge(sem("gp_cum"), 1)
            act.activation(EG, psum[:, 4, 0:48], ACT.Exp).then_inc(sem("gp_exp"), 1)
            act.activation(ED, psum[:, 4, 64:112], ACT.Exp).then_inc(sem("gp_exp"), 1)
            for c in range(2):
                for par, rows in enumerate((LO, HI)):
                    src = psum[rows, 4, 128 + 64 * c:176 + 64 * c].rearrange("p (t h e) -> p t h e", t=NT, e=2)[:, :, :, par]
                    act.activation(EGL[rows, :, c, :], src, ACT.Exp).then_inc(sem("gp_exp"), 1)
            act.wait_ge(sem("vc_mm"), 1)
            act.wait_ge(sem("kc_zero"), 2)
            vc = psum[0:NCMP, 7, 0:P]
            for p, kv in ((0, 0), (1, 0), (2, 1)):
                act.activation(vcbd[0:NCMP, p, 0:HD], vc[:, HD * kv:HD * kv + HD], ACT.Copy).then_inc(sem("vc_out"), 1)
            act.activation(flat(qn)[0:NCMP, P:2 * P], vc, ACT.Copy).then_inc(sem("vc_out"), 1)
            act.wait_ge(sem("kcT_mm"), 1)
            act.activation(kcT, psum[:, 2, 0:CH], ACT.Copy).then_inc(sem("kcT_out"), 1)

            act.wait_ge(sem("mix_zero"), 1)

            def A1a(t):
                act.wait_ge(sem("g_qk"), t + 1)
                for i in range(2):
                    act.activation(flat(sq)[:, GDIM * i:GDIM * i + GDIM], psum[:, i, 0:GDIM], ACT.Square).then_inc(sem("g_sq"), 1)

            def A1s(t):
                act.wait_ge(sem("g_ss"), t + 1)
                act.activation(rs, ss, ACT.Ln, bias=eps_c).then_inc(sem("g_ln"), 1)
                act.wait_ge(sem("g_ln"), t + 1)
                act.activation(rs, rs, ACT.Exp, scale=-0.5).then_inc(sem("g_rs"), 1)

            def A2a(t):
                act.wait_ge(sem("g_t1"), 2 * t + 2)
                act.activation(kTn, psum[:, 1, 0:GDIM].rearrange("p (h c) -> p h c", h=3), ACT.Copy).then_inc(sem("g_kT"), 1)

            def A2b(t):
                act.wait_ge(sem("g_t2"), 2 * t + 2)
                act.activation(flat(qT), psum[:, 1, 0:GDIM], ACT.Copy).then_inc(sem("g_qT"), 1)

            def A3a(t):
                act.wait_ge(sem("g_D"), t + 1)
                act.activation(flat(DTc), psum[:, 0, 0:GDIM], ACT.Exp).then_inc(sem("g_DT"), 1)

            def X(t, l):
                act.wait_ge(sem("g_Xm"), 4 * t + l)
                act.activation(flat(Xc), psum[:, 1, 0:GDIM], ACT.Copy).then_inc(sem("g_X"), 1)

            def XT(t, l):
                act.wait_ge(sem("g_Tm"), LEVELS * t + l + 1)
                act.activation(flat(Tc), psum[:, 0, 0:GDIM], ACT.Copy).then_inc(sem("g_Tc"), 1)

            def A4(t):
                act.wait_ge(sem("g_uwm"), 2 * t + 1)
                act.activation(flat(uu[t % 2]), psum[:, 0, 0:GDIM], ACT.Copy).then_inc(sem("g_uw"), 1)
                act.wait_ge(sem("g_uwm"), 2 * t + 2)
                act.activation(flat(nwT[t % 2]), psum[:, 1, 0:GDIM], ACT.Copy, scale=-1.0).then_inc(sem("g_uw"), 1)

            def C1(t):
                act.wait_ge(sem("b_o"), t + 1)
                if t:
                    act.wait_ge(sem("m_lo"), t)
                act.activation(flat(sq2), psum[:, 3, 0:GDIM], ACT.Square).then_inc(sem("c_sq"), 1)

            def C1s(t):
                act.wait_ge(sem("c_ss"), t + 1)
                act.activation(rs2, ss2, ACT.Ln, bias=eps_c, scale=1.0 / HD).then_inc(sem("c_ln"), 1)
                act.wait_ge(sem("c_ln"), t + 1)
                act.activation(rs2, rs2, ACT.Exp, scale=-0.5).then_inc(sem("c_rs"), 1)

            def C2(t):
                act.wait_ge(sem("c_tp"), t + 1)
                tok = slice(t * P, (t + 1) * P)
                act.activation(flat(mtmp), psum[:, 2, 0:GDIM], ACT.Copy, scale=gng).then_inc(sem("c_m"), 1)
                act.wait_ge(sem("c_m"), t + 1)
                act.activation(mix_hi[:, 0:3, tok], mtmp, ACT.Copy).then_inc(sem("c_hi"), 1)

            def Nq(t):
                act.wait_ge(sem("n_ptm"), pt_use(("Nq", t)) + 1)
                ps = psum[:, 6, 0:GDIM].rearrange("p (g c) -> p g c", g=GRP)
                act.activation(qpad[LO, 0], ps[LO], ACT.Copy).then_inc(sem("n_q"), 1)
                act.activation(qpad[HI, 1], ps[HI], ACT.Copy).then_inc(sem("n_pt"), 1)

            def Nc1(t):
                act.wait_ge(sem("n_csc"), t + 1)
                act.activation(flat(csc), flat(csc), ACT.Exp).then_inc(sem("n_cex"), 1)

            def Nc2(t):
                u = pt_use(("Nc2", t))
                act.wait_ge(sem("n_ptm"), u + 1)
                act.activation(pts(("Nc2", t))[:, 0:GDIM], psum[:, 6, 0:GDIM], ACT.Copy).then_inc(sem("n_pt"), 1)

            def Nidx(t):
                act.wait_ge(sem("n_ptm"), pt_use(("Nidx", t)) + 1)
                act.activation(selT[0:NSLC], psum[0:NSLC, 6, 0:2 * P].rearrange("p (k c) -> p k c", k=KV), ACT.Copy).then_inc(sem("n_pt"), 1)

            def Nx(t, kind, h):
                k0, k1 = key_blocks(t, kind)
                u = s_use(t, kind, h)
                n = (k1 - k0) * P
                act.wait_ge(sem("n_mx"), u + 1)
                act.activation(Pb[u % 2][:, 0:n], psum[:, 4:6, :].rearrange("p a b -> p (a b)")[:, 0:n], ACT.Exp,
                               bias=nmx[:, u % 2:u % 2 + 1], accum_out=psums[:, NH * kind + h:NH * kind + h + 1]).then_inc(sem("n_exp"), 1)

            def NT_(t, kind, h, n):
                u = pt_use(("NT", t, kind, h, n))
                b0, b1 = batches(t, kind)[n]
                act.wait_ge(sem("n_ptm"), u + 1)
                act.activation(pts(("NT", t, kind, h, n))[:, 0:(b1 - b0) * P], psum[:, 6, 0:(b1 - b0) * P], ACT.Copy).then_inc(sem("n_pt"), 1)

            def No(t):
                act.wait_ge(sem("n_ptm"), pt_use(("No", t)) + 1)
                tok = slice(t * P, (t + 1) * P)
                act.activation(flat(mtmp_n), psum[:, 6, 0:GDIM], ACT.Copy).then_inc(sem("n_pt"), 1)
                act.wait_ge(sem("n_pt"), pt_use(("No", t)) + 1)
                act.activation(mix_hi[:, 3:6, tok], mtmp_n, ACT.Copy).then_inc(sem("n_hi"), 1)

            def WO(c):
                act.wait_ge(*late(f"wo_st{c % 4}", 16 * (c // 4 + 1)))
                act.activation(wo_hi[:, c], wo_st[c % 4], ACT.Copy).then_inc(late("wo_hi")[0], 1)

            run(dict(WO=WO, A1a=A1a, A1s=A1s, A2a=A2a, A2b=A2b, A3a=A3a, X=X, XT=XT, A4=A4, C1=C1, C1s=C1s, C2=C2, Nq=Nq, Nc1=Nc1, Nc2=Nc2,
                     Nidx=Nidx, Nx=Nx, NT=NT_, No=No))

        def mixer_dve(v):
            flat = lambda x: x.rearrange("p h d -> p (h d)")
            own = Count(sem("dve_own2"))

            def then(ins):
                own.up(ins)
                own.settle(v)

            v.wait_ge(sem("gp_in"), 32)
            v.wait_ge(sem("mix_consts"), 1)
            v.wait_ge(sem("tm_act"), 3 * NT)
            y3 = beta.rearrange("p (t h) -> p t h", h=GH)
            then(v.tensor_tensor(y3, zab[:, :, GDIM:GDIM + GH], bc(dtb, 1, NT), ALU.add))
            v.scalar_tensor_tensor(out=stat_b, in0=beta, scalar=-1.0, in1=beta, op0=ALU.mult, op1=ALU.max).then_inc(sem("gp_abs"), 1)
            v.wait_ge(sem("gp_e"), 5)
            then(v.scalar_tensor_tensor(out=graw, in0=beta, scalar=0.0, in1=stat_a, op0=ALU.max, op1=ALU.add))
            g3 = graw.rearrange("p (t h) -> p t h", h=GH)
            v.scalar_tensor_tensor(out=g3, in0=g3, scalar=-1.0, in1=bc(alog, 1, NT), op0=ALU.mult, op1=ALU.mult).then_inc(sem("graw"), 1)
            then(v.tensor_scalar(stat_c, stat_c, 1.0, None, ALU.add))
            then(v.reciprocal(beta.rearrange("p (t h) -> p t h", h=GH), stat_c))
            then(v.tensor_scalar(gate, gate, 1.0, None, ALU.add))
            then(v.reciprocal(gate, gate))
            v.wait_ge(sem("kc_mm"), 1)
            ps = psum[0:NCMP, 6, 0:P].rearrange("p (c d) -> p c d", d=32)
            for tab, dst in ((cos_t, vn), (sin_t, on)):
                v.tensor_tensor(flat(dst)[0:NCMP, 0:P].rearrange("p (c d) -> p c d", d=32), ps, bc(tab[0:NCMP, NT], 1, 4), ALU.mult)\
                    .then_inc(sem("kc_mul"), 1)
            v.wait_ge(sem("vc_mm"), 1)
            then(v.memset(Sbd, 0.0))

            def A1r(t):
                v.wait_ge(sem("g_sq"), 2 * t + 2)
                v.tensor_reduce(ss, sq, AX.X, ALU.add).then_inc(sem("g_ss"), 1)

            def A1n(t):
                v.wait_ge(sem("g_rs"), t + 1)
                if t == 0:
                    v.wait_ge(sem("vcbd_in"), 48)
                v.scalar_tensor_tensor(out=qn, in0=psum[:, 0, 0:GDIM].rearrange("p (h d) -> p h d", h=GH), scalar=HD ** -0.5,
                                       in1=bc(rs[:, 0:GH], 2, HD), op0=ALU.mult, op1=ALU.mult).then_inc(sem("g_n"), 1)
                v.tensor_tensor(kn, psum[:, 1, 0:GDIM].rearrange("p (h d) -> p h d", h=GH), bc(rs[:, GH:], 2, HD), ALU.mult)\
                    .then_inc(sem("g_n"), 1)

            def A1b(t):
                v.wait_ge(sem("g_v"), t + 1)
                v.tensor_tensor(vb, psum[:, 0, 0:GDIM].rearrange("p (h d) -> p h d", h=GH),
                                bc(beta[:, GH * t:GH * t + GH], 2, HD), ALU.mult).then_inc(sem("g_vb"), 1)

            def A2a(t):
                v.wait_ge(sem("g_t1"), 2 * t + 2)
                v.tensor_copy(flat(kbT), psum[:, 0, 0:GDIM]).then_inc(sem("g_kbT"), 1)

            def A2b(t):
                v.wait_ge(sem("g_t2"), 2 * t + 2)
                v.tensor_copy(flat(qgT[t % 2]), psum[:, 0, 0:GDIM]).then_inc(sem("g_qgT"), 1)

            def A3a(t):
                v.wait_ge(sem("g_DTs"), t + 1)
                v.wait_ge(sem("g_kk"), t + 1)
                v.tensor_tensor(flat(LTc), psum[:, 1, 0:GDIM], flat(DTs), ALU.mult).then_inc(sem("g_LT"), 1)

            def A3b(t):
                v.wait_ge(sem("g_qk2"), t + 1)
                if t >= 2:
                    v.wait_ge(sem("b_o"), t - 1)
                v.tensor_tensor(flat(QTc[t % 2]), psum[:, 0, 0:GDIM], flat(DTc), ALU.mult).then_inc(sem("g_QTc"), 1)

            def M(t, l):
                v.wait_ge(sem("g_M"), LEVELS * t + l + 1)
                v.tensor_tensor(MIc, psum[:, 0, 0:GDIM].rearrange("p (h c) -> p h c", h=GH), bc(nm[:, l], 1, GH), ALU.mult)\
                    .then_inc(sem("g_MIc"), 1)

            def B1(t, c):
                rows = (LO, HI)[c]
                n = 2 * t + c
                v.wait_ge(sem("b_vm"), n + 1)
                v.tensor_tensor(flat(vn)[rows], psum[rows, 2, 0:GDIM], flat(uu[t % 2])[rows], ALU.add).then_inc(sem("b_vn"), 1)
                v.wait_ge(sem("b_o1"), n + 1)
                then(v.tensor_tensor(Sbd, Sbd, bc(EGL[:, t, c], 2, P), ALU.mult))

            def B2(t, c):
                n = 2 * t + c
                v.wait_ge(sem("b_dm"), n + 1)
                ps = psum[:, 2, 0:GDIM].rearrange("p (h c) -> p h c", h=3)
                for rows in (LO, HI):
                    v.tensor_tensor(Sbd[rows, :, rows], Sbd[rows, :, rows], ps[rows, :, rows], ALU.add).then_inc(sem("b_S"), 1)

            def C1r(t):
                v.wait_ge(sem("c_sq"), t + 1)
                v.tensor_reduce(ss2, sq2, AX.X, ALU.add).then_inc(sem("c_ss"), 1)

            def C1n(t):
                v.wait_ge(sem("c_rs"), t + 1)
                v.tensor_tensor(on, psum[:, 3, 0:GDIM].rearrange("p (h d) -> p h d", h=GH), bc(rs2, 2, HD), ALU.mult).then_inc(sem("c_on"), 1)

            gates = gate.rearrange("p t (h k) -> p t h k", k=3)
            heads = lambda ap: ap.rearrange("p (h d) -> p h d", h=NH)

            def Nc1(t):
                v.wait_ge(sem("n_cm"), t + 1)
                ps = heads(psum[:, 4, 0:GDIM])
                then(v.tensor_reduce(cmx, ps, AX.X, ALU.max))
                if t:
                    v.wait_ge(sem("n_ptm"), pt_use(("Nc2", t - 1)) + 1)
                v.tensor_tensor(csc, ps, bc(cmx, 2, CH), ALU.subtract).then_inc(sem("n_csc"), 1)

            def Nc1b(t):
                v.wait_ge(sem("n_cex"), t + 1)
                then(v.tensor_reduce(csum, csc, AX.X, ALU.add))
                then(v.reciprocal(csum, csum))
                v.tensor_tensor(csc, csc, bc(csum, 2, CH), ALU.mult).then_inc(sem("n_pcn"), 1)

            def Nc3(t):
                v.wait_ge(sem("n_om"), 3 * t + 2)
                if t:
                    v.wait_ge(sem("mn_lo"), t)
                v.tensor_tensor(otmp, heads(psum[:, 7, 0:GDIM]), bc(gates[:, t, :, 0], 2, HD), ALU.mult).then_inc(sem("n_ot"), 1)

            def Nr(t, kv, part):
                i4 = t - 4
                of_i, of_j = bc(imp, 1, NSLC), bc(imp, 2, NSLC)
                if part == 0:
                    pcs = csc[:, GRP * kv:GRP * kv + GRP].rearrange("p g n -> p n g")
                    if kv == 0:
                        then(v.memset(pg[:, 0:1], 0.0))
                    then(v.tensor_reduce(pg[:, 1:1 + CH], pcs, AX.X, ALU.add))
                    then(v.tensor_reduce(imp, pg[:, 1:1 + CH].rearrange("p (j i) -> p j i", i=4), AX.X, ALU.add))
                elif part == 1:
                    then(v.tensor_tensor(imp, imp, pg[:, 0:CH].rearrange("p (j i) -> p j i", i=4)[:, :, 0], ALU.add))
                    then(v.tensor_tensor(imp, imp, scored[:, i4], ALU.mult))
                    then(v.tensor_tensor(imp, imp, forced[:, i4], ALU.add))
                elif part == 2:
                    then(v.tensor_tensor(cmpe, of_i, of_j, ALU.is_equal))
                    then(v.tensor_tensor(cmpe, cmpe, tri, ALU.mult))
                    then(v.tensor_tensor(cmpg, of_i, of_j, ALU.is_gt))
                else:
                    then(v.tensor_tensor(cmpg, cmpg, cmpe, ALU.add))
                    then(v.tensor_reduce(rank, cmpg, AX.X, ALU.add))
                    if kv == 0 and i4:
                        v.wait_ge(sem("n_ptm"), pt_use(("Nidx", t - 1)) + 1)
                    v.tensor_scalar(selb[:, kv], rank, float(TOPK), NEG, ALU.is_ge, ALU.mult).then_inc(sem("n_sel"), 1)

            def Ns(t, kind, h):
                k0, k1 = key_blocks(t, kind)
                u = s_use(t, kind, h)
                n = (k1 - k0) * P
                v.wait_ge(sem("n_sm"), u + 1)
                v.tensor_reduce(nmx[:, u % 2:u % 2 + 1], psum[:, 4:6, :].rearrange("p a b -> p (a b)")[:, 0:n], AX.X, ALU.max,
                                negate=True).then_inc(sem("n_mx"), 1)

            def Ne(t, kind):
                v.wait_ge(sem("n_exp"), s_use(t, kind, NH - 1) + 1)
                then(v.reciprocal(coef, psums[:, NH * kind:NH * kind + NH]))
                then(v.tensor_tensor(coef, coef, gates[:, t, :, 1 + kind], ALU.mult))
                v.wait_ge(sem("n_om"), 3 * t + (1 if kind else 3))
                o = heads(psum[:, 7, 0:GDIM])
                if kind:
                    if t:
                        v.wait_ge(sem("n_ptm"), pt_use(("No", t - 1)) + 1)
                    v.tensor_tensor(oacc, o, bc(coef, 2, HD), ALU.mult).then_inc(sem("n_oc"), 1)
                else:
                    v.wait_ge(sem("n_acc"), 2 * t + 1)
                    v.tensor_tensor(otmp, o, bc(coef, 2, HD), ALU.mult).then_inc(sem("n_ot"), 1)

            run(dict(A1r=A1r, A1n=A1n, A1b=A1b, A2a=A2a, A2b=A2b, A3a=A3a, A3b=A3b, M=M, B1=B1, B2=B2, C1r=C1r,
                     C1n=C1n, Nc1=Nc1, Nc1b=Nc1b, Nc3=Nc3, Nr=Nr, Ns=Ns, Ne=Ne))

        def mixer_pe(pe):
            pe.wait_ge(sem("rot_mul"), 2 * NT)
            pe.wait_ge(sem("cc_tok"), NT)
            for cat, w, bank, name, out_ in ((kcat, wck, 6, "wck_in", "kc_mm"), (vcat, wcv, 7, "wcv_in", "vc_mm")):
                pe.wait_ge(sem(name), 32)
                for l in range(CLEN):
                    lhs = cat[:, l // STRIDE, l:l + STRIDE * (NCMP - 1) + 1:STRIDE]
                    ins = pe.matmul(psum[0:NCMP, bank, 0:P], lhs, w[:, l], start=(l == 0), stop=(l == CLEN - 1))
                ins.then_inc(sem(out_), 1)
                if cat is kcat:
                    conf_back(pe)
            pe.wait_ge(sem("graw"), 1)
            pe.wait_ge(sem("mix_consts"), 1)
            pe.wait_ge(sem("tm_act"), 3 * NT)
            for i, m in enumerate((Ucum, SL, half_ones[0], half_ones[1])):
                ins = pe.matmul(psum[:, 4, 64 * i:64 * i + 48], m, graw, start=True, stop=True)
            ins.then_inc(sem("gp_cum"), 1)
            pe.wait_ge(sem("cc_act"), 2)
            pe.wait_ge(sem("kc_rot"), 2)
            pe.transpose(psum[:, 2, 0:CH], qn.rearrange("p h d -> p (h d)")[0:CH, 0:P], ident[0:CH, 0:CH]).then_inc(sem("kcT_mm"), 1)
            def blocks(bank, src, s):
                for p in range(3):
                    ins = pe.transpose(psum[:, bank, p * P:(p + 1) * P], src[:, p * P:(p + 1) * P], ident)
                return ins.then_inc(sem(s), 1)

            flat = lambda x: x.rearrange("p h d -> p (h d)")

            def A1a(t):
                if t:
                    pe.wait_ge(sem("g_uw"), 2 * t)
                tok = slice(t * P, (t + 1) * P)
                for i in range(2):
                    for p in range(3):
                        ins = pe.transpose(psum[:, i, p * P:(p + 1) * P], qkvT[:, 3 * i + p, tok], ident)
                ins.then_inc(sem("g_qk"), 1)

            def A1b(t):
                pe.wait_ge(sem("g_n"), 2 * t + 2)
                tok = slice(t * P, (t + 1) * P)
                for p in range(3):
                    ins = pe.transpose(psum[:, 0, p * P:(p + 1) * P], qkvT[:, 6 + p, tok], ident)
                ins.then_inc(sem("g_v"), 1)

            def A2a(t):
                blocks(1, flat(kn), "g_t1")
                pe.wait_ge(sem("g_vb"), t + 1)
                pe.wait_ge(sem("g_kq"), 2 * t + 2)
                blocks(0, flat(kb), "g_t1")

            def A2b(t):
                pe.wait_ge(sem("g_kT"), t + 1)
                blocks(1, flat(qn), "g_t2")
                pe.wait_ge(sem("g_kbT"), t + 1)
                blocks(0, flat(qg), "g_t2")

            own = Count(sem("pe_half"))

            def quarters(product, s):
                for swap in range(2):
                    for h in range(GH):
                        par = (LO, HI)[h % 2]
                        ins = product(h, par, (LO, HI)[h % 2 ^ swap])
                    if swap == 0:
                        own.up(ins)
                        own.settle(pe)
                ins.then_inc(sem(s), 1)

            def products(bank, rhs, s):
                quarters(lambda h, par, rows: pe.matmul(psum[rows, bank, h * CH:(h + 1) * CH], kTn[par, h // 2, rows],
                                                        rhs[par, h // 2, rows], start=True, stop=True), s)

            def per_chunk(out, lhs, rhs, start=True):
                for h in range(GH):
                    for rows in (LO, HI):
                        ins = pe.matmul(out[rows, h * CH:(h + 1) * CH], lhs[rows, h], rhs[rows, h], start=start, stop=True,
                                        skip_group_check=True)
                return ins

            def A3a(t):
                pe.wait_ge(sem("g_qgT"), t + 1)
                pe.wait_ge(sem("g_drhs"), t + 1)
                o = psum[:, 0, 0:GDIM].rearrange("p (h c) -> p h c", h=GH)
                pe.matmul(o, identb, bc(maskD, 1, GH), start=True, stop=True, skip_group_check=True)
                pe.matmul(o, SL, Drhs, start=False, stop=True, skip_group_check=True).then_inc(sem("g_D"), 1)
                pe.wait_ge(sem("g_qT"), t + 1)
                products(1, kbT, "g_kk")

            def A3b(t):
                pe.wait_ge(sem("g_DT"), t + 1)
                products(0, qT, "g_qk2")

            def M(t, l):
                if l == 0:
                    pe.wait_ge(sem("g_QTc"), t + 1)
                    pe.wait_ge(sem("g_LT"), t + 1)
                else:
                    pe.wait_ge(sem("g_Tc"), LEVELS * t + l)
                    if l >= 2:
                        pe.wait_ge(sem("g_X"), 4 * t + l - 1)
                o = psum[:, 0, 0:GDIM].rearrange("p (h c) -> p h c", h=GH)
                pe.matmul(o, identb, bc(negI, 1, GH), start=True, stop=True, skip_group_check=True)
                x = bc(Ic, 1, GH) if l == 0 else MIc if l == 1 else Xc
                per_chunk(psum[:, 0, :], LTc, x, start=False).then_inc(sem("g_M"), 1)

            def X(t, l):
                pe.wait_ge(sem("g_MIc"), LEVELS * t + l + 1)
                pe.wait_ge(sem("g_Tc"), LEVELS * t + l)
                per_chunk(psum[:, 1, :], Tc, MIc).then_inc(sem("g_Xm"), 1)

            def XT(t, l):
                pe.wait_ge(sem("g_MIc"), LEVELS * t + l + 1)
                per_chunk(psum[:, 0, :], MIc, bc(Ic, 1, GH) if l == 0 else Tc).then_inc(sem("g_Tm"), 1)

            def A4(t):
                pe.wait_ge(sem("g_Tc"), LEVELS * (t + 1))
                pe.wait_ge(sem("g_kk2"), 2 * t + 2)
                per_chunk(psum[:, 0, :], Tc, vb).then_inc(sem("g_uwm"), 1)
                quarters(lambda h, par, rows: pe.matmul(psum[par, 1, (h // 2) * P + rows.start:(h // 2) * P + rows.stop],
                                                        kbg[rows, h], Tc[rows, h], start=True, stop=True), "g_uwm")

            def B1(t, c):
                n = 2 * t + c
                rows = (LO, HI)[c]
                pe.wait_ge(sem("g_uw"), 2 * t + 2)
                if n:
                    pe.wait_ge(sem("b_S"), 2 * n)
                if c == 0 and t:
                    pe.wait_ge(sem("c_m"), t)
                for p in range(3):
                    ins = pe.matmul(psum[rows, 2, p * P:(p + 1) * P], nwT[t % 2][:, p, rows], Sbd[:, p], start=True, stop=True)
                ins.then_inc(sem("b_vm"), 1)
                if c == 0 and t:
                    pe.wait_ge(sem("c_on"), t)
                for p in range(3):
                    ins = pe.matmul(psum[rows, 3, p * P:(p + 1) * P], qgT[t % 2][:, p, rows], Sbd[:, p], start=(p == 0), stop=True,
                                    skip_group_check=True)
                ins.then_inc(sem("b_o1"), 1)

            def B2(t, c):
                rows = (LO, HI)[c]
                pe.wait_ge(sem("b_vn"), 2 * t + c + 1)
                for p in range(3):
                    ins = pe.matmul(psum[:, 2, p * P:(p + 1) * P], flat(kdec[t % 2])[rows, p * P:(p + 1) * P],
                                    flat(vn)[rows, p * P:(p + 1) * P], start=True, stop=True)
                ins.then_inc(sem("b_dm"), 1)

            def B3(t):
                pe.wait_ge(sem("g_QTc"), t + 1)
                per_chunk(psum[:, 3, :], QTc[t % 2], vn, start=False).then_inc(sem("b_o"), 1)

            def C2(t):
                pe.wait_ge(sem("c_og"), t + 1)
                pe.wait_ge(sem("b_S"), 4 * t + 4)
                blocks(2, flat(on), "c_tp")

            def pt_free(step):
                u = pt_use(step)
                if u:
                    pe.wait_ge(sem("n_pt"), u)

            def Nq(t):
                pt_free(("Nq", t))
                for g in range(GRP):
                    ins = pe.transpose(psum[:, 6, g * P:(g + 1) * P], qr[:, t, g].rearrange("p k d -> p (k d)"), ident)
                ins.then_inc(sem("n_ptm"), 1)

            def Nc1(t):
                pe.wait_ge(sem("n_pt"), pt_use(("Nq", t)) + 1)
                pe.wait_ge(sem("n_q"), t + 1)
                if t:
                    pe.wait_ge(sem("n_exp"), 2 * NH * t)
                else:
                    pe.wait_ge(sem("gp_exp"), 6)
                o = psum[:, 4, 0:GDIM].rearrange("p (h c) -> p h c", h=NH)
                pe.matmul(o, identb, bc(cmask[:, t], 1, NH), start=True, stop=True, skip_group_check=True)
                for h in range(NH):
                    ins = pe.matmul(o[:, h], qpad[:, h // GRP, h % GRP], kcT, start=False, stop=True, skip_group_check=True)
                ins.then_inc(sem("n_cm"), 1)

            def Nc2(t):
                pt_free(("Nc2", t))
                pe.wait_ge(sem("n_pc0"), 1) if t == 0 else pe.wait_ge(sem("n_pcn"), t + 1)
                for p in range(3):
                    ins = pe.transpose(psum[:, 6, p * P:(p + 1) * P], csc.rearrange("p h c -> p (h c)")[:, p * P:(p + 1) * P], ident)
                ins.then_inc(sem("n_ptm"), 1)

            def o_free(n):
                t, k = divmod(n, 3)
                if k == 0 and t:
                    pe.wait_ge(sem("n_ot"), 2 * t)
                elif k == 1:
                    pe.wait_ge(sem("n_oc"), t + 1)
                elif k == 2:
                    pe.wait_ge(sem("n_ot"), 2 * t + 1)

            def Nc3(t):
                u = pt_use(("Nc2", t))
                pe.wait_ge(sem("n_pt"), u + 1)
                if t == 0:
                    pe.wait_ge(sem("vcbd_in"), 48)
                o_free(3 * t + 1)
                for p in range(3):
                    ins = pe.matmul(psum[:, 7, p * P:(p + 1) * P], pts(("Nc2", t))[:, p * P:(p + 1) * P], vcbd[:, p], start=True, stop=True)
                ins.then_inc(sem("n_om"), 1)

            def Nidx(t):
                pt_free(("Nidx", t))
                pe.wait_ge(sem("n_sel"), 2 * (t - 3))
                for kv in range(KV):
                    ins = pe.transpose(psum[0:NSLC, 6, kv * P:(kv + 1) * P], selb[:, kv], ident)
                ins.then_inc(sem("n_ptm"), 1)

            def Ns(t, kind, h):
                k0, k1 = key_blocks(t, kind)
                u = s_use(t, kind, h)
                kv, g = divmod(h, GRP)
                if u % (2 * NH):
                    pe.wait_ge(sem("n_exp"), u)
                else:
                    pe.wait_ge(sem("n_csc"), t + 1)
                if kind == 0 and h == 0 and t >= 4:
                    pe.wait_ge(sem("n_pt"), pt_use(("Nidx", t)) + 1)
                for c0 in range(k0, k1, 4):
                    c1 = min(c0 + 4, k1)
                    bank = 4 + (c0 - k0) // 4
                    o = psum[:, bank, 0:(c1 - c0) * P]
                    last = c1 == k1
                    sel = kind == 0 and t >= 4
                    far_c = kind == 1 and t >= WINDOW // P and c0 == k0
                    ins = pe.matmul(o, qpad[:, kv, g], kT2[:, kind, c0 * P:c1 * P], start=True, stop=True, skip_group_check=True)
                    if sel:
                        ins = pe.matmul(o, selT[0:NSLC, kv], blk_of[0:NSLC, c0 * P:c1 * P], start=False, stop=True,
                                    skip_group_check=True)
                    if far_c:
                        ins = pe.matmul(o[:, 0:P], identb, far, start=False, stop=True, skip_group_check=True)
                    if last:
                        ins = pe.matmul(o[:, (c1 - c0 - 1) * P:], identb, causal, start=False, stop=True, skip_group_check=True)
                ins.then_inc(sem("n_sm"), 1)

            def NT_(t, kind, h, n):
                step = ("NT", t, kind, h, n)
                pt_free(step)
                u = s_use(t, kind, h)
                pe.wait_ge(sem("n_exp"), u + 1)
                k0, _ = key_blocks(t, kind)
                b0, b1 = batches(t, kind)[n]
                for b in range(b0, b1):
                    ins = pe.transpose(psum[:, 6, (b - b0) * P:(b - b0 + 1) * P], Pb[u % 2][:, (b - k0) * P:(b - k0 + 1) * P], ident)
                ins.then_inc(sem("n_ptm"), 1)

            def NV(t, kind, h, n):
                u = pt_use(("NT", t, kind, h, n))
                pe.wait_ge(sem("n_pt"), u + 1)
                if h == 0 and n == 0:
                    o_free(3 * t + 2 * (1 - kind))
                k0, k1 = key_blocks(t, kind)
                b0, b1 = batches(t, kind)[n]
                kv = h // GRP
                for b in range(b0, b1):
                    ins = pe.matmul(psum[:, 7, h * HD:(h + 1) * HD], pts(("NT", t, kind, h, n))[:, (b - b0) * P:(b - b0 + 1) * P],
                                    vsw[:, b, kind, kv * HD:kv * HD + HD], start=(h == 0 and b == k0), stop=True,
                                    skip_group_check=True)
                if h == NH - 1 and b1 == k1:
                    ins.then_inc(sem("n_om"), 1)

            def No(t):
                pt_free(("No", t))
                pe.wait_ge(sem("n_acc"), 2 * t + 2)
                for p in range(3):
                    ins = pe.transpose(psum[:, 6, p * P:(p + 1) * P], flat(oacc)[:, p * P:(p + 1) * P], ident)
                ins.then_inc(sem("n_ptm"), 1)

            run(dict(A1a=A1a, A1b=A1b, A2a=A2a, A2b=A2b, A3a=A3a, A3b=A3b, M=M, X=X, XT=XT, A4=A4, B1=B1, B2=B2, B3=B3,
                     C2=C2, Nq=Nq, Nc1=Nc1, Nc2=Nc2, Nc3=Nc3, Nidx=Nidx, Ns=Ns, NT=NT_, NV=NV, No=No))

        W_ORDER = [x for t in range(NT + 1) for x in ([("W1", t), ("WN", t)] if t < NT else []) + ([("W2", t - 1)] if t else [])]
        W_ORDER.insert(W_ORDER.index(("W1", HT)), ("US", 0))
        W_ORDER.insert(W_ORDER.index(("W2", NT - 1)), ("U1", 0))
        W_ORDER.append(("U2", 0))

        def wrun(steps):
            for name, t in W_ORDER:
                if name in steps:
                    steps[name](t)

        def wout_loads(sp):
            sp.wait_ge(sem("g_v"), NT)
            sp.wait_ge(sem("n_ptm"), pt_use(("Nq", NT - 1)) + 1)
            for c in range(KD):
                if c >= 4:
                    sp.wait_ge(*late("wo_lo", c - 3))
                sp.dma_start(wo_st[c % 4], a["w_out"][0, c * P:(c + 1) * P, :]).then_inc(late(f"wo_st{c % 4}")[0], 16)
            sp.wait_ge(sem("m_lo"), NT)
            sp.wait_ge(sem("mn_lo"), NT)
            sp.wait_ge(sem("b_S"), 4 * NT)
            sp.dma_start(gpost_mix, a["norm_mix_post"][0].partition_broadcast(P)).then_inc(sem("gpost_in"), 16)
            for t in range(2):
                sp.dma_start(xr[t], x_d[0, t * P:(t + 1) * P, :]).then_inc(late(f"xr_in{t}")[0], 16)
            sp.wait_ge(*late("wo_lo", KD))
            for s in range(2):
                up_load(sp, s, s)
            for t in range(NT):
                sp.wait_ge(*late("x1", t + 1))
                sp.dma_start(scratch[t * P:(t + 1) * P, :], x1[t % 2]).then_inc(sem(f"x1_st{t % 2}"), 16)
                if t + 2 < NT:
                    sp.dma_start(xr[t % 2], x_d[0, (t + 2) * P:(t + 3) * P, :]).then_inc(late(f"xr_in{t % 2}")[0], 16)

        def wout_act(act):
            def W1(t):
                act.wait_ge(*late("wo_mm", t + 1))
                act.activation(junk, cm_ps[t % 2], ACT.Square, accum_out=wss[:, t:t + 1]).then_inc(late("w_sq")[0], 1)
                act.wait_ge(*late("w_sq", t + 1))
                act.activation(wrs[:, t:t + 1], wss[:, t:t + 1], ACT.Ln, bias=eps_c, scale=1.0 / D).then_inc(late("w_ln")[0], 1)
                act.wait_ge(*late("w_ln", t + 1))
                act.activation(wrs[:, t:t + 1], wrs[:, t:t + 1], ACT.Exp, scale=-0.5).then_inc(late("w_rs")[0], 1)

            def WN(t):
                act.wait_ge(*late("x1", t + 1))
                act.activation(junk, x1[t % 2], ACT.Square, accum_out=wss[:, NT + t:NT + t + 1]).then_inc(late("v_sq")[0], 1)
                act.wait_ge(*late("v_sq", t + 1))
                act.activation(wrs[:, NT + t:NT + t + 1], wss[:, NT + t:NT + t + 1], ACT.Ln, bias=eps_c, scale=1.0 / D).then_inc(late("v_ln")[0], 1)
                act.wait_ge(*late("v_ln", t + 1))
                act.activation(wrs[:, NT + t:NT + t + 1], wrs[:, NT + t:NT + t + 1], ACT.Exp, scale=-0.5).then_inc(late("v_rs")[0], 1)

            def W2(t):
                act.wait_ge(*late("v_hg", t + 1))
                act.activation(h2_hi[:, :, t * P:(t + 1) * P], hg2[t % 2], ACT.Copy).then_inc(late("v_hi")[0], 1)

            def US(_):
                for s in range(2):
                    act.wait_ge(*late(f"up_st{s}", 32))
                    act.activation(up_hi[s], up_st[s], ACT.Copy).then_inc(late("up_hi")[0], 1)

            wrun(dict(W1=W1, WN=WN, W2=W2, US=US))

        def wout_pool(pool):
            def W1(t):
                pool.wait_ge(*late("w_y", t + 1))
                pool.wait_ge(*late(f"xr_in{t % 2}", 16 * (t // 2 + 1)))
                pool.tensor_tensor(x1[t % 2], x1[t % 2], xr[t % 2], ALU.add).then_inc(late("x1")[0], 1)

            def W2(t):
                pool.wait_ge(*late("v_hi", t + 1))
                tok = slice(t * P, (t + 1) * P)
                pool.tensor_tensor(h2_lo[:, :, tok], hg2[t % 2], h2_hi[:, :, tok], ALU.subtract).then_inc(late("v_lo")[0], 1)

            def US(_):
                for s in range(2):
                    pool.wait_ge(*late("up_hi", s + 1))
                    pool.tensor_tensor(up_lo[s], up_st[s], up_hi[s], ALU.subtract).then_inc(late("up_lo")[0], 1)

            wrun(dict(W1=W1, W2=W2, US=US))

        def wout_dve(v):
            v.wait_ge(sem("gpost_in"), 16)

            def W1(t):
                v.wait_ge(*late("w_rs", t + 1))
                if t >= 2:
                    v.wait_ge(sem(f"x1_st{t % 2}"), 16 * (t // 2))
                v.scalar_tensor_tensor(out=x1[t % 2], in0=cm_ps[t % 2], scalar=wrs[:, t:t + 1], in1=gpost_mix,
                                       op0=ALU.mult, op1=ALU.mult).then_inc(late("w_y")[0], 1)

            def WN(t):
                v.wait_ge(*late("v_rs", t + 1))
                v.tensor_scalar(hn2[t % 2], x1[t % 2], wrs[:, NT + t:NT + t + 1], None, ALU.mult).then_inc(late("v_hn")[0], 1)

            def W2(t):
                v.wait_ge(*late("v_tp", t + 1))
                if t >= 2:
                    v.wait_ge(*late("v_lo", t - 1))
                v.tensor_tensor(hg2[t % 2], tq_ps[t % 2].rearrange("p (k c) -> p k c", k=KD), bc(pcol[:, PC_GFFN:PC_GFFN + KD], 2, P),
                                ALU.mult).then_inc(late("v_hg")[0], 1)

            wrun(dict(W1=W1, WN=WN, W2=W2))

        def three(pe, outs, lhs, rhs, first):
            for part, side in ((0, 0), (0, 1), (1, 0)):
                for o, r in zip(outs, rhs):
                    ins = pe.matmul(o, lhs[part], r[side], start=first and part == side == 0, stop=True, skip_group_check=True)
            return ins

        def up_products(pe, s, g, halves):
            cols = slice(g * P, (g + 1) * P)
            for k in range(KD):
                ins = three(pe, [up_ps[s][:, g, h * 512:(h + 1) * 512] for h in halves],
                            (up_hi[s][:, k, cols], up_lo[s][:, k, cols]),
                            [(h2_hi[:, k, h * 512:(h + 1) * 512], h2_lo[:, k, h * 512:(h + 1) * 512]) for h in halves], k == 0)
            return ins

        def wout_pe(pe):
            pe.wait_ge(sem("cc_lo"), 1)
            pe.wait_ge(sem("m_lo"), NT)
            pe.wait_ge(sem("mn_lo"), NT)

            def W1(t):
                if t >= 2:
                    pe.wait_ge(*late("w_y", t - 1))
                tok = slice(t * P, (t + 1) * P)
                for k in range(KD):
                    if t == 0:
                        pe.wait_ge(*late("wo_lo", k + 1))
                    ins = three(pe, [cm_ps[t % 2][:, 0:512], cm_ps[t % 2][:, 512:1024]], (mix_hi[:, k, tok], mix_lo[:, k, tok]),
                                [(wo_hi[:, k, h * 512:(h + 1) * 512], wo_lo[:, k, h * 512:(h + 1) * 512]) for h in range(2)], k == 0)
                ins.then_inc(late("wo_mm")[0], 1)

            def W2(t):
                pe.wait_ge(*late("v_hn", t + 1))
                if t >= 2:
                    pe.wait_ge(*late("v_hg", t - 1))
                for k in range(KD):
                    ins = pe.transpose(tq_ps[t % 2][:, k * P:(k + 1) * P], hn2[t % 2][:, k * P:(k + 1) * P], ident)
                ins.then_inc(late("v_tp")[0], 1)

            def U1(_):
                pe.wait_ge(*late("up_lo", 1))
                pe.wait_ge(*late("v_lo", HT))
                for g in range(2):
                    pe.wait_ge(*late("w_y", NT - 1 + g))
                    up_products(pe, 0, g, (0,))

            def U2(_):
                pe.wait_ge(*late("up_lo", 2))
                pe.wait_ge(*late("v_hg", NT - 1))
                up_products(pe, 1, 0, (0,))

            wrun(dict(W1=W1, W2=W2, U1=U1, U2=U2))

        def up_load(sp, j, s):
            for g in range(2):
                sp.dma_start(up_st[s][:, :, g * P:(g + 1) * P],
                             a["ffn_w_up"][0].rearrange("(k p) n -> p k n", p=P)[:, :, bass.ds(j * P + g * DFF, P)])\
                    .then_inc(late(f"up_st{s}")[0], 16)

        def up_loads(sp):
            with sp.Fori(1, NF // 2) as i:
                for s in range(2):
                    sp.wait_ge(*late("up_lo", 2 * i + s - 1))
                    up_load(sp, 2 * i + s, s)

        def up_act(act):
            def split(i, s, after):
                act.wait_ge(*late(f"up_st{s}", 32 * i + 32))
                act.wait_ge(*late("up_mm", after))
                act.activation(up_hi[s], up_st[s], ACT.Copy).then_inc(late("up_hi")[0], 1)

            def body(i, more):
                for s in range(2):
                    j = 2 * i + s
                    act.wait_ge(*late("up_mm", j + 1))
                    act.wait_ge(*late("wcol", j + 1))
                    for g in range(2):
                        act.activation(y_up[s][:, g], up_ps[s][:, g], ACT.Copy, scale=wcol[s][:, 4 + g:5 + g]).then_inc(late("up_tap")[0], 1)
                    if more:
                        split(i + 1, s, j + 1)
                    act.wait_ge(*late("up_conv", 2 * j + 1))
                    act.activation(y_up[s][:, 0], y_up[s][:, 0], ACT.Silu).then_inc(late("up_silu")[0], 1)
                    act.wait_ge(*late("up_prod", j + 1))
                    act.activation(act_hi[:, bass.ds(j, 1)].rearrange('p o c -> p (o c)'), prod[s], ACT.Copy).then_inc(late("a_hi")[0], 1)

            for s in range(2):
                act.wait_ge(sem(f"x1_st{s}"), 16 * NT // 2)
            with act.Fori(0, NF // 2 - 1) as i:
                body(i, True)
            for s in range(2):
                act.wait_ge(*late(f"dn_st{s}", 16))
                act.activation(dn_hi[s], dn_st[s], ACT.Copy).then_inc(late("dn_hi")[0], 1)
            body(NF // 2 - 1, False)

        def up_pool(pool):
            def split(s, n):
                pool.wait_ge(*late("up_hi", n))
                pool.tensor_tensor(up_lo[s], up_st[s], up_hi[s], ALU.subtract).then_inc(late("up_lo")[0], 1)

            def body(i, more):
                for s in range(2):
                    j = 2 * i + s
                    if more:
                        split(s, j + 3)
                    pool.wait_ge(*late("up_silu", j + 1))
                    pool.wait_ge(*late("up_conv", 2 * j + 2))
                    pool.tensor_tensor(prod[s], y_up[s][:, 0], y_up[s][:, 1], ALU.mult).then_inc(late("up_prod")[0], 1)
                    pool.wait_ge(*late("a_hi", j + 1))
                    pool.tensor_tensor(act_lo[:, bass.ds(j, 1)].rearrange('p o c -> p (o c)'), prod[s], act_hi[:, bass.ds(j, 1)].rearrange('p o c -> p (o c)'), ALU.subtract).then_inc(late("a_lo")[0], 1)

            with pool.Fori(0, NF // 2 - 1) as i:
                body(i, True)
            for s in range(2):
                pool.wait_ge(*late("dn_hi", s + 1))
                pool.tensor_tensor(dn_lo[s], dn_st[s], dn_hi[s], ALU.subtract).then_inc(late("dn_lo")[0], 1)
            body(NF // 2 - 1, False)

        def up_dve(v):
            taps = pcol[:, PC_FCONV:PC_FCONV + 6 * NF].rearrange("p (l j) -> p l j", j=NF)

            def body(i, first):
                for s in range(2):
                    j = 2 * i + s
                    if not first:
                        v.wait_ge(*late("up_tap", 4 * i + 2 * s - 2))
                    v.tensor_copy(wcol[s], taps[:, :, bass.ds(j, 1)].rearrange('p l o -> p (l o)')).then_inc(late("wcol")[0], 1)
                    v.wait_ge(*late("wcol", j + 1))
                    v.wait_ge(*late("up_tap", 2 * j + 2))
                    for g in range(2):
                        ps = up_ps[s][:, g]
                        v.scalar_tensor_tensor(out=y_up[s][:, g, 1:S], in0=ps[:, 0:S - 1], scalar=wcol[s][:, 2 + g:3 + g],
                                               in1=y_up[s][:, g, 1:S], op0=ALU.mult, op1=ALU.add).then_inc(late("up_c1")[0], 1)
                        v.wait_ge(*late("up_c1", 2 * j + g + 1))
                        v.scalar_tensor_tensor(out=y_up[s][:, g, 2:S], in0=ps[:, 0:S - 2], scalar=wcol[s][:, g:g + 1],
                                               in1=y_up[s][:, g, 2:S], op0=ALU.mult, op1=ALU.add).then_inc(late("up_conv")[0], 1)

            body(0, True)
            with v.Fori(1, NF // 2) as i:
                body(i, False)

        def up_pe(pe):
            pe.wait_ge(*late("v_lo", NT))

            def body(i, first):
                for s in range(2):
                    j = 2 * i + s
                    pe.wait_ge(*late("up_lo", j + 1))
                    if not first:
                        pe.wait_ge(*late("up_conv", 2 * j - 2))
                    for g in range(2):
                        ins = up_products(pe, s, g, (1,) if first and (s == 0 or g == 0) else (0, 1))
                    ins.then_inc(late("up_mm")[0], 1)

            body(0, True)
            with pe.Fori(1, NF // 2) as i:
                body(i, False)

        def down_load(sp, k, s):
            sp.dma_start(dn_st[s], a["ffn_w_down"][0].rearrange("(k p) n -> p k n", p=P)[:, bass.ds(k, 1), :]
                         .rearrange("p k n -> p (k n)")).then_inc(late(f"dn_st{s}")[0], 16)

        def down_loads(sp):
            sp.dma_start(gpost_ffn, a["norm_ffn_post"][0].partition_broadcast(P)).then_inc(sem("gpost2_in"), 16)
            for s in range(2):
                down_load(sp, s, s)

            def loads(i, m):
                for s in range(2):
                    sp.wait_ge(*late("dn_lo", 2 * i + s - 1 + NF * m))
                    down_load(sp, 2 * i + s, s)

            def x1_loads(m):
                for t in range(HT):
                    sp.dma_start(x1r[t], scratch[(HT * m + t) * P:(HT * m + t + 1) * P, :]).then_inc(late(f"x1r{t}")[0], 16)

            def stores(m):
                for t in range(HT * m, HT * m + HT):
                    if m and t % 2:
                        sp.wait_ge(sem("fin_v"), (t - HT) // 2 + 1)
                    else:
                        sp.wait_ge(*late("fin", t + 1 if m == 0 else HT + (t - HT) // 2 + 1))
                    sp.dma_start(out[0, t * P:(t + 1) * P, :], y_dn[:, t]).then_inc(sem("stored"), 16)

            with sp.Fori(1, NF // 2) as i:
                loads(i, 0)
            for s in range(2):
                sp.wait_ge(sem(f"x1_st{s}"), 16 * NT // 2)
            sp.wait_ge(*late("a_lo", NF))
            x1_loads(0)
            loads(0, 1)
            loads(1, 1)
            stores(0)
            x1_loads(1)
            with sp.Fori(2, NF // 2) as i:
                loads(i, 1)
            stores(1)
            sp.wait_ge(sem("stored"), 16 * NT)

        def down_act(act):
            act.preload_act_table_set("natural_log_exp_and_others")

            def split(i, s, m):
                act.wait_ge(*late(f"dn_st{s}", 16 * i + 16 + 8 * NF * m))
                act.activation(dn_hi[s], dn_st[s], ACT.Copy).then_inc(late("dn_hi")[0], 1)

            def body(i, m):
                for s in range(2):
                    act.wait_ge(*late("dn_mm", 2 * i + s - 1 + (NF - 1) * m))
                    split(i, s, m)

            def norm(t0, t1):
                for t in range(t0, t1):
                    act.wait_ge(*late("dn_t", t + 1))
                    act.activation(junk2, dn_ps[t % HT], ACT.Square, accum_out=wss[:, t:t + 1]).then_inc(late("f_sq")[0], 1)
                    act.wait_ge(*late("f_sq", t + 1))
                    act.activation(wrs[:, t:t + 1], wss[:, t:t + 1], ACT.Ln, bias=eps_c, scale=1.0 / D).then_inc(late("f_ln")[0], 1)
                    act.wait_ge(*late("f_ln", t + 1))
                    act.activation(wrs[:, t:t + 1], wrs[:, t:t + 1], ACT.Exp, scale=-0.5).then_inc(late("f_rs")[0], 1)

            with act.Fori(1, NF // 2) as i:
                body(i, 0)
            act.wait_ge(*late("dn_mm", NF - 1))
            split(0, 0, 1)
            norm(0, HT - 1)
            act.wait_ge(*late("dn_t", HT))
            split(0, 1, 1)
            norm(HT - 1, HT)
            with act.Fori(1, NF // 2) as i:
                body(i, 1)
            norm(HT, NT)

        def down_pool(pool):
            def split(s, n):
                pool.wait_ge(*late("dn_hi", n))
                pool.tensor_tensor(dn_lo[s], dn_st[s], dn_hi[s], ALU.subtract).then_inc(late("dn_lo")[0], 1)

            def add(m):
                for t in range(HT * m, HT * m + HT, m + 1):
                    pool.wait_ge(*late("f_y", t + 1))
                    pool.wait_ge(*late(f"x1r{t % HT}", 16 * (m + 1)))
                    pool.tensor_tensor(y_dn[:, t], y_dn[:, t], x1r[t % HT], ALU.add).then_inc(late("fin")[0], 1)

            with pool.Fori(1, NF // 2 + 1) as i:
                for s in range(2):
                    split(s, 2 * i + s + 1)
            add(0)
            with pool.Fori(NF // 2 + 1, NF) as i:
                for s in range(2):
                    split(s, 2 * i + s + 1)
            add(1)

        def down_dve(v):
            v.wait_ge(sem("gpost2_in"), 16)
            for t in range(NT):
                v.wait_ge(*late("f_rs", t + 1))
                v.scalar_tensor_tensor(out=y_dn[:, t], in0=dn_ps[t % HT], scalar=wrs[:, t:t + 1], in1=gpost_ffn,
                                       op0=ALU.mult, op1=ALU.mult).then_inc(late("f_y")[0], 1)
                if t >= HT and t % 2:
                    v.wait_ge(*late("f_y", t + 1))
                    v.wait_ge(*late(f"x1r{t % HT}", 32))
                    v.tensor_tensor(y_dn[:, t], y_dn[:, t], x1r[t % HT], ALU.add).then_inc(sem("fin_v"), 1)

        def down_pe(pe):
            def step(k, s, m, place, tiles=range(HT)):
                pe.wait_ge(*late("dn_lo", k + 1 + NF * m))
                part = lambda x, tok: x[:, bass.ds(k, 1), tok].rearrange("p o c -> p (o c)")
                for t in tiles:
                    tok = slice((HT * m + t) * P, (HT * m + t + 1) * P)
                    if place == "first" and m:
                        pe.wait_ge(*late("f_y", t + 1))
                    elif place == "first":
                        pe.wait_ge(*late("up_conv", 2 * NF - (2 if t < HT // 2 else 0)))
                    ins = three(pe, [dn_ps[t][:, 0:512], dn_ps[t][:, 512:1024]], (part(act_hi, tok), part(act_lo, tok)),
                                [(dn_hi[s][:, n * 512:(n + 1) * 512], dn_lo[s][:, n * 512:(n + 1) * 512]) for n in range(2)],
                                place == "first")
                    if place == "last":
                        ins.then_inc(late("dn_t")[0], 1)
                if place != "last" and HT - 1 in tiles:
                    ins.then_inc(late("dn_mm")[0], 1)

            pe.wait_ge(*late("a_lo", NF - 2))
            for m in range(2):
                for tiles in (range(HT // 2), range(HT // 2, HT)) if m == 0 else (range(HT),):
                    step(0, 0, m, "first", tiles)
                    step(1, 1, m, "", tiles)
                with pe.Fori(1, NF // 2 - 1) as i:
                    for s in range(2):
                        step(2 * i + s, s, m, "")
                if m == 0:
                    pe.wait_ge(*late("a_lo", NF))
                step(NF - 2, 0, m, "")
                step(NF - 1, 1, m, "last")

        def split_hi_part(act, b, c):
            n = BLOCKS[b][1]
            act.wait_ge(sem(f"w_st{c}"), 16 * (b + 1))
            if b == NCM + 2:
                act.wait_ge(sem("w_gate"), 64)
            act.activation(wb_hi[b % 2][:, 2 * c:2 * c + 2, 0:n], wst[c][:, :, 0:n], ACT.Copy).then_inc(sem("w_hi"), 1)

        def split_lo_part(eng, b, c):
            n = BLOCKS[b][1]
            eng.wait_ge(sem("w_hi"), 4 * b + c + 1)
            eng.tensor_tensor(wb_lo[b % 2][:, 2 * c:2 * c + 2, 0:n], wst[c][:, :, 0:n],
                              wb_hi[b % 2][:, 2 * c:2 * c + 2, 0:n], ALU.subtract).then_inc(sem("w_lo"), 1)

        def h_hi(act, t):
            act.wait_ge(sem("h_gained"), t + 1)
            act.activation(hT_hi[:, :, t * P:(t + 1) * P], x_hg[t % 2], ACT.Copy).then_inc(sem("h_hi"), 1)

        def silu(act, c):
            act.wait_ge(sem("conv_done"), c + 1)
            act.activation(qkvT[:, c], qkvT[:, c], ACT.Silu).then_inc(sem("qkv_ready"), 1)

        def kt_copy(act, t):
            act.wait_ge(sem("kT_done"), t + 1)
            act.activation(kT2[:, :, t * P:(t + 1) * P],
                           tp_ps[t % 2][:, 0:256].rearrange("p (w c) -> p w c", w=2), ACT.Copy).then_inc(sem("kT_out"), 1)

        def h_gain(v, t):
            v.wait_ge(sem("h_tp"), t + 1)
            if t >= 2:
                v.wait_ge(sem("h_lo"), t - 1)
            ps = cm_ps[t % 2].rearrange("p (k c) -> p k c", k=KD)
            v.tensor_tensor(x_hg[t % 2], ps, bc(pcol[:, PC_GMIX:PC_GMIX + KD], 2, P), ALU.mult).then_inc(sem("h_gained"), 1)

        def kt_transpose(pe, t):
            pe.wait_ge(sem("rot"), 2 * t + 2)
            if t >= 2:
                pe.wait_ge(sem("kT_out"), t - 1)
            else:
                pe.wait_ge(sem("pcol_ready"), 3)
            for w in range(2):
                ins = pe.transpose(tp_ps[t % 2][:, w * P:(w + 1) * P], kr[t % 2][:, w], ident)
            ins.then_inc(sem("kT_done"), 1)


        @block.sync
        def _(sp):
            for t in range(4):
                sp.dma_start(x_in[t], x_d[0, t * P:(t + 1) * P, :]).then_inc(sem(f"x_in{t}"), 16)
            sp.wait_ge(sem("prow_zeroed"), 1)
            rows = [(PC_GMIX, a["norm_mix_pre"][0], 8), (PC_GFFN, a["norm_ffn_pre"][0], 8)]
            for at_, v, n in rows:
                sp.dma_start(prow[at_:at_ + n, 0, :], v.rearrange("(c p) -> c p", p=P)).then_inc(sem("prow_in"), 16)
            for at_, v, n in ((PC_GCONV, a["gdn_conv_w"], 36), (PC_CCW, a["cc_dw_w"], 62)):
                sp.dma_start(prow[at_:at_ + n, 0, :], v[0].rearrange("l (c p) -> (l c) p", p=P)).then_inc(sem("prow_in"), 16)
            for at_, v in ((PC_CCB, a["cc_dw_b"]), (PC_LNG, a["cc_ln_g"]), (PC_LNB, a["cc_ln_b"])):
                sp.dma_start(prow[at_:at_ + 2, 0, :], v[0].rearrange("(c p) -> c p", p=P)).then_inc(sem("prow_in"), 16)
            fc = a["ffn_conv_w"][0].rearrange("l (c p) -> (l c) p", p=P)
            sp.dma_start(prow[:, 1, :], fc[0:P, :]).then_inc(sem("prow_in"), 16)
            sp.dma_start(prow[0:4, 2, :], fc[P:P + 4, :]).then_inc(sem("prow_in"), 16)
            for half in range(2):
                c = slice(HD * half, HD * half + HD)
                sp.dma_start(prow[PC_GNG:PC_GNG + 1, 0, c], a["gdn_norm_g"]).then_inc(sem("prow_in"), 16)
                sp.dma_start(prow[4:4 + CLEN, 2, c], a["nsa_cmp_pe_k"][0]).then_inc(sem("prow_in"), 16)
                sp.dma_start(prow[36:36 + CLEN, 2, c], a["nsa_cmp_pe_v"][0]).then_inc(sem("prow_in"), 16)
            sp.wait_ge(sem("pos_zeroed"), 1)
            sp.dma_start(pos_i[:, 0:NT], a["positions"][0].rearrange("(t p) -> p t", p=P),
                         allow_slow_non_contiguous=True).then_inc(sem("pos_in"), 16)
            sp.dma_start(pos_i[0:NCMP, NT:NT + 1],
                         a["positions"][0, CLEN - 1:S].rearrange("(n o) -> n o", o=1)[0:(NCMP - 1) * STRIDE + 1:STRIDE, :],
                         allow_slow_non_contiguous=True
                         ).then_inc(sem("pos_in"), 16)
            sp.dma_start(inv_t, a["inv"][0].partition_broadcast(P)).then_inc(sem("pos_in"), 16)
            def x_load(t):
                sp.wait_ge(sem("h_scaled"), t - 3)
                sp.dma_start(x_in[t % 4], x_d[0, t * P:(t + 1) * P, :]).then_inc(sem(f"x_in{t % 4}"), 16)

            wv = w_in[0].rearrange("(c k p) n -> c p k n", k=2, p=P)
            for b, (col, n) in enumerate(BLOCKS):
                for c in range(4):
                    if b == 0:
                        x_load(4 + c)
                    if b:
                        sp.wait_ge(sem("w_lo"), 4 * (b - 1) + c + 1)
                    if (col, n) == TM_BLOCKS[2]:
                        sp.dma_start(wst[c][:, :, 0:384], wv[c][:, :, col:col + 384]).then_inc(sem(f"w_st{c}"), 16)
                        sp.dma_start(wst[c][:, :, 384:402], wv[c][:, :, C_NG:C_NG + 18]).then_inc(sem("w_gate"), 16)
                    else:
                        sp.dma_start(wst[c][:, :, 0:n], wv[c][:, :, col:col + n]).then_inc(sem(f"w_st{c}"), 16)
            mixer_loads(sp)
            wout_loads(sp)
            up_loads(sp)
            down_loads(sp)

        @block.gpsimd
        def _(pool):
            own = Count(sem("pool_own"))
            own_consts = Count(sem("pool_own2"))
            pool.memset(prow, 0.0).then_inc(sem("prow_zeroed"), 1)
            pool.memset(pos_i, 0).then_inc(sem("pos_zeroed"), 1)
            own.up(pool.memset(eps_c, EPS))
            own.up(pool.memset(ident, 0.0))
            own.up(pool.memset(identb, 0.0))
            own.settle(pool)
            for m in (ident, identb):
                pool.affine_select(out=m, in_=m, compare_op=ALU.not_equal, fill=1.0, base=0,
                                   pattern=[[-1, P]], channel_multiplier=1).then_inc(sem("ident_ready"), 1)
            for t in range(NT):
                pool.wait_ge(sem("h_hi"), t + 1)
                pool.tensor_tensor(hT_lo[:, :, t * P:(t + 1) * P], x_hg[t % 2], hT_hi[:, :, t * P:(t + 1) * P],
                                   ALU.subtract).then_inc(sem("h_lo"), 1)
            def split_lo(b):
                for c in range(4):
                    split_lo_part(pool, b, c)

            pool.wait_ge(sem("w_lo"), 4)
            split_lo(1)
            for b in range(len(BLOCKS)):
                if b == NCM + 1:
                    for t in range(NT):
                        s = t % 2
                        pool.wait_ge(sem("rot_mul"), t + 1)
                        if t >= 2:
                            pool.wait_ge(sem("kT_done"), t - 1)
                        vc = tmc[s][:, 0:256].rearrange("p (w h e d) -> p w h e d", w=2, h=2, e=2)
                        vs = tms[s][:, 0:256].rearrange("p (w h e d) -> p w h e d", w=2, h=2, e=2)
                        o = kr[s].rearrange("p w (h e d) -> p w h e d", h=2, e=2)
                        pool.tensor_tensor(o[:, :, :, 0, :], vc[:, :, :, 0, :], vs[:, :, :, 1, :], ALU.subtract).then_inc(sem("rot"), 1)
                        pool.tensor_tensor(o[:, :, :, 1, :], vs[:, :, :, 0, :], vc[:, :, :, 1, :], ALU.add).then_inc(sem("rot"), 1)
                        pool.wait_ge(sem("rot"), 2 * t + 2)
                        mixer_constants(pool, own_consts, t)
                if b == NCM + 2:
                    for t in range(NT):
                        s = t % 2
                        pool.wait_ge(sem("rot_mul"), NT + t + 1)
                        vc = tmc[s].rearrange("p (k g e d) -> p k g e d", k=KV, g=GRP, e=2)
                        vs = tms[s].rearrange("p (k g e d) -> p k g e d", k=KV, g=GRP, e=2)
                        o = qr[:, t].rearrange("p g k (e d) -> p k g e d", e=2)
                        if t == 1:
                            pool.wait_ge(sem("tm_done"), 2 * NT)
                            pool.wait_ge(sem("rot"), 2 * NT + 2)
                            zero_cmp_weights(pool, wck)
                            pool.wait_ge(sem("wc_zero"), 2)
                        pool.tensor_tensor(o[:, :, :, 0, :], vc[:, :, :, 0, :], vs[:, :, :, 1, :], ALU.subtract).then_inc(sem("rot"), 1)
                        pool.tensor_tensor(o[:, :, :, 1, :], vs[:, :, :, 0, :], vc[:, :, :, 1, :], ALU.add).then_inc(sem("rot"), 1)
                if b + 2 < len(BLOCKS):
                    split_lo(b + 2)
            mixer_pool(pool)
            wout_pool(pool)
            up_pool(pool)
            down_pool(pool)

        @block.scalar
        def _(act):
            act.wait_ge(sem("pool_own"), 3)
            for t in range(NT):
                act.wait_ge(sem(f"x_in{t % 4}"), 16 * (t // 4 + 1))
                act.activation(psum[:, 4:6, :].rearrange("p a b -> p (a b)"), x_in[t % 4], ACT.Square,
                               accum_out=ssq[:, t:t + 1]).then_inc(sem("ssq"), 1)
                act.wait_ge(sem("ssq"), t + 1)
                act.activation(rms[:, t:t + 1], ssq[:, t:t + 1], ACT.Sqrt, bias=eps_c, scale=1.0 / D).then_inc(sem("rms"), 1)
                if t >= 2:
                    h_hi(act, t - 2)
                if t >= 4:
                    split_hi_part(act, 0, t - 4)
            h_hi(act, NT - 2)
            h_hi(act, NT - 1)

            def split_hi(b):
                if b >= 2:
                    if b - 2 < NCM:
                        act.wait_ge(sem("cm_done"), CM_AFTER[b - 2])
                    else:
                        act.wait_ge(sem("tm_done"), NT * (b - 1 - NCM))
                for c in range(4):
                    split_hi_part(act, b, c)

            split_hi(1)
            act.wait_ge(sem("rope_arg"), 1)
            act.activation(sin_t, ang, ACT.Sin).then_inc(sem("rope_tab"), 1)
            act.wait_ge(sem("rope_arg"), 2)
            act.activation(cos_t, turns, ACT.Sin).then_inc(sem("rope_tab"), 1)
            i = 0
            for b in range(NCM):
                for _, j in [x for x in CM_ORDER if x[0] == b]:
                    ps = cm_ps[i % 2]
                    act.wait_ge(sem("cm_done"), i + 1)
                    if b == 0:
                        if j < 2:
                            act.activation(cacc[:, j], ps, ACT.Copy).then_inc(sem("cu_out"), 1)
                        else:
                            act.wait_ge(sem("pcol_ready"), 3)
                            act.wait_ge(sem("rope_tab"), 2)
                            act.activation(glu[:, j - 2], ps, ACT.Tanh, scale=0.5).then_inc(sem("cu_out"), 1)
                    elif b <= 3:
                        c = 3 * (b - 1) + j
                        act.wait_ge(sem("pcol_ready"), 3)
                        act.activation(qkvT[:, c], ps, ACT.Copy,
                                       scale=pcol[:, PC_GCONV + 27 + c:PC_GCONV + 28 + c]).then_inc(sem("tap0"), 1)
                        if c >= 1:
                            silu(act, c - 1)
                    i += 1
                if b + 2 < len(BLOCKS):
                    split_hi(b + 2)
            silu(act, 8)
            for b in range(3):
                for t in range(NT):
                    n = b * NT + t
                    act.wait_ge(sem("tm_done"), n + 1)
                    ps = tm_ps[n % 2]
                    if b == 0:
                        act.activation(zab[:, t, 0:GDIM], ps[:, 0:GDIM], ACT.Silu).then_inc(sem("z_out"), 1)
                        act.activation(zab[:, t, GDIM:], ps[:, GDIM:GDIM + 2 * GH], ACT.Copy).then_inc(sem("tm_act"), 1)
                    elif b == 1:
                        act.activation(vsw[:, t], ps.rearrange("p (w c) -> p w c", w=4)[:, 1:4:2, :], ACT.Copy).then_inc(sem("tm_act"), 1)
                        if t >= 1:
                            kt_copy(act, t - 1)
                    else:
                        act.activation(gate[:, t], ps[:, 384:402], ACT.Copy).then_inc(sem("tm_act"), 1)
                if b == 1:
                    kt_copy(act, NT - 1)
                if NCM + b + 2 < len(BLOCKS):
                    split_hi(NCM + b + 2)
            conf_act(act)
            mixer_act(act)
            wout_act(act)
            up_act(act)
            down_act(act)

        @block.vector
        def _(v):
            own = Count(sem("dve_own"))

            def rope_tables():
                v.wait_ge(sem("pos_in"), 48)
                own.up(v.tensor_copy(pos_f, pos_i))
                own.settle(v)
                own.up(v.tensor_tensor(ang, bc(pos_f, 2, HD // 2), bc(inv_t, 1, NT + 1), ALU.mult))
                own.settle(v)
                magic = 12582912.0
                own.up(v.tensor_scalar(turns, ang, 1.0 / (2 * math.pi), magic, ALU.mult, ALU.add))
                own.settle(v)
                own.up(v.tensor_scalar(turns, turns, -magic, None, ALU.add))
                own.settle(v)
                c1 = 6.28125
                c2 = float(np.float32(round((2 * math.pi - c1) * 2 ** 20) / 2 ** 20))
                c3 = 2 * math.pi - c1 - c2
                for c in (c1, c2, c3):
                    own.up(v.scalar_tensor_tensor(out=ang, in0=turns, scalar=-c, in1=ang, op0=ALU.mult, op1=ALU.add))
                    own.settle(v)
                edge = 3.1415925
                v.tensor_scalar(ang, ang, edge, -edge, ALU.min, ALU.max).then_inc(sem("rope_arg"), 1)
                v.wait_ge(sem("rope_arg"), 1)
                own.up(v.scalar_tensor_tensor(out=turns, in0=ang, scalar=-1.0, in1=ang, op0=ALU.mult, op1=ALU.max))
                own.settle(v)
                v.tensor_scalar(turns, turns, -1.0, math.pi / 2, ALU.mult, ALU.add).then_inc(sem("rope_arg"), 1)

            for t in range(NT):
                v.wait_ge(sem("rms"), t + 1)
                own.up(v.reciprocal(rstd[:, t:t + 1], rms[:, t:t + 1]))
                own.settle(v)
                if t >= 2:
                    v.wait_ge(sem("h_tp"), t - 1)
                v.tensor_scalar(x_hn[t % 2], x_in[t % 4], rstd[:, t:t + 1], None, ALU.mult).then_inc(sem("h_scaled"), 1)
                if t == 0:
                    v.wait_ge(sem("pcol_tp"), 3)
                    for j in range(3):
                        v.tensor_copy(pcol[:, j * P:(j + 1) * P], psum[:, 6, j * P:(j + 1) * P]).then_inc(sem("pcol_ready"), 1)
                    v.wait_ge(sem("pcol_ready"), 3)
                    own.up(v.tensor_scalar(pcol[:, PC_CCW:PC_CCW + 62], pcol[:, PC_CCW:PC_CCW + 62], 0.5, None, ALU.mult))
                if t >= 1:
                    h_gain(v, t - 1)
                if t >= 5:
                    split_lo_part(v, 0, t - 5)
            h_gain(v, NT - 1)
            split_lo_part(v, 0, 3)
            rope_tables()

            i = 0
            conv_at = [0]

            def cc_taps(c, s0, s1):
                for s in range(s0, s1):
                    col = PC_CCW + 2 * (CW - 1 - s) + c
                    w = pcol[:, col:col + 1]
                    if s == 0:
                        own.up(v.tensor_scalar(cacc[:, c], glu[:, c], w, pcol[:, PC_CCB + c:PC_CCB + c + 1], ALU.mult, ALU.add))
                    else:
                        own.settle(v)
                        own.up(v.scalar_tensor_tensor(out=cacc[:, c, s:S], in0=glu[:, c, 0:S - s], scalar=w,
                                                      in1=cacc[:, c, s:S], op0=ALU.mult, op1=ALU.add))

            cc_plan = [(c, s0, min(s0 + 5, CW)) for c in range(2) for s0 in range(0, CW, 5)]
            for b in range(NCM):
                for _, j in [x for x in CM_ORDER if x[0] == b]:
                    ps = cm_ps[i % 2]
                    if b == 0 and j >= 2:
                        v.wait_ge(sem("cu_out"), i + 1)
                        own.up(v.scalar_tensor_tensor(out=glu[:, j - 2], in0=glu[:, j - 2], scalar=1.0, in1=cacc[:, j - 2],
                                                      op0=ALU.add, op1=ALU.mult))
                        own.settle(v)
                    elif 1 <= b <= 3:
                        c = 3 * (b - 1) + j
                        v.wait_ge(sem("tap0"), c + 1)
                        for s in range(1, 4):
                            col = PC_GCONV + 9 * (3 - s) + c
                            ins = v.scalar_tensor_tensor(out=qkvT[:, c, s:S], in0=ps[:, 0:S - s], scalar=pcol[:, col:col + 1],
                                                         in1=qkvT[:, c, s:S], op0=ALU.mult, op1=ALU.add)
                            if s < 3:
                                own.up(ins)
                                own.settle(v)
                            else:
                                ins.then_inc(sem("conv_done"), 1)
                    elif b == 4:
                        v.wait_ge(sem("cm_done"), i + 1)
                        dst = (kcat, vcat)[j]
                        pe0 = (PC_PEK, PC_PEV)[j]
                        for half in range(2):
                            pe_ = pcol[:, pe0 + STRIDE * half:pe0 + STRIDE * half + STRIDE]
                            v.tensor_tensor(dst[:, half].rearrange("p (n l) -> p n l", l=STRIDE),
                                            ps.rearrange("p (n l) -> p n l", l=STRIDE), bc(pe_, 1, S // STRIDE),
                                            ALU.add).then_inc(sem("cat_out"), 1)
                    if b >= 1 and cc_plan:
                        cc_taps(*cc_plan.pop(0))
                    i += 1
            while cc_plan:
                cc_taps(*cc_plan.pop(0))
            own.settle(v)
            v.tensor_copy(gng, pcol[:, PC_GNG:PC_GNG + 1]).then_inc(sem("cc_conv"), 1)
            for b in (1, 2):
                for t in range(NT):
                    n = b * NT + t
                    ps = tm_ps[n % 2]
                    v.wait_ge(sem("tm_act"), n + 1)
                    if t == 0:
                        v.wait_ge(sem("rope_tab"), 2)
                    s = t % 2
                    if n >= NT + 2:
                        v.wait_ge(sem("rot"), 2 * (n - NT - 1))
                    for tab, dst in ((cos_t, tmc), (sin_t, tms)):
                        if b == 1:
                            ins = v.tensor_tensor(dst[s][:, 0:256].rearrange("p (w c d) -> p w c d", w=2, d=32),
                                                  ps.rearrange("p (w c d) -> p w c d", w=4, d=32)[:, 0:4:2],
                                                  bc(bc(tab[:, t], 1, 4), 1, 2), ALU.mult)
                        else:
                            ins = v.scalar_tensor_tensor(out=dst[s].rearrange("p (c d) -> p c d", d=32),
                                                         in0=ps[:, 0:384].rearrange("p (c d) -> p c d", d=32),
                                                         scalar=HD ** -0.5, in1=bc(tab[:, t], 1, 12), op0=ALU.mult, op1=ALU.mult)
                        if tab is cos_t:
                            own.up(ins)
                    ins.then_inc(sem("rot_mul"), 1)
                    if b == 2:
                        conf_stats(v, t)
            own.settle(v)
            conf_dve(v)
            mixer_dve(v)
            wout_dve(v)
            up_dve(v)
            down_dve(v)

        @block.tensor
        def _(pe):
            pe.wait_ge(sem("ident_ready"), 2)
            for t in range(NT):
                if t == 1:
                    pe.wait_ge(sem("prow_in"), 16 * 15)
                    for j in range(3):
                        pe.transpose(psum[:, 6, j * P:(j + 1) * P], prow[:, j, :], ident).then_inc(sem("pcol_tp"), 1)
                pe.wait_ge(sem("h_scaled"), t + 1)
                if t >= 2:
                    pe.wait_ge(sem("h_gained"), t - 1)
                for k in range(KD):
                    ins = pe.transpose(cm_ps[t % 2][:, k * P:(k + 1) * P], x_hn[t % 2][:, k * P:(k + 1) * P], ident)
                ins.then_inc(sem("h_tp"), 1)

            def three(outs, lhs, rhs, first, last):
                for o, (r_hi, r_lo) in zip(outs, rhs):
                    pe.matmul(o, lhs[0], r_hi, start=first, stop=False)
                for o, (r_hi, r_lo) in zip(outs, rhs):
                    pe.matmul(o, lhs[0], r_lo, start=False, stop=False)
                for o, (r_hi, r_lo) in zip(outs, rhs):
                    ins = pe.matmul(o, lhs[1], r_hi, start=False, stop=last)
                return ins

            i = 0
            for b in range(NCM):
                pe.wait_ge(sem("w_lo"), 4 * b + 4)
                for _, j in [x for x in CM_ORDER if x[0] == b]:
                    if i < 2:
                        pe.wait_ge(sem("h_lo"), NT)
                    if i >= 2:
                        q = i - 2
                        if q < 4:
                            pe.wait_ge(sem("cu_out"), q + 1)
                        elif q < 13:
                            pe.wait_ge(sem("conv_done"), q - 3)
                        else:
                            pe.wait_ge(sem("cat_out"), 2 * (q - 12))
                    ps = cm_ps[i % 2]
                    cols = slice(j * P, (j + 1) * P)
                    for k in range(KD):
                        ins = three([ps[:, 0:512], ps[:, 512:1024]],
                                    (wb_hi[b % 2][:, k, cols], wb_lo[b % 2][:, k, cols]),
                                    [(hT_hi[:, k, h * 512:(h + 1) * 512], hT_lo[:, k, h * 512:(h + 1) * 512]) for h in range(2)],
                                    k == 0, k == KD - 1)
                    ins.then_inc(sem("cm_done"), 1)
                    i += 1
            for b in range(3):
                B = NCM + b
                n_cols = BLOCKS[B][1]
                pe.wait_ge(sem("w_lo"), 4 * B + 4)
                for t in range(NT):
                    n = b * NT + t
                    if n >= 2:
                        q = n - 2
                        if q < NT:
                            pe.wait_ge(sem("tm_act"), q + 1)
                        else:
                            pe.wait_ge(sem("rot_mul"), q - NT + 1)
                    ps = tm_ps[n % 2][:, 0:n_cols]
                    tok = slice(t * P, (t + 1) * P)
                    for k in range(KD):
                        ins = three([ps], (hT_hi[:, k, tok], hT_lo[:, k, tok]),
                                    [(wb_hi[B % 2][:, k, 0:n_cols], wb_lo[B % 2][:, k, 0:n_cols])], k == 0, k == KD - 1)
                    ins.then_inc(sem("tm_done"), 1)
                    if b == 1 and t >= 1:
                        kt_transpose(pe, t - 1)
                    if b == 2:
                        conf_transpose(pe, t)
                if b == 1:
                    kt_transpose(pe, NT - 1)
            mixer_pe(pe)
            wout_pe(pe)
            up_pe(pe)
            down_pe(pe)


INPUTS = ["x", "positions", "norm_mix_pre", "norm_mix_post", "norm_ffn_pre", "norm_ffn_post", "w_in", "w_out",
          "gdn_conv_w", "gdn_a_log", "gdn_dt_bias", "gdn_norm_g", "nsa_cmp_wk", "nsa_cmp_wv", "nsa_cmp_pe_k",
          "nsa_cmp_pe_v", "cc_dw_w", "cc_dw_b", "cc_ln_g", "cc_ln_b", "ffn_w_up", "ffn_conv_w", "ffn_w_down"]


def kernel(**inputs):
    import concourse.bacc as bacc
    from concourse.bass_utils import run_bass_kernel_spmd

    nc = bacc.Bacc("TRN2", target_bir_lowering=False, num_devices=1)
    arrays, a = {}, {}
    for name in INPUTS:
        v = np.ascontiguousarray(inputs[name])
        arrays["in_" + name] = v
        a[name] = nc.dram_tensor("in_" + name, v.shape, mybir.dt.from_np(v.dtype), kind="ExternalInput").ap()
    inv = inv_freq().reshape(1, HD // 2)
    arrays["inv_freq"] = inv
    a["inv"] = nc.dram_tensor("inv_freq", inv.shape, F32, kind="ExternalInput").ap()
    out = nc.dram_tensor("out_0", (1, S, D), F32, kind="ExternalOutput").ap()
    scratch = nc.dram_tensor("x_mid", (S, D), F32, kind="Internal").ap()
    build(nc, a, out, scratch)
    r = run_bass_kernel_spmd(nc, [arrays], core_ids=[0])
    return r.results[0]["out_0"]
```
